# Optimizing a Trainium2 kernel written in Bass

```python
import jax, jax.numpy as jnp
from jax import lax
import numpy as np

D_MODEL = 1024
BATCH = 1
SEQ = 256
DEPTH = 1

PLE_DIM = 256
MIX_WIDTH = D_MODEL
HG_WIDTH = D_MODEL // 2
HG_HEADS = 4
HG_DK = HG_WIDTH // HG_HEADS
HG_DV = HG_WIDTH // HG_HEADS
HG_CHUNK = 64
SB_WIDTH = MIX_WIDTH - HG_WIDTH
SB_HEADS = 8
SB_DH = SB_WIDTH // SB_HEADS
SB_BLOCK = 128
D_FF = -(-8 * D_MODEL // (3 * 256)) * 256
IN_COLS = 4 * HG_WIDTH + 3 * SB_WIDTH
EPS = 1e-6


def rmsnorm(x, w):
    xf = x.astype(jnp.float32)
    xf = xf * lax.rsqrt(jnp.mean(xf * xf, axis=-1, keepdims=True) + EPS)
    return xf.astype(x.dtype) * w

def _to_chunks(a, heads, d):
    B, T, _ = a.shape
    return a.reshape(B, T // HG_CHUNK, HG_CHUNK, heads, d).transpose(1, 0, 3, 2, 4)

def hgrn2_mix(q, f_logit, i_in, lb):
    B, T, _ = q.shape
    q = jax.nn.silu(q.astype(jnp.float32))
    z = f_logit.astype(jnp.float32)
    log_f = jnp.logaddexp(jnp.log(lb), jnp.log1p(-lb) + jax.nn.log_sigmoid(z))
    k = -jnp.expm1(log_f)
    v = i_in.astype(jnp.float32)
    qc = _to_chunks(q, HG_HEADS, HG_DK)
    kc = _to_chunks(k, HG_HEADS, HG_DK)
    gc = _to_chunks(log_f, HG_HEADS, HG_DK)
    vc = _to_chunks(v, HG_HEADS, HG_DV)
    incl = jnp.tril(jnp.ones((HG_CHUNK, HG_CHUNK), dtype=bool))

    def step(S, inp):
        qb, kb, gb, vb = inp
        b = jnp.cumsum(gb, axis=2)
        o_inter = jnp.einsum('bhtk,bhkv->bhtv', qb * jnp.exp(b), S)
        diff = b[:, :, :, None, :] - b[:, :, None, :, :]
        decay = jnp.where(incl[:, :, None], jnp.exp(jnp.minimum(diff, 0.0)), 0.0)
        scores = jnp.einsum('bhtsk,bhsk->bhts', qb[:, :, :, None, :] * decay, kb)
        o_intra = jnp.einsum('bhts,bhsv->bhtv', scores, vb)
        b_last = b[:, :, -1:, :]
        S_new = jnp.exp(b_last[:, :, 0, :])[..., None] * S + jnp.einsum(
            'bhsk,bhsv->bhkv', kb * jnp.exp(b_last - b), vb)
        return S_new, o_inter + o_intra

    S0 = jnp.zeros((B, HG_HEADS, HG_DK, HG_DV), jnp.float32)
    _, oc = lax.scan(step, S0, (qc, kc, gc, vc))
    return oc.transpose(1, 0, 3, 2, 4).reshape(B, T, HG_HEADS * HG_DV)

def stick_breaking_mix(q, k, v):
    B, T, H, d = q.shape
    scale = d ** -0.5
    outs = []
    for blk in range(T // SB_BLOCK):
        t0 = blk * SB_BLOCK
        t1 = t0 + SB_BLOCK
        qb = q[:, t0:t1]
        kp = k[:, :t1]
        vp = v[:, :t1]
        z = jnp.einsum('bthd,bshd->bhts', qb, kp).astype(jnp.float32) * scale
        causal = jnp.arange(t1)[None, :] < jnp.arange(t0, t1)[:, None]
        log_1mb = jnp.where(causal, -jax.nn.softplus(z), 0.0)
        rem = lax.cumsum(log_1mb, axis=3, reverse=True) - log_1mb
        a = jnp.where(causal, jnp.exp(jax.nn.log_sigmoid(z) + rem), 0.0)
        outs.append(jnp.einsum('bhts,bshd->bthd', a.astype(v.dtype), vp))
    return jnp.concatenate(outs, axis=1)

def first_inputs(seed: int = 0) -> dict:
    key = jax.random.key(seed)
    ks = jax.random.split(key, 16)
    f32 = jnp.float32
    nrm = lambda k, shape, s: jax.random.normal(k, shape, f32) * s
    gain = lambda k, shape: 1.0 + 0.05 * jax.random.normal(k, shape, f32)
    return {
        "x": jax.random.normal(ks[0], (BATCH, SEQ, D_MODEL), f32),
        "p": jax.random.normal(ks[1], (DEPTH, BATCH, SEQ, PLE_DIM), f32),
        "attn_pre_norm": gain(ks[2], (DEPTH, D_MODEL)),
        "w_in": nrm(ks[3], (DEPTH, D_MODEL, IN_COLS), D_MODEL ** -0.5),
        "hg_lower_gamma": nrm(ks[4], (DEPTH + 1, HG_WIDTH), 0.5),
        "hg_out_norm": gain(ks[5], (DEPTH, HG_WIDTH)),
        "sb_out_norm": gain(ks[6], (DEPTH, SB_WIDTH)),
        "w_out": nrm(ks[7], (DEPTH, MIX_WIDTH, D_MODEL), MIX_WIDTH ** -0.5),
        "attn_post_norm": gain(ks[8], (DEPTH, D_MODEL)),
        "ffn_pre_norm": gain(ks[9], (DEPTH, D_MODEL)),
        "w_gate_up": nrm(ks[10], (DEPTH, D_MODEL, 2 * D_FF), D_MODEL ** -0.5),
        "w_down": nrm(ks[11], (DEPTH, D_FF, D_MODEL), D_FF ** -0.5),
        "ffn_post_norm": gain(ks[12], (DEPTH, D_MODEL)),
        "ple_proj": nrm(ks[13], (DEPTH, PLE_DIM, D_MODEL), PLE_DIM ** -0.5),
        "ple_gate": nrm(ks[14], (DEPTH, D_MODEL, D_MODEL), D_MODEL ** -0.5),
    }

def first_block(x, p, attn_pre_norm, w_in, hg_lower_gamma, hg_out_norm, sb_out_norm, w_out,
              attn_post_norm, ffn_pre_norm, w_gate_up, w_down, ffn_post_norm, ple_proj, ple_gate):
    B, T, _ = x.shape
    lb_all = jnp.cumsum(jax.nn.softmax(hg_lower_gamma.astype(jnp.float32), axis=0), axis=0)
    splits = [HG_WIDTH, 2 * HG_WIDTH, 3 * HG_WIDTH, 4 * HG_WIDTH,
              4 * HG_WIDTH + SB_WIDTH, 4 * HG_WIDTH + 2 * SB_WIDTH]
    h = x
    for i in range(DEPTH):
        u = rmsnorm(h, attn_pre_norm[i])
        proj = u @ w_in[i]
        hq, hf, hi, hg, sq, sk, sv = jnp.split(proj, splits, axis=-1)
        o_hg = hgrn2_mix(hq, hf, hi, lb_all[i])
        o_hg = rmsnorm(o_hg.astype(x.dtype), hg_out_norm[i]) * jax.nn.silu(hg)
        o_sb = stick_breaking_mix(sq.reshape(B, T, SB_HEADS, SB_DH),
                                  sk.reshape(B, T, SB_HEADS, SB_DH),
                                  sv.reshape(B, T, SB_HEADS, SB_DH)).reshape(B, T, SB_WIDTH)
        o_sb = rmsnorm(o_sb, sb_out_norm[i])
        mix = jnp.concatenate([o_hg, o_sb], axis=-1) @ w_out[i]
        h = h + rmsnorm(mix, attn_post_norm[i])
        u = rmsnorm(h, ffn_pre_norm[i])
        gate, up = jnp.split(u @ w_gate_up[i], [D_FF], axis=-1)
        y = (jax.nn.silu(gate) * up) @ w_down[i]
        h = h + rmsnorm(y, ffn_post_norm[i])
        h = h + (p[i] @ ple_proj[i]) * jax.nn.sigmoid(h @ ple_gate[i])
    return h


D_MIX = D_MODEL
D_LRU = D_MIX // 2
LRU_HEADS = 8
LRU_HEAD_DIM = D_LRU // LRU_HEADS
CONV_WIDTH = 4
LRU_C = 8.0
D_GLA = D_MIX - D_LRU
GLA_HEADS = 4
GLA_DV = D_GLA // GLA_HEADS
GLA_DK = GLA_DV // 2
GLA_GATE_RANK = 16
GLA_GATE_NORM = 16.0
GLA_CHUNK = 64
N_GROUPS = 4
EXPERTS_PER_GROUP = 8
N_EXPERTS = N_GROUPS * EXPERTS_PER_GROUP
TOP_K = 2
D_EXPERT = D_MODEL // 2
MOE_BLOCK = 256
D_IN_PROJ = 2 * D_LRU + 2 * GLA_HEADS * GLA_DK + 2 * D_GLA + GLA_GATE_RANK


def rms_norm(x, gain):
    x32 = x.astype(jnp.float32)
    y = x32 * lax.rsqrt(jnp.mean(x32 * x32, axis=-1, keepdims=True) + EPS)
    return (y * gain.astype(jnp.float32)).astype(x.dtype)

def causal_depthwise_conv(x, w, b):
    seq = x.shape[1]
    xp = jnp.pad(x, ((0, 0), (CONV_WIDTH - 1, 0), (0, 0)))
    return b + sum(w[k] * xp[:, k:k + seq] for k in range(CONV_WIDTH))

def rg_lru(x, w_r, b_r, w_i, b_i, lam):
    bsz, seq, width = x.shape
    xh = x.reshape(bsz, seq, LRU_HEADS, LRU_HEAD_DIM)
    r = jax.nn.sigmoid(jnp.einsum("bshi,hij->bshj", xh, w_r).reshape(bsz, seq, width) + b_r)
    gate_i = jax.nn.sigmoid(jnp.einsum("bshi,hij->bshj", xh, w_i).reshape(bsz, seq, width) + b_i)
    log_a = -LRU_C * r.astype(jnp.float32) * jax.nn.softplus(-lam.astype(jnp.float32))
    a = jnp.exp(log_a)
    u = jnp.sqrt(-jnp.expm1(2.0 * log_a)) * (gate_i * x).astype(jnp.float32)

    def step(h, au):
        a_t, u_t = au
        h = a_t * h + u_t
        return h, h

    _, hs = lax.scan(step, jnp.zeros((bsz, width), jnp.float32),
                     (a.swapaxes(0, 1), u.swapaxes(0, 1)))
    return hs.swapaxes(0, 1).astype(x.dtype)

def gla_chunked(q, k, v, log_alpha):
    bsz, seq, nh, dk = q.shape
    dv = v.shape[-1]
    n = seq // GLA_CHUNK
    f32 = jnp.float32
    q = q.astype(f32).reshape(bsz, n, GLA_CHUNK, nh, dk) * dk ** -0.5
    k = k.astype(f32).reshape(bsz, n, GLA_CHUNK, nh, dk)
    v32 = v.astype(f32).reshape(bsz, n, GLA_CHUNK, nh, dv)
    b = jnp.cumsum(log_alpha.astype(f32).reshape(bsz, n, GLA_CHUNK, nh, dk), axis=2)
    b_last = b[:, :, -1]
    q_dec = q * jnp.exp(b)
    scores = jnp.einsum("bnchd,bnshd->bnhcs", q_dec, k * jnp.exp(-b))
    causal = jnp.tril(jnp.ones((GLA_CHUNK, GLA_CHUNK), dtype=bool))
    scores = jnp.where(causal, scores, 0.0)
    o_intra = jnp.einsum("bnhcs,bnshe->bnche", scores, v32)
    chunk_kv = jnp.einsum("bnchd,bnche->bnhde", k * jnp.exp(b_last[:, :, None] - b), v32)

    def step(state, inp):
        decay, kv = inp
        return decay[..., None] * state + kv, state

    _, states = lax.scan(step, jnp.zeros((bsz, nh, dk, dv), f32),
                         (jnp.exp(b_last).swapaxes(0, 1), chunk_kv.swapaxes(0, 1)))
    o_inter = jnp.einsum("bnchd,bnhde->bnche", q_dec, states.swapaxes(0, 1))
    return (o_intra + o_inter).reshape(bsz, seq, nh, dv).astype(v.dtype)

def hierarchical_moe(h, w_coarse, b_coarse, w_fine, b_fine, w_gate, w_up, w_down):
    bsz, seq, d = h.shape
    f32 = jnp.float32
    n_tok = bsz * seq
    xf = h.reshape(n_tok, d)
    coarse_logits = (xf @ w_coarse).astype(f32) + b_coarse.astype(f32)
    coarse_p = jax.nn.softmax(coarse_logits, axis=-1)
    grp = jnp.argmax(coarse_logits, axis=-1).astype(jnp.int32)
    p_grp = jnp.take_along_axis(coarse_p, grp[:, None], axis=-1)
    fine_logits = ((xf @ w_fine).astype(f32) + b_fine.astype(f32)).reshape(
        n_tok, N_GROUPS, EXPERTS_PER_GROUP)
    fine_logits = jnp.take_along_axis(fine_logits, grp[:, None, None], axis=1)[:, 0]
    top_p, top_i = lax.top_k(jax.nn.softmax(fine_logits, axis=-1), TOP_K)
    weights = p_grp * top_p / jnp.sum(top_p, axis=-1, keepdims=True)
    experts = grp[:, None] * EXPERTS_PER_GROUP + top_i.astype(jnp.int32)

    n_assign = n_tok * TOP_K
    flat_e = experts.reshape(n_assign)
    flat_t = jnp.repeat(jnp.arange(n_tok, dtype=jnp.int32), TOP_K)
    flat_w = weights.reshape(n_assign)
    order = jnp.argsort(flat_e)
    se, st, sw = flat_e[order], flat_t[order], flat_w[order]
    counts = jnp.bincount(flat_e, length=N_EXPERTS)
    starts = jnp.cumsum(counts) - counts
    padded = (counts + MOE_BLOCK - 1) // MOE_BLOCK * MOE_BLOCK
    pends = jnp.cumsum(padded)
    dest = (pends - padded)[se] + jnp.arange(n_assign, dtype=jnp.int32) - starts[se]
    cap = (n_assign + MOE_BLOCK - 1) // MOE_BLOCK * MOE_BLOCK + N_EXPERTS * MOE_BLOCK
    n_blocks = cap // MOE_BLOCK
    buf_t = jnp.zeros((cap,), jnp.int32).at[dest].set(st)
    buf_w = jnp.zeros((cap,), f32).at[dest].set(sw)
    block_e = jnp.minimum(
        jnp.searchsorted(pends, jnp.arange(n_blocks, dtype=jnp.int32) * MOE_BLOCK, side="right"),
        N_EXPERTS - 1)

    def run_block(args):
        tok, e = args
        xb = xf[tok]
        hid = jax.nn.silu(xb @ w_gate[e]) * (xb @ w_up[e])
        return hid @ w_down[e]

    outs = lax.map(run_block, (buf_t.reshape(n_blocks, MOE_BLOCK), block_e))
    y = jnp.zeros((n_tok, d), f32).at[buf_t].add(
        outs.reshape(cap, d).astype(f32) * buf_w[:, None])
    return y.reshape(bsz, seq, d).astype(h.dtype)

def second_inputs(seed: int = 0) -> dict:
    key = jax.random.key(seed)
    ks = jax.random.split(key, 32)
    f32 = jnp.float32
    L = DEPTH
    qk = GLA_HEADS * GLA_DK

    def nrm(k, shape, scale):
        return jax.random.normal(k, shape, f32) * scale

    a_c = jax.random.uniform(ks[14], (L, D_LRU), f32, 0.9, 0.999)
    a_base = a_c ** (1.0 / LRU_C)
    lru_lambda = jnp.log(a_base) - jnp.log1p(-a_base)
    return {
        "x": nrm(ks[0], (BATCH, SEQ, D_MODEL), 1.0),
        "c": nrm(ks[1], (BATCH, D_MODEL), 1.0),
        "w_ada": nrm(ks[2], (L, D_MODEL, 6 * D_MODEL), D_MODEL ** -0.5),
        "b_ada": nrm(ks[3], (L, 6 * D_MODEL), 0.02),
        "g_mix": 1.0 + nrm(ks[4], (L, D_MODEL), 0.1),
        "g_ffn": 1.0 + nrm(ks[5], (L, D_MODEL), 0.1),
        "g_final": 1.0 + nrm(ks[6], (D_MODEL,), 0.1),
        "w_in": nrm(ks[7], (L, D_MODEL, D_IN_PROJ), D_MODEL ** -0.5),
        "conv_w": nrm(ks[8], (L, CONV_WIDTH, D_LRU), CONV_WIDTH ** -0.5),
        "conv_b": nrm(ks[9], (L, D_LRU), 0.02),
        "lru_wr": nrm(ks[10], (L, LRU_HEADS, LRU_HEAD_DIM, LRU_HEAD_DIM), LRU_HEAD_DIM ** -0.5),
        "lru_br": nrm(ks[11], (L, D_LRU), 0.02),
        "lru_wi": nrm(ks[12], (L, LRU_HEADS, LRU_HEAD_DIM, LRU_HEAD_DIM), LRU_HEAD_DIM ** -0.5),
        "lru_bi": nrm(ks[13], (L, D_LRU), 0.02),
        "lru_lambda": lru_lambda,
        "gla_wa2": nrm(ks[15], (L, GLA_GATE_RANK, qk), GLA_GATE_RANK ** -0.5),
        "gla_ba": nrm(ks[16], (L, qk), 0.02),
        "gla_gnorm": 1.0 + nrm(ks[17], (L, GLA_DV), 0.1),
        "w_out": nrm(ks[18], (L, D_MIX, D_MODEL), D_MIX ** -0.5),
        "w_coarse": nrm(ks[19], (L, D_MODEL, N_GROUPS), D_MODEL ** -0.5),
        "b_coarse": nrm(ks[20], (L, N_GROUPS), 0.01),
        "w_fine": nrm(ks[21], (L, D_MODEL, N_EXPERTS), D_MODEL ** -0.5),
        "b_fine": nrm(ks[22], (L, N_EXPERTS), 0.01),
        "w_gate": nrm(ks[23], (L, N_EXPERTS, D_MODEL, D_EXPERT), D_MODEL ** -0.5),
        "w_up": nrm(ks[24], (L, N_EXPERTS, D_MODEL, D_EXPERT), D_MODEL ** -0.5),
        "w_down": nrm(ks[25], (L, N_EXPERTS, D_EXPERT, D_MODEL), D_EXPERT ** -0.5),
    }

def second_block(x, c, w_ada, b_ada, g_mix, g_ffn, g_final, w_in, conv_w, conv_b, lru_wr, lru_br,
              lru_wi, lru_bi, lru_lambda, gla_wa2, gla_ba, gla_gnorm, w_out, w_coarse, b_coarse,
              w_fine, b_fine, w_gate, w_up, w_down):
    bsz, seq, _ = x.shape
    qk = GLA_HEADS * GLA_DK
    splits = [D_LRU, 2 * D_LRU, 2 * D_LRU + qk, 2 * D_LRU + 2 * qk,
              2 * D_LRU + 2 * qk + D_GLA, 2 * D_LRU + 2 * qk + 2 * D_GLA]
    for l in range(DEPTH):
        mod = jax.nn.silu(c) @ w_ada[l] + b_ada[l]
        sh1, sc1, gt1, sh2, sc2, gt2 = [m[:, None, :] for m in jnp.split(mod, 6, axis=-1)]

        h = rms_norm(x, g_mix[l]) * (1 + sc1) + sh1
        proj = h @ w_in[l]
        lru_x, lru_y, q, k, v, g_out, gate_lr = jnp.split(proj, splits, axis=-1)

        lru_h = rg_lru(causal_depthwise_conv(lru_x, conv_w[l], conv_b[l]),
                       lru_wr[l], lru_br[l], lru_wi[l], lru_bi[l], lru_lambda[l])
        lru_out = lru_h * jax.nn.gelu(lru_y)

        log_alpha = jax.nn.log_sigmoid(
            (gate_lr @ gla_wa2[l] + gla_ba[l]).astype(jnp.float32)) / GLA_GATE_NORM
        o = gla_chunked(q.reshape(bsz, seq, GLA_HEADS, GLA_DK),
                        k.reshape(bsz, seq, GLA_HEADS, GLA_DK),
                        v.reshape(bsz, seq, GLA_HEADS, GLA_DV),
                        log_alpha.reshape(bsz, seq, GLA_HEADS, GLA_DK))
        gla_out = rms_norm(o, gla_gnorm[l]).reshape(bsz, seq, D_GLA) * jax.nn.silu(g_out)

        mix = jnp.concatenate([lru_out, gla_out], axis=-1) @ w_out[l]
        x = x + gt1 * mix

        h2 = rms_norm(x, g_ffn[l]) * (1 + sc2) + sh2
        x = x + gt2 * hierarchical_moe(h2, w_coarse[l], b_coarse[l], w_fine[l], b_fine[l],
                                       w_gate[l], w_up[l], w_down[l])
    return rms_norm(x, g_final)


def setup_inputs(seed=0):
    out = dict(first_inputs(seed))
    for name, value in second_inputs(seed + 1).items():
        if name != "x":
            out[name + "_2"] = value
    return out


def reference(
    x, p, attn_pre_norm, w_in, hg_lower_gamma, hg_out_norm, sb_out_norm, w_out, attn_post_norm,
    ffn_pre_norm, w_gate_up, w_down, ffn_post_norm, ple_proj, ple_gate, c_2, w_ada_2, b_ada_2,
    g_mix_2, g_ffn_2, g_final_2, w_in_2, conv_w_2, conv_b_2, lru_wr_2, lru_br_2, lru_wi_2,
    lru_bi_2, lru_lambda_2, gla_wa2_2, gla_ba_2, gla_gnorm_2, w_out_2, w_coarse_2, b_coarse_2,
    w_fine_2, b_fine_2, w_gate_2, w_up_2, w_down_2,
):
    x = first_block(
        x, p, attn_pre_norm, w_in, hg_lower_gamma, hg_out_norm, sb_out_norm, w_out,
        attn_post_norm, ffn_pre_norm, w_gate_up, w_down, ffn_post_norm, ple_proj, ple_gate,
    )
    return second_block(
        x, c_2, w_ada_2, b_ada_2, g_mix_2, g_ffn_2, g_final_2, w_in_2, conv_w_2, conv_b_2,
        lru_wr_2, lru_br_2, lru_wi_2, lru_bi_2, lru_lambda_2, gla_wa2_2, gla_ba_2, gla_gnorm_2,
        w_out_2, w_coarse_2, b_coarse_2, w_fine_2, b_fine_2, w_gate_2, w_up_2, w_down_2,
    )


_drawn_inputs = setup_inputs


def setup_inputs(seed=0):
    import zlib

    import numpy as np

    out = dict(_drawn_inputs(seed))
    spreads = {}
    factors = {'conv_b_2': 3.393,
     'lru_br_2': 23.312,
     'lru_bi_2': 7.56,
     'gla_ba_2': 8.0,
     'b_coarse_2': 28.581,
     'b_fine_2': 8.0}
    for name, (base, spread) in spreads.items():
        noise = np.random.default_rng([zlib.crc32(name.encode()), seed]).standard_normal(out[name].shape)
        drawn = base * np.exp(spread * noise) if base else spread * noise
        out[name] = __import__('jax').numpy.asarray(drawn.astype(out[name].dtype))
    for name, factor in factors.items():
        out[name] = (out[name] * factor).astype(out[name].dtype)
    return out
```

```python
from contextlib import ExitStack

import concourse.bass as bass
from concourse import mybir

F32 = mybir.dt.float32
I32 = mybir.dt.int32
U32 = mybir.dt.uint32
ALU = mybir.AluOpType
ACT = mybir.ActivationFunctionType
AX = mybir.AxisListType

P = 128
EPS = 1e-6
SQRT_2_OVER_PI = 0.7978845608028654
GELU_CUBIC = 0.044715
NEG_BIG = -1.0e30


def build_program(nc, d, out):
    T, D = d["x"].shape[1:]
    KT = D // P
    TT = T // P
    D_FF = d["w_down"].shape[1]
    IN1 = d["w_in"].shape[2]
    IN2 = d["w_in_2"].shape[2]
    PLE = d["p"].shape[3]
    HW = d["hg_out_norm"].shape[1]
    HT = HW // P
    HG_HEADS = HT
    SB_DH = 64
    SB_HEADS = HW // SB_DH
    SCALE_SB = float(SB_DH) ** -0.5
    GLA_HEADS, GLA_DK = 4, 64
    GLA_QT = GLA_HEADS * GLA_DK // P
    GLA_CHUNK = 64
    GATE_RANK = d["gla_wa2_2"].shape[1]
    GATE_NORM = 16.0
    LRU_C = 8.0
    NE, _, DE = d["w_gate_2"].shape[1:]
    NG = d["w_coarse_2"].shape[2]
    EPG = NE // NG
    TOPK = 2
    SLOTS = TOPK * T
    WIN = 32
    NWIN = T // WIN
    PADDED = SLOTS + T
    CH = 2048
    assert (T, D, DE, NE) == (256, 1024, 512, 32) and HW == 512

    ctx = ExitStack()
    with ctx:
        def sb(name, shape, dt=F32):
            return ctx.enter_context(nc.sbuf_tensor(name, shape, dt))

        shared, outs = {}, 0
        for n, (norm, tiles) in enumerate((("n1", KT), ("nhg", HT), ("nsb", HT), ("npost", KT),
                                           ("nffn", KT), ("nfpost", KT), ("nmix2", KT),
                                           ("nffn2", KT))):
            for part in ("sq", "ss", "rms", "rinv"):
                shared[f"{norm}_{part}"] = (f"norm_{part}", n)
            shared[f"{norm}_out"] = ("norm_out", outs)
            outs += tiles
        for layers in ((("proj1", IN1 // 512), ("proj2", IN2 // 512)),
                       (("wout1", D // 512), ("pgate", D // 512), ("wout2", D // 512))):
            group, rounds = layers[0][0], 0
            for layer, n in layers:
                for j in range(2):
                    shared[f"{layer}_full{j}"] = (f"{group}_slot{j}_full", 16 * rounds)
                    shared[f"{layer}_done{j}"] = (f"{group}_slot{j}_done", rounds)
                    shared[f"{layer}_out{j}"] = (f"{group}_bank{j}_out", rounds + 1)
                rounds += n

        FREE = {"act": ["proj1_out0", "wout1_out0", "silu_ready"],
                "dve": ["proj1_out1", "wout1_out1", "hid_ready", "yt_out0", "yt_out1",
                        "byt_out0", "byt_out1"],
                "pe": ["down_done", "gu_free0", "gu_free1", "d_free0", "d_free1"]}
        for names in FREE.values():
            for name in names:
                shared.setdefault(name, (name, 1))

        levels = 8
        for engine, steps in (
                ("act_a", (("hT_ready", 4), ("vec_ready", 2), ("pT_ready", 1), ("lb_ready", 2),
                           ("csig_ready", 1), ("hg_sig", 4), ("g_ready", 1), ("vtok_ready", 4),
                           ("z_out", 8), ("sp", 3), ("e_ready", levels), ("a_ready", 8),
                           ("ohg_out", 2), ("osb_out", 2), ("y_out", 4), ("pp_out", 4))),
                ("act_b", (("lam", 3), ("glr_out", 1), ("gv_out", 2), ("ga", 5), ("ge_ready", 4),
                           ("lgate_out", 8), ("lru_a", 1), ("lru_th", 1), ("gelu_tanh", 1),
                           ("lru_root", 1), ("gout_ready", 1), ("og_out", 2), ("og_sq", 1),
                           ("og_rms", 2), ("ec_ready", 1), ("h2tok", 4), ("x2tok", 4),
                           ("e21_ready", 1), ("xs_out", 8), ("pwt_out", 2), ("yt_out", 8))),
                ("dve_a", (("lbd_ready", 1), ("csil_ready", 1), ("crep_ready", 8), ("f_ready", 4),
                           ("q_ready", 1), ("k_ready", 4), ("hgate_ready", 1), ("b_ready", 4),
                           ("lv_zero", 5), ("ada_row", 3), ("mod_ready", 3), ("sp_full", 8),
                           ("lm_ready", 8), ("sx_ready", 8), ("ohg_ready", 1), ("h1_ready", 1),
                           ("h2_ready", 1), ("ple_ready", 1), ("h3_ready", 1))),
                ("dve_b", (("gs_ready", 2), ("lam_v", 3), ("conv", 16), ("ls_ready", 1),
                           ("b64_ready", 8), ("b256_ready", 2), ("la_ready", 4), ("gi_ready", 1),
                           ("gelu_a", 2), ("gelu_in", 1), ("a2_ready", 1), ("lru_m", 1),
                           ("gelu_y", 1), ("u_ready", 1), ("lru_h", 4), ("og_rinv", 1),
                           ("og_normed", 1), ("x2_ready", 8), ("cs_ready", 1), ("a_set", 1),
                           ("dm_ready", 1), ("tbl_ready", 2), ("psel_ready", 2), ("pw_ready", 2),
                           ("x3_ready", 4))),
                ("pe_a", (("xT_done", 4), ("vT_done", 1), ("vtok_done", 4), ("z_done", 8),
                          ("lv_done", levels + 1), ("mod_done", 3), ("sx_done", 8),
                          ("ohg_done", 2), ("osb_done", 2), ("y_done", 1), ("pp_done", 4))),
                ("pe_b", (("glr_done", 1), ("gv_done", 2), ("ga_done", 1), ("lgate_done", 2),
                          ("gl_done", 6), ("og_done", 2), ("og_ss", 2), ("lg_done", 2),
                          ("tok_done", 8), ("rank_done", 1), ("xs_done", 8), ("pwt_done", 2),
                          ("pw_done", 1), ("yt_done", 8), ("comb_done", 4)))):
            done = 0
            for name, n in steps:
                shared[name] = (f"{engine}_steps", done)
                done += n

        sems = {}

        def sem(name):
            name, _ = shared.get(name, (name, 0))
            if name not in sems:
                sems[name] = ctx.enter_context(nc.semaphore(name))
            return sems[name]

        Wlo = sb("Wlo", [P, 6 * CH])
        Whi = sb("Whi", [P, 6 * CH])
        slot = [Wlo[:, i * CH:(i + 1) * CH] for i in range(6)]
        slot += [Whi[:, i * CH:(i + 1) * CH] for i in range(6)]
        projR = sb("projR", [P, (IN1 // P) * T])
        R24 = sb("R24", [P, 3 * KT * T])
        hT = sb("hT", [P, KT * T])
        mixin = sb("mixin", [P, KT * T])
        G4 = sb("G4", [P, HT * T])
        T4 = sb("T4", [P, HT * T])
        V4 = sb("V4", [P, TT * HW])
        SV4 = sb("SV4", [P, TT * HW])
        S4 = sb("S4", [P, HT * T])
        SX2 = sb("SX2", [P, HT * P])
        rms = sb("rms", [P, HT * T])

        uT = R24[:, 0:KT * T]
        sq = R24[:, KT * T:2 * KT * T]
        xk = R24[:, 2 * KT * T:3 * KT * T]
        mixT = Whi[:, 5 * CH:6 * CH]
        zb = Whi[:, 0:3072]
        lb_ = Whi[:, 3072:6144]
        eb = Whi[:, 6144:9216]

        ident = sb("ident", [P, P])
        ones = sb("ones", [P, T])
        tri_ge = sb("tri_ge", [P, P])
        tri_lt = sb("tri_lt", [P, P])
        LEVELS = [1, 2, 4, 8, 16, 32, 64]
        lmask = sb("lmask", [P, 9, P])
        DIAG, CHUNK = 7, 8
        negm = sb("negm", [P, 3 * P])
        bigm = sb("bigm", [P, 3 * P])
        epsc = sb("epsc", [P, 1])
        vrow = sb("vrow", [P, P])
        brow = sb("brow", [P, P])
        vec = sb("vec", [P, P])
        badaT = sb("badaT", [P, 6 * KT])
        modT = sb("modT", [P, 6 * KT])
        small = sb("small", [P, 64])

        VROWS = [("attn_pre_norm", KT), ("hg_lower_gamma", 2 * HT), ("hg_out_norm", HT),
                 ("sb_out_norm", HT), ("attn_post_norm", KT), ("ffn_pre_norm", KT),
                 ("ffn_post_norm", KT), ("c_2", KT), ("g_mix_2", KT), ("g_ffn_2", KT),
                 ("conv_w_2", 4 * HT), ("conv_b_2", HT), ("lru_br_2", HT), ("lru_bi_2", HT),
                 ("lru_lambda_2", HT), ("gla_ba_2", GLA_QT), ("gla_gnorm_2", 1)]
        VO, at = {}, 0
        for name, n in VROWS:
            VO[name] = at
            at += n
        NV = at

        def v(name, k=0):
            return vec[:, VO[name] + k:VO[name] + k + 1]

        bank = [ctx.enter_context(nc.psum_tensor(f"bank{i}", [P, 512], F32)) for i in range(8)]

        def tile(region, k, n=1):
            return region[:, k * T:(k + n) * T]

        def half(region, k, t):
            return region[:, k * T + t * P:k * T + (t + 1) * P]

        def vector_rows(name):
            src = d[name]
            if len(src.shape) == 3:
                src = src.rearrange("a b n -> a (b n)")
            return src.rearrange("a (k p) -> (a k) p", p=P)

        x_tok = xk
        p_tok = sb("p_tok", [P, TT * PLE])
        pT = sb("pT", [P, (PLE // P) * T])
        crep = sb("crep", [P, KT * 36])
        csil = sb("csil", [P, KT])
        cnow = crep[:, KT * 32:KT * 36]

        def upto(name, value=1):
            _, before = shared.get(name, (name, 0))
            return sem(name), value + before

        def signal_free(e, engine):
            for name in FREE[engine]:
                e.drain().then_inc(sem(name), 1)

        proj1 = ("proj1", d["w_in"][0], IN1 // 256, (0, 1), (0, 1))
        wout1 = ("wout1", d["w_out"][0], D // 256, (2, 3), (2, 3))
        pgate = ("pgate", d["ple_gate"][0], D // 256, (2, 3), (2, 3))

        proj2 = ("proj2", d["w_in_2"][0], IN2 // 256, (0, 1), (0, 1))
        wout2 = ("wout2", d["w_out_2"][0], D // 256, (2, 3), (2, 3))
        IN2_FULL = IN2 // 256 * 256

        def sp_dense(sp, layer):
            name, w, n, sl, _ = layer
            wv = w.rearrange("(k p) n -> p k n", p=P)
            for j in range(2):
                sp.dma_start(slot[sl[j]].rearrange("p (k n) -> p k n", k=KT),
                             wv[:, :, j * 256:(j + 1) * 256]).then_inc(sem(f"{name}_full{j}"), 16)
            with sp.Fori(1, n // 2) as i:
                for j in range(2):
                    sp.wait_ge(*upto(f"{name}_done{j}", i))
                    sp.dma_start(slot[sl[j]].rearrange("p (k n) -> p k n", k=KT),
                                 wv[:, :, bass.ds(i * 512 + j * 256, 256)]
                                 ).then_inc(sem(f"{name}_full{j}"), 16)

        def pe_chunk(pe, b, w, src, name):
            for t in range(2):
                for k in range(KT):
                    mm = pe.matmul(b[:, t * T:(t + 1) * T],
                                   w[:, k * 256 + t * P:k * 256 + (t + 1) * P],
                                   tile(src, k), start=(k == 0), stop=(k == KT - 1))
            mm.then_inc(sem(name), 1)

        def pe_dense(pe, layer, src):
            name, _, n, sl, bk = layer
            with pe.Fori(0, n // 2) as i:
                for j in range(2):
                    pe.wait_ge(*upto(f"{name}_full{j}", i * 16 + 16))
                    pe.wait_ge(*upto(f"{name}_out{j}", i))
                    pe_chunk(pe, bank[bk[j]], slot[sl[j]], src, f"{name}_done{j}")

        def out_dense(e, layer, j, dst):
            name, _, n, _, bk = layer
            with e.Fori(0, n // 2) as i:
                e.wait_ge(*upto(f"{name}_done{j}", i + 1))
                to = dst[:, bass.ds(i * 1024 + j * 512, 512)]
                if j == 0:
                    ins = e.activation(to, bank[bk[j]][:, :], ACT.Copy)
                else:
                    ins = e.tensor_copy(to, bank[bk[j]][:, :])
                ins.then_inc(sem(f"{name}_out{j}"), 1)

        def rms_of(name):
            return rms[:, T:2 * T] if name == "nsb" else rms[:, 0:T]

        def act_norm(act, name, src, n, width):
            act.activation(sq[:, 0:n * T], src, ACT.Square).then_inc(sem(f"{name}_sq"), 1)
            act.wait_ge(*upto(f"{name}_ss"))
            act.activation(rms_of(name), bank[7][:, 0:T], ACT.Sqrt, bias=epsc[:, :],
                           scale=1.0 / width).then_inc(sem(f"{name}_rms"), 1)

        def pe_norm(pe, name, n):
            pe.wait_ge(*upto(f"{name}_sq"))
            for k in range(n):
                mm = pe.matmul(bank[7][:, 0:T], ones[:, 0:P], tile(sq, k),
                               start=(k == 0), stop=(k == n - 1))
            mm.then_inc(sem(f"{name}_ss"), 1)

        def dve_norm(dve, name, src, gain, dst, n):
            dve.wait_ge(*upto(f"{name}_rms"))
            dve.reciprocal(rms_of(name), rms_of(name)).then_inc(sem(f"{name}_rinv"), 1)
            dve.wait_ge(*upto(f"{name}_rinv"))
            for k in range(n):
                dve.scalar_tensor_tensor(out=tile(dst, k), in0=tile(src, k), scalar=gain(k),
                                         in1=rms_of(name), op0=ALU.mult, op1=ALU.mult
                                         ).then_inc(sem(f"{name}_out"), 1)

        mixT2 = xk
        XC = V4[:, :]
        A8 = mixin[:, HT * T:2 * HT * T]
        gel, th = xk[:, 0:1024], xk[:, 1024:2048]
        e2 = [uT[:, 0:512], uT[:, 512:1024]]
        b64, b256 = uT[:, 1024:1536], uT[:, 1536:2048]
        q2 = [sq[:, 0:512], sq[:, 512:1024]]
        k2 = [sq[:, 1024:1536], sq[:, 1536:2048]]
        GV = projR[:, 20 * T:20 * T + TT * HW]
        TA, TA1, TA2 = 384, 448, 512
        lsx = SV4
        wrb = projR[:, 24 * T:24 * T + HT * P]
        wib = projR[:, 26 * T:26 * T + HT * P]
        wa2 = rms[0:GATE_RANK, 3 * T:4 * T]
        wlr = SX2
        glr = rms[0:GATE_RANK, 2 * T:3 * T]
        wcf = crep
        bcf = sb("bcf", [1, NG + NE])
        gfin = rms
        gs = sb("gs", [P, 2 * KT])
        lru = sb("lru", [P, 4 * HT])
        NL = NG + NE
        lg = vrow[:, 0:TT * NL]
        rt = V4
        rs = vrow[:, 96:P]
        tbl = sb("tbl", [1, 2 * NE], I32)
        iot = p_tok
        iotg = brow[:, 0:TT * NE]
        iotc = brow[:, TT * NE:TT * NL]
        xsT = projR[:, 0:KT * PADDED].rearrange("p (k s) -> p k s", k=KT)
        ysT = R24[:, :].rearrange("p (k s) -> p k s", k=KT)
        h2tok = sq
        x2tok = mixin
        Psel = T4[:, :].rearrange("p (t s) -> p t s", t=TT)
        Pw = S4[:, :].rearrange("p (t s) -> p t s", t=TT)
        PwT = G4[:, :].rearrange("p (c t) -> p c t", t=T)
        xw = [S4[:, 0:KT * WIN], S4[:, KT * WIN:2 * KT * WIN]]
        sil, hid = V4[2 * WIN:P, 0:256], V4[2 * WIN:P, 256:512]
        hidw = V4[:, 256:512]
        hidT, yb = SV4[:, 0:P], SV4[:, P:P + 256]
        ystok = projR[:, 0:SLOTS // P * D]
        Wx = [Whi, Wlo]
        WG, WU, WD = 0, KT * DE, 2 * KT * DE

        qd = [sq[:, 0:1024], sq[:, 1024:2048]]
        kd = [xk[:, 0:1024], xk[:, 1024:2048]]
        ed = [uT[:, 0:1024], uT[:, 1024:2048]]
        ALL_LEVELS = LEVELS + [P]
        NC1 = 3 * len(LEVELS) + 4
        hb = G4[:, :]

        def blocks(ap, L):
            return ap.rearrange("p (n l) -> p n l", l=2 * L)

        def mod_row(b):
            return mixin[:, b * 512:(b + 1) * 512]

        block = ctx.enter_context(nc.Block())

        ffn_g = d["w_gate_up"][0].rearrange("(k p) n -> p k n", p=P)
        ffn_d = d["w_down"][0].rearrange("(k p) n -> p k n", p=P)
        NF = D_FF // 256
        ada_w = d["w_ada_2"][0].rearrange("(k p) n -> p k n", p=P)
        ADA_B = 6 * D // CH
        ADA_SLOT = 6
        ADA_AFTER = ((0,), (1, 2))
        assert IN1 // 512 == KT - 1

        @block.sync
        def _(sp):
            def proj1_load(i, j):
                sp.dma_start(slot[j].rearrange("p (k n) -> p k n", k=KT),
                             d["w_in"][0].rearrange("(k p) n -> p k n", p=P)
                             [:, :, bass.ds(i * 512 + j * 256, 256)]
                             ).then_inc(sem(f"proj1_full{j}"), 16)

            for name, n in VROWS[0::2]:
                sp.dma_start(vrow[VO[name]:VO[name] + n, :], vector_rows(name)
                             ).then_inc(sem("v_in"), 16)
            sp.wait_ge(*upto("x_in", 16))

            def ada_load(k, b):
                sp.dma_start(slot[ADA_SLOT + b],
                             ada_w[:, bass.ds(k, 1), b * CH:(b + 1) * CH].rearrange("p k n -> p (k n)")
                             ).then_inc(sem(f"ada_full{b}"), 16)

            for j in range(2):
                proj1_load(0, j)
            for b in range(ADA_B):
                ada_load(0, b)
            for b in range(ADA_B):
                sp.wait_ge(*upto(f"ada_done{b}", 1))
                ada_load(1, b)
            with sp.Fori(1, IN1 // 512) as i:
                for j in range(2):
                    sp.wait_ge(*upto(f"proj1_done{j}", i))
                    proj1_load(i, j)
                    for b in ADA_AFTER[j]:
                        sp.wait_ge(*upto(f"ada_done{b}", i + 1))
                        ada_load(i + 1, b)
            sp_dense(sp, wout1)
            sp.wait_ge(*upto("proj1_done0", IN1 // 512))
            sp.wait_ge(*upto("proj1_done1", IN1 // 512))

            def ffn_load(i, first):
                if not first:
                    sp.wait_ge(*upto("gate_done", i))
                sp.dma_start(slot[0].rearrange("p (k n) -> p k n", k=KT),
                             ffn_g[:, :, bass.ds(i * 256, 256)]).then_inc(sem("gate_full"), 16)
                if not first:
                    sp.wait_ge(*upto("up_done", i))
                sp.dma_start(slot[1].rearrange("p (k n) -> p k n", k=KT),
                             ffn_g[:, :, bass.ds(i * 256 + D_FF, 256)]).then_inc(sem("up_full"), 16)
                if not first:
                    sp.wait_ge(*upto("down_done", i))
                sp.dma_start(slot[4].rearrange("p (k n) -> p k n", k=2),
                             ffn_d[:, bass.ds(i * 2, 2), :]).then_inc(sem("down_full"), 16)

            ffn_load(0, True)
            with sp.Fori(1, NF) as i:
                ffn_load(i, False)
            sp.dma_start(slot[5].rearrange("p (k n) -> p k n", k=PLE // P),
                         d["ple_proj"][0].rearrange("(k p) n -> p k n", p=P)
                         ).then_inc(sem("pproj_full"), 16)
            sp.wait_ge(*upto("wout1_done0", 2))
            sp.wait_ge(*upto("wout1_done1", 2))
            sp_dense(sp, pgate)
            sp.wait_ge(*upto("gate_done", NF))
            sp.wait_ge(*upto("up_done", NF))
            sp_dense(sp, proj2)
            sp.wait_ge(*upto("h3_ready"))
            sp.wait_ge(*upto("pgate_done0", 2))
            sp.wait_ge(*upto("pgate_done1", 2))
            sp_dense(sp, wout2)

            def expert_load(e, par, i):
                for name, w, at, n in (("wg", "w_gate_2", WG, KT), ("wu", "w_up_2", WU, KT),
                                       ("wd", "w_down_2", WD, DE // P)):
                    if i is not None and name == "wg":
                        sp.wait_ge(*upto(f"gu_free{par}", i))
                    if i is not None and name == "wd":
                        sp.wait_ge(*upto(f"d_free{par}", i))
                    sp.dma_start(Wx[par][:, at:at + KT * DE].rearrange("p (k n) -> p k n", k=n),
                                 d[w][0][bass.ds(e, 1)].rearrange("a (k p) n -> p (a k) n", p=P)
                                 ).then_inc(sem(f"{name}_full{par}"), 16)

            expert_load(0, 0, None)
            for j in range(2):
                sp.wait_ge(*upto(f"proj2_done{j}", IN2_FULL // 512))
                sp.wait_ge(*upto(f"wout2_done{j}", 2))
            sp.wait_ge(*upto("down_done", NF))
            sp.wait_ge(*upto("pp_done", 4))
            expert_load(1, 1, None)
            sp.wait_ge(*upto("nffn2_out", KT))
            sp.dma_start(gfin[:, :], d["g_final_2"].partition_broadcast(P)
                         ).then_inc(sem("gfin_in"), 16)
            sp.wait_ge(*upto("tbl_ready", 2))
            with sp.Fori(1, NE // 2) as i:
                for par in range(2):
                    count = sp.value_load(tbl[0:1, bass.ds(i * 2 + (NE + par), 1)],
                                          min_val=0, max_val=T)
                    with sp.If(count > 0):
                        expert_load(i * 2 + par, par, i)
                    with sp.Else():
                        sp.wait_ge(*upto(f"gu_free{par}", i))
                        for name in ("wg_full", "wu_full"):
                            sp.drain().then_inc(sem(f"{name}{par}"), 16)
                        sp.wait_ge(*upto(f"d_free{par}", i))
                        sp.drain().then_inc(sem(f"wd_full{par}"), 16)
            sp.wait_ge(*upto("y_ready", 2))
            sp.dma_start(out[0].rearrange("(t p) n -> p t n", p=P),
                         x2tok[:, :].rearrange("p (t n) -> p t n", t=TT)).then_inc(sem("stored"), 16)
            sp.wait_ge(*upto("stored", 16))

        @block.gpsimd
        def _(pool):
            pool.memset(ones[:, :], 1.0).then_inc(sem("ones_set"), 1)
            pool.memset(ident[:, :], 0.0).then_inc(sem("c0"), 1)
            pool.memset(tri_ge[:, :], 1.0).then_inc(sem("c0"), 1)
            pool.memset(tri_lt[:, :], 1.0).then_inc(sem("c0"), 1)
            pool.memset(epsc[:, :], EPS).then_inc(sem("c0"), 1)
            pool.memset(negm[:, :], -1.0).then_inc(sem("c0"), 1)
            pool.memset(bigm[:, :], 0.0).then_inc(sem("c0"), 1)
            pool.memset(lmask[:, :, :], 0.0).then_inc(sem("c0"), 1)
            pool.wait_ge(*upto("c0", 7))
            pool.affine_select(out=ident[:, :], in_=ident[:, :], compare_op=ALU.not_equal, fill=1.0,
                               base=0, pattern=[[-1, P]], channel_multiplier=1
                               ).then_inc(sem("ident_set"), 1)
            pool.affine_select(out=tri_ge[:, :], in_=tri_ge[:, :], compare_op=ALU.is_ge, fill=0.0,
                               base=0, pattern=[[-1, P]], channel_multiplier=1
                               ).then_inc(sem("const"), 1)
            pool.affine_select(out=tri_lt[:, :], in_=tri_lt[:, :], compare_op=ALU.is_gt, fill=0.0,
                               base=0, pattern=[[1, P]], channel_multiplier=-1
                               ).then_inc(sem("const"), 1)
            for m, fill in ((negm, 0.0), (bigm, NEG_BIG)):
                for c in (0, 2):
                    pool.affine_select(out=m[:, c * P:(c + 1) * P], in_=m[:, c * P:(c + 1) * P],
                                       compare_op=ALU.is_gt, fill=fill, base=0, pattern=[[1, P]],
                                       channel_multiplier=-1).then_inc(sem("const"), 1)
            n = 0
            for li, L in enumerate(LEVELS):
                second = blocks(lmask[:, li, :], L)[:, :, L:2 * L]
                pool.memset(second, 1.0).then_inc(sem("c1"), 1)
                pool.wait_ge(*upto("c1", n + 1))
                pool.affine_select(out=second, in_=second, compare_op=ALU.is_ge, fill=0.0, base=0,
                                   pattern=[[-2 * L, P // (2 * L)], [0, L]], channel_multiplier=1
                                   ).then_inc(sem("c1"), 1)
                pool.wait_ge(*upto("c1", n + 2))
                pool.affine_select(out=second, in_=second, compare_op=ALU.is_ge, fill=0.0, base=L - 1,
                                   pattern=[[2 * L, P // (2 * L)], [0, L]], channel_multiplier=-1
                                   ).then_inc(sem("c1"), 1)
                n += 3
            ch = lmask[:, CHUNK, :].rearrange("p (n l) -> p n l", l=GLA_CHUNK)
            pool.memset(ch, 1.0).then_inc(sem("c1"), 1)
            pool.wait_ge(*upto("c1", n + 1))
            pool.affine_select(out=ch, in_=ch, compare_op=ALU.is_ge, fill=0.0, base=0,
                               pattern=[[GLA_CHUNK, P // GLA_CHUNK], [1, GLA_CHUNK]],
                               channel_multiplier=-1).then_inc(sem("c1"), 1)
            pool.wait_ge(*upto("c1", n + 2))
            pool.affine_select(out=ch, in_=ch, compare_op=ALU.is_ge, fill=0.0, base=0,
                               pattern=[[-GLA_CHUNK, P // GLA_CHUNK], [0, GLA_CHUNK]],
                               channel_multiplier=1).then_inc(sem("c1"), 1)
            pool.affine_select(out=lmask[:, DIAG, :], in_=lmask[:, DIAG, :],
                               compare_op=ALU.not_equal, fill=1.0, base=0, pattern=[[-1, P]],
                               channel_multiplier=1).then_inc(sem("c1"), 1)
            pool.wait_ge(*upto("crep_ready", KT))
            with pool.Fori(0, KT - 1) as i:
                pool.wait_ge(*upto("ada_done2", i + 1))
                pool.tensor_copy(cnow, crep[:, bass.ds(i * 32 + 32, 32)]
                                 ).then_inc(sem("cnow_ready"), 1)
            pool.wait_ge(*upto("vtok_done", 2 * TT))
            pool.memset(wrb[:, :], 0.0).then_inc(sem("bd_zero"), 1)
            pool.memset(wib[:, :], 0.0).then_inc(sem("bd_zero"), 1)
            pool.wait_ge(*upto("vT_done"))
            pool.iota(iot[:, :], pattern=[[1, SLOTS]], base=0, channel_multiplier=0,
                      allow_small_or_imprecise_dtypes=True).then_inc(sem("iotas"), 1)
            pool.iota(iotg[:, :], pattern=[[0, TT], [1, NE]], base=0, channel_multiplier=0,
                      allow_small_or_imprecise_dtypes=True).then_inc(sem("iotas"), 1)
            pool.iota(iotc[:, :], pattern=[[0, TT], [1, NG]], base=0, channel_multiplier=0,
                      allow_small_or_imprecise_dtypes=True).then_inc(sem("iotas"), 1)
            pool.wait_ge(*upto("const", 6))
            pool.wait_ge(*upto("z_out", SB_HEADS))
            for h in range(SB_HEADS):
                pool.tensor_tensor(eb[:, h * 384:(h + 1) * 384], zb[:, h * 384:(h + 1) * 384],
                                   bigm[:, :], ALU.add).then_inc(sem("zm_ready"), 1)


            pool.wait_ge(*upto("wout2_done1", 2))
            pool.wait_ge(*upto("mix2_ready", 2))
            pool.memset(xsT[:, :, SLOTS:PADDED], 0.0).then_inc(sem("pad_zero"), 1)
            pool.wait_ge(*upto("pad_zero"))
            pool.wait_ge(*upto("tbl_ready", 2))
            pool.wait_ge(*upto("xs_out", KT))
            pool.wait_ge(*upto("pw_done"))

            def window(start, par, name):
                pool.tensor_copy(xw[par].rearrange("p (k s) -> p k s", k=KT),
                                 xsT[:, :, bass.ds(start, WIN)]
                                 ).then_inc(sem(f"{name}{par}"), 1)

            with pool.Fori(0, NE // 2) as i:
                for par in range(2):
                    start = pool.value_load(tbl[0:1, bass.ds(i * 2 + par, 1)],
                                            min_val=0, max_val=SLOTS)
                    count = pool.value_load(tbl[0:1, bass.ds(i * 2 + (NE + par), 1)],
                                            min_val=0, max_val=T)
                    with pool.If(count > 0):
                        pool.wait_ge(*upto(f"gu_free{par}", i))
                        window(start, par, "xw")
                        with pool.If(count > WIN):
                            pool.wait_ge(*upto(f"gu_done{par}", i + 1))
                            window(start + WIN, par, "bxw")
                            with pool.If(count > 2 * WIN):
                                with pool.Fori(2, NWIN) as w:
                                    with pool.If(count > w * WIN):
                                        pool.wait_ge(*upto(f"bgu_done{par}",
                                                           i * (NWIN - 1) + w - 1))
                                        window(start + w * WIN, par, "bxw")
                                    with pool.Else():
                                        pool.drain().then_inc(sem(f"bxw{par}"), 1)
                            with pool.Else():
                                pool.drain().then_inc(sem(f"bxw{par}"), NWIN - 2)
                        with pool.Else():
                            pool.drain().then_inc(sem(f"bxw{par}"), NWIN - 1)
                    with pool.Else():
                        pool.drain().then_inc(sem(f"xw{par}"), 1)
                        pool.drain().then_inc(sem(f"bxw{par}"), NWIN - 1)

        @block.scalar
        def _(act):
            signal_free(act, "act")
            act.dma_start(x_tok.rearrange("p (t n) -> p t n", t=TT),
                          d["x"][0].rearrange("(t p) n -> p t n", p=P)).then_inc(sem("x_in"), 16)
            for name, n in VROWS[1::2]:
                act.dma_start(vrow[VO[name]:VO[name] + n, :], vector_rows(name)
                              ).then_inc(sem("v_in"), 16)
            act.dma_start(brow[0:6 * KT, :], d["b_ada_2"].rearrange("a (k p) -> (a k) p", p=P)
                          ).then_inc(sem("v_in"), 16)
            act.dma_start(p_tok[:, :].rearrange("p (t n) -> p t n", t=TT),
                          d["p"][0, 0].rearrange("(t p) n -> p t n", p=P)).then_inc(sem("v_in"), 16)

            for b in range(4):
                act.wait_ge(*upto("xT_done", b + 1))
                act.activation(tile(hT, 2 * b, 2), bank[b][:, :], ACT.Copy
                               ).then_inc(sem("hT_ready"), 1)
            act.wait_ge(*upto("hT_ready", 4))
            act.wait_ge(*upto("c0", 7))
            act_norm(act, "n1", hT[:, :], KT, D)
            act.wait_ge(*upto("vT_done"))
            act.activation(vec[:, 0:NV], bank[4][:, 0:NV], ACT.Copy).then_inc(sem("vec_ready"), 1)
            act.activation(badaT[:, :], bank[4][:, P:P + 6 * KT], ACT.Copy
                           ).then_inc(sem("vec_ready"), 1)
            act.activation(pT[:, :], bank[5][:, :], ACT.Copy).then_inc(sem("pT_ready"), 1)
            act.wait_ge(*upto("lbd_ready"))
            act.activation(small[:, 4:8], small[:, 0:4], ACT.Sigmoid).then_inc(sem("lb_ready"), 1)
            act.activation(small[:, 8:12], small[:, 0:4], ACT.Sigmoid, scale=-1.0
                           ).then_inc(sem("lb_ready"), 1)
            act.wait_ge(*upto("vec_ready", 2))
            act.activation(small[:, 16:24], vec[:, VO["c_2"]:VO["c_2"] + KT], ACT.Sigmoid
                           ).then_inc(sem("csig_ready"), 1)
            out_dense(act, proj1, 0, projR)
            act.wait_ge(*upto("proj1_out0", IN1 // 512))
            act.wait_ge(*upto("proj1_out1", IN1 // 512))
            act.activation(T4[:, :], tile(projR, 4, 4), ACT.Sigmoid).then_inc(sem("hg_sig"), 1)
            act.activation(S4[:, :], tile(projR, 0, 4), ACT.Sigmoid).then_inc(sem("hg_sig"), 1)
            act.wait_ge(*upto("f_ready", 4))
            act.activation(tile(projR, 4, 4), tile(projR, 4, 4), ACT.Sigmoid, scale=-1.0
                           ).then_inc(sem("hg_sig"), 1)
            act.activation(G4[:, :], tile(projR, 12, 4), ACT.Sigmoid).then_inc(sem("hg_sig"), 1)
            act.activation(T4[:, :], T4[:, :], ACT.Ln).then_inc(sem("g_ready"), 1)
            for n, dst in enumerate((V4, SV4)):
                for t in range(TT):
                    act.wait_ge(*upto("vtok_done", n * TT + t + 1))
                    act.activation(dst[:, t * HW:(t + 1) * HW], bank[2 + t][:, :], ACT.Copy
                                   ).then_inc(sem("vtok_ready"), 1)
            for h in range(SB_HEADS):
                act.wait_ge(*upto("z_done", h + 1))
                act.activation(zb[:, h * 384:(h + 1) * 384], bank[h % 4][:, 0:384], ACT.Copy,
                               scale=SCALE_SB).then_inc(sem("z_out"), 1)
            act.wait_ge(*upto("z_out", SB_HEADS))
            act.activation(lb_, zb, ACT.Abs).then_inc(sem("sp"), 1)
            act.wait_ge(*upto("sp", 1))
            act.activation(lb_, lb_, ACT.Exp, scale=-1.0).then_inc(sem("sp"), 1)
            act.wait_ge(*upto("sp", 2))
            act.activation(lb_, lb_, ACT.Ln, bias=1.0).then_inc(sem("sp"), 1)
            for li in range(len(ALL_LEVELS)):
                act.wait_ge(*upto("d_ready", 2 * li + 2))
                act.activation(ed[li % 2], ed[li % 2], ACT.Exp).then_inc(sem("e_ready"), 1)
            for h in range(SB_HEADS):
                act.wait_ge(*upto("sx_ready", h + 1))
                act.activation(zb[:, h * 384:(h + 1) * 384], zb[:, h * 384:(h + 1) * 384], ACT.Exp
                               ).then_inc(sem("a_ready"), 1)
            for b in range(2):
                act.wait_ge(*upto("ohg_done", b + 1))
                act.activation(tile(mixin, 2 * b, 2), bank[b][:, :], ACT.Copy
                               ).then_inc(sem("ohg_out"), 1)
            act.wait_ge(*upto("ohg_out", 2))
            act_norm(act, "nhg", mixin[:, 0:HT * T], HT, HW)
            for b in range(2):
                act.wait_ge(*upto("osb_done", b + 1))
                act.activation(tile(mixin, HT + 2 * b, 2), bank[2 + b][:, :], ACT.Copy
                               ).then_inc(sem("osb_out"), 1)
            act.wait_ge(*upto("osb_out", 2))
            act_norm(act, "nsb", mixin[:, HT * T:2 * HT * T], HT, HW)
            out_dense(act, wout1, 0, mixT)
            act.wait_ge(*upto("wout1_out0", 2))
            act.wait_ge(*upto("wout1_out1", 2))
            act_norm(act, "npost", mixT, KT, D)
            act.wait_ge(*upto("h1_ready"))
            act_norm(act, "nffn", hT[:, :], KT, D)

            def silu(i, last):
                act.wait_ge(*upto("gate_done", i + 1))
                act.wait_ge(*upto("hid_ready", i))
                act.activation(S4[:, 0:512], bank[0][:, :], ACT.Silu).then_inc(sem("silu_ready"), 1)

            with act.Fori(0, NF) as i:
                silu(i, False)
            for b in range(4):
                act.wait_ge(*upto("y_done"))
                act.activation(tile(mixT, 2 * b, 2), bank[2 + b][:, :], ACT.Copy
                               ).then_inc(sem("y_out"), 1)
            act.wait_ge(*upto("y_out", 4))
            act_norm(act, "nfpost", mixT, KT, D)
            for b in range(4):
                act.wait_ge(*upto("pp_done", b + 1))
                act.activation(tile(xk, 2 * b, 2), bank[(0, 1, 4, 5)[b]][:, :], ACT.Copy
                               ).then_inc(sem("pp_out"), 1)
            with act.Fori(0, 2) as i:
                for j in range(2):
                    act.wait_ge(*upto(f"pgate_done{j}", i + 1))
                    act.activation(mixT[:, bass.ds(i * 1024 + j * 512, 512)], bank[2 + j][:, :],
                                   ACT.Sigmoid).then_inc(sem(f"pgate_out{j}"), 1)
            for b in range(ADA_B):
                act.wait_ge(*upto(f"ada_done{b}", KT))
            act.wait_ge(*upto("bd_zero", 2))
            for dst, w in ((wrb, "lru_wr_2"), (wib, "lru_wi_2")):
                wv = d[w][0].rearrange("(n two) i j -> two i n j", two=2)
                for r in range(2):
                    act.dma_start(dst[r * 64:(r + 1) * 64, :].rearrange("p (n j) -> p n j", j=P)
                                  [:, :, r * 64:(r + 1) * 64], wv[r]).then_inc(sem("sw_in"), 16)
            act.dma_start(wa2[:, :], d["gla_wa2_2"][0]).then_inc(sem("sw_in"), 16)
            act.dma_start(wlr[:, 0:KT * GATE_RANK].rearrange("p (k n) -> p k n", k=KT),
                          d["w_in_2"][0].rearrange("(k p) n -> p k n", p=P)[:, :, IN2_FULL:IN2]
                          ).then_inc(sem("sw_in"), 16)
            wv = wcf[:, 0:KT * NL].rearrange("p (k n) -> p k n", k=KT)
            act.dma_start(wv[:, :, 0:NG], d["w_coarse_2"][0].rearrange("(k p) n -> p k n", p=P)
                          ).then_inc(sem("sw_in"), 16)
            act.dma_start(wv[:, :, NG:NL], d["w_fine_2"][0].rearrange("(k p) n -> p k n", p=P)
                          ).then_inc(sem("sw_in"), 16)
            act.dma_start(bcf[:, 0:NG], d["b_coarse_2"]).then_inc(sem("sw_in"), 16)
            act.dma_start(bcf[:, NG:NL], d["b_fine_2"]).then_inc(sem("sw_in"), 16)

            act.wait_ge(*upto("vec_ready", 2))
            lam = vec[:, VO["lru_lambda_2"]:VO["lru_lambda_2"] + HT]
            act.activation(lru[:, 0:HT], lam, ACT.Abs).then_inc(sem("lam"), 1)
            act.wait_ge(*upto("lam", 1))
            act.activation(lru[:, 0:HT], lru[:, 0:HT], ACT.Exp, scale=-1.0).then_inc(sem("lam"), 1)
            act.wait_ge(*upto("lam", 2))
            act.activation(lru[:, 0:HT], lru[:, 0:HT], ACT.Ln, bias=1.0).then_inc(sem("lam"), 1)

            def shift(name, mod_tile):
                for k in range(KT):
                    act.wait_ge(*upto(f"{name}_out", k + 1))
                    act.activation(tile(uT, k), tile(uT, k), ACT.Identity,
                                   bias=modT[:, mod_tile + k:mod_tile + k + 1]
                                   ).then_inc(sem(f"{name}_shift"), 1)

            act.wait_ge(*upto("h3_ready"))
            act_norm(act, "nmix2", hT[:, :], KT, D)
            shift("nmix2", 0)
            out_dense(act, proj2, 0, projR)
            act.wait_ge(*upto("glr_done"))
            act.activation(glr[:, :], bank[4][0:GATE_RANK, 0:T], ACT.Copy).then_inc(sem("glr_out"), 1)
            act.wait_ge(*upto("proj2_out0", IN2_FULL // 512))
            act.wait_ge(*upto("proj2_out1", IN2_FULL // 512))
            for t in range(TT):
                act.wait_ge(*upto("gv_done", t + 1))
                act.activation(GV[:, t * HW:(t + 1) * HW], bank[5 + t][:, :], ACT.Copy
                               ).then_inc(sem("gv_out"), 1)
            act.wait_ge(*upto("ga_done"))
            for k in range(GLA_QT):
                act.activation(lsx[:, k * T:(k + 1) * T], bank[4][:, k * T:(k + 1) * T], ACT.Identity,
                               bias=v("gla_ba_2", k)).then_inc(sem("ga"), 1)
            act.wait_ge(*upto("ga", 2))
            act.activation(lsx[:, 512:1024], lsx[:, 0:512], ACT.Abs).then_inc(sem("ga"), 1)
            act.wait_ge(*upto("ga", 3))
            act.activation(lsx[:, 512:1024], lsx[:, 512:1024], ACT.Exp, scale=-1.0
                           ).then_inc(sem("ga"), 1)
            act.wait_ge(*upto("ga", 4))
            act.activation(lsx[:, 512:1024], lsx[:, 512:1024], ACT.Ln, bias=1.0
                           ).then_inc(sem("ga"), 1)
            IG = 1.0 / GATE_NORM
            act.wait_ge(*upto("b64_ready", 8))
            act.activation(e2[0], b64, ACT.Exp, scale=IG).then_inc(sem("ge_ready"), 1)
            act.activation(e2[1], b64, ACT.Exp, scale=-IG).then_inc(sem("ge_ready"), 1)
            for n in range(2):
                act.wait_ge(*upto("gd_ready", 2 * n + 2))
                act.activation(e2[n], e2[n], ACT.Exp, scale=IG).then_inc(sem("ge_ready"), 1)
            for n, (b0, dst, bias) in enumerate(((0, T4, "lru_br_2"), (2, G4, "lru_bi_2"))):
                act.wait_ge(*upto("lgate_done", n + 1))
                for k in range(HT):
                    act.activation(tile(dst, k), bank[b0 + k // 2][:, (k % 2) * T:(k % 2 + 1) * T],
                                   ACT.Sigmoid, bias=v(bias, k)).then_inc(sem("lgate_out"), 1)
            act.wait_ge(*upto("la_ready", HT))
            act.activation(A8, T4[:, :], ACT.Exp).then_inc(sem("lru_a"), 1)
            act.activation(th, T4[:, :], ACT.Tanh, scale=-1.0).then_inc(sem("lru_th"), 1)
            act.wait_ge(*upto("gelu_in"))
            act.activation(gel, gel, ACT.Tanh, scale=SQRT_2_OVER_PI).then_inc(sem("gelu_tanh"), 1)
            act.wait_ge(*upto("lru_m"))
            act.activation(th, th, ACT.Sqrt).then_inc(sem("lru_root"), 1)
            act.activation(tile(projR, 16, 4), tile(projR, 16, 4), ACT.Silu
                           ).then_inc(sem("gout_ready"), 1)
            for b in range(2):
                act.wait_ge(*upto("og_done", b + 1))
                if b == 0:
                    act.wait_ge(*upto("gi_ready"))
                act.activation(tile(XC, 2 * b, 2), bank[b][:, :], ACT.Copy).then_inc(sem("og_out"), 1)
            act.wait_ge(*upto("og_out", 2))
            act.activation(sq[:, 0:1024], XC, ACT.Square).then_inc(sem("og_sq"), 1)
            for b in range(2):
                act.wait_ge(*upto("og_ss", b + 1))
                act.activation(rms[:, b * 512:(b + 1) * 512], bank[2 + b][:, :], ACT.Sqrt,
                               bias=epsc[:, :], scale=1.0 / P).then_inc(sem("og_rms"), 1)
            out_dense(act, wout2, 0, mixT2)
            act.wait_ge(*upto("x2_ready", KT))
            act_norm(act, "nffn2", hT[:, :], KT, D)
            shift("nffn2", 3 * KT)
            act.wait_ge(*upto("cs_ready"))
            act.activation(rt[:, 0:TT * NG], rt[:, 0:TT * NG], ACT.Exp).then_inc(sem("ec_ready"), 1)
            for n, (dst, name) in enumerate(((h2tok, "h2tok"), (x2tok, "x2tok"))):
                for b in range(4):
                    act.wait_ge(*upto("tok_done", 4 * n + b + 1))
                    act.activation(dst[:, b * 512:(b + 1) * 512], bank[4 + b][:, :], ACT.Copy
                                   ).then_inc(sem(name), 1)
            act.wait_ge(*upto("dm_ready"))
            act.activation(rs[:, 8:8 + TT], rs[:, 8:8 + TT], ACT.Exp).then_inc(sem("e21_ready"), 1)
            for k in range(KT):
                act.wait_ge(*upto("xs_done", k + 1))
                act.activation(xsT[:, k, 0:SLOTS], bank[k % 4][:, :], ACT.Copy
                               ).then_inc(sem("xs_out"), 1)
            for b in range(2):
                act.wait_ge(*upto("pwt_done", b + 1))
                act.activation(PwT[:, 2 * b:2 * b + 2, :],
                               bank[4 + b][:, :].rearrange("p (c t) -> p c t", t=T), ACT.Copy
                               ).then_inc(sem("pwt_out"), 1)

            def window(par, name, count):
                act.wait_ge(*upto(f"{name}gu_done{par}", count))
                act.activation(sil, bank[par][0:2 * WIN, 0:256], ACT.Silu).then_inc(sem(f"{name}sil{par}"), 1)
                act.wait_ge(*upto(f"{name}ht_done{par}", count))
                act.activation(hidT.rearrange("p (c s) -> p c s", c=2),
                               bank[2 + par][:, 0:2 * P].rearrange("p (c s) -> p c s", c=2)
                               [:, :, 2 * WIN:P], ACT.Copy
                               ).then_inc(sem(f"{name}ht_out{par}"), 1)
                act.wait_ge(*upto(f"{name}y_done{par}", count))
                act.activation(yb, bank[4 + par][:, 0:256], ACT.Copy).then_inc(sem(f"{name}y_out{par}"), 1)

            with act.Fori(0, NE // 2) as i:
                for par in range(2):
                    count = act.value_load(tbl[0:1, bass.ds(i * 2 + (NE + par), 1)],
                                           min_val=0, max_val=T)
                    with act.If(count > 0):
                        window(par, "", i + 1)
                        with act.If(count > WIN):
                            window(par, "b", i * (NWIN - 1) + 1)
                            with act.If(count > 2 * WIN):
                                with act.Fori(2, NWIN) as w:
                                    with act.If(count > w * WIN):
                                        window(par, "b", i * (NWIN - 1) + w)
                                    with act.Else():
                                        for name in ("sil", "ht_out", "y_out"):
                                            act.drain().then_inc(sem(f"b{name}{par}"), 1)
                            with act.Else():
                                for name in ("sil", "ht_out", "y_out"):
                                    act.drain().then_inc(sem(f"b{name}{par}"), NWIN - 2)
                        with act.Else():
                            for name in ("sil", "ht_out", "y_out"):
                                act.drain().then_inc(sem(f"b{name}{par}"), NWIN - 1)
                    with act.Else():
                        for name in ("sil", "ht_out", "y_out"):
                            act.drain().then_inc(sem(f"{name}{par}"), 1)
                            act.drain().then_inc(sem(f"b{name}{par}"), NWIN - 1)
            for n in range(8):
                act.wait_ge(*upto("yt_done", n + 1))
                act.activation(ystok[:, n * 512:(n + 1) * 512], bank[n][:, :], ACT.Copy
                               ).then_inc(sem("yt_out"), 1)
            for t in range(TT):
                act.wait_ge(*upto("x3_ready", t * 2 + 2))
                act.activation(R24[:, t * D:(t + 1) * D], x2tok[:, t * D:(t + 1) * D], ACT.Square,
                               accum_out=rs[:, 20 + t:21 + t]).then_inc(sem("fin_ss"), 1)
                act.wait_ge(*upto("fin_ss", t + 1))
                act.activation(rs[:, 22 + t:23 + t], rs[:, 20 + t:21 + t], ACT.Sqrt, bias=epsc[:, :],
                               scale=1.0 / D).then_inc(sem("fin_rms"), 1)

        @block.tensor
        def _(pe):
            signal_free(pe, "pe")
            pe.wait_ge(*upto("ident_set"))
            pe.wait_ge(*upto("x_in", 16))
            for b in range(4):
                for k in range(2):
                    for t in range(TT):
                        mm = pe.transpose(bank[b][:, k * T + t * P:k * T + (t + 1) * P],
                                          x_tok[:, t * D + (2 * b + k) * P:t * D + (2 * b + k + 1) * P],
                                          ident[:, :])
                mm.then_inc(sem("xT_done"), 1)
            pe.wait_ge(*upto("ones_set"))
            pe_norm(pe, "n1", KT)
            pe.wait_ge(*upto("v_in", 16 * (len(VROWS) + 2)))
            pe.transpose(bank[4][:, 0:NV], vrow[0:NV, :], ident[0:NV, 0:NV])
            pe.transpose(bank[4][:, P:P + 6 * KT], brow[0:6 * KT, :], ident[0:6 * KT, 0:6 * KT])
            for k in range(PLE // P):
                for t in range(TT):
                    mm = pe.transpose(bank[5][:, k * T + t * P:k * T + (t + 1) * P],
                                      p_tok[:, t * PLE + k * P:t * PLE + (k + 1) * P], ident[:, :])
            mm.then_inc(sem("vT_done"), 1)

            def ada(k, b, c, first, last):
                pe.wait_ge(*upto(f"ada_full{b}", k * 16 + 16))
                for j in range(4):
                    mm = pe.matmul(bank[4 + b][32 * j:32 * j + 32, :],
                                   c, slot[ADA_SLOT + b][:, j * 512:(j + 1) * 512],
                                   start=first, stop=last, skip_group_check=True)
                mm.then_inc(sem(f"ada_done{b}"), 1)

            pe.wait_ge(*upto("crep_ready", KT))
            pe.wait_ge(*upto("pT_ready"))
            for b in range(ADA_B):
                ada(0, b, crep[:, 0:32], True, False)
            pe.wait_ge(*upto("n1_out", KT))
            pe.wait_ge(*upto("hT_ready", 4))

            def proj1_round(i, last):
                for j in range(2):
                    pe.wait_ge(*upto(f"proj1_full{j}", i * 16 + 16))
                    pe.wait_ge(*upto(f"proj1_out{j}", i))
                    pe_chunk(pe, bank[j], slot[j], uT, f"proj1_done{j}")
                    for b in ADA_AFTER[j]:
                        if b == 0:
                            pe.wait_ge(*upto("cnow_ready", i + 1))
                        ada(i + 1, b, cnow, False, last)

            with pe.Fori(0, IN1 // 512 - 1) as i:
                proj1_round(i, False)
            proj1_round(IN1 // 512 - 1, True)
            pe.wait_ge(*upto("proj1_out0", IN1 // 512))
            pe.wait_ge(*upto("proj1_out1", IN1 // 512))
            for n, first in enumerate((8, 24)):
                for t in range(TT):
                    if n:
                        pe.wait_ge(*upto("vtok_ready", t + 1))
                    for c in range(4):
                        mm = pe.transpose(bank[2 + t][:, c * P:(c + 1) * P],
                                          half(projR, first + c, t), ident[:, :])
                    mm.then_inc(sem("vtok_done"), 1)
            pe.wait_ge(*upto("vtok_ready", 2 * TT))
            for h in range(SB_HEADS):
                if h >= 4:
                    pe.wait_ge(*upto("z_out", h - 3))
                r = slice((h % 2) * 64, (h % 2) * 64 + 64)
                q, k = tile(projR, 16 + h // 2)[r, :], tile(projR, 20 + h // 2)[r, :]
                pe.matmul(bank[h % 4][:, 0:256], k[:, 0:P], q[:, 0:T], start=True, stop=True)
                pe.matmul(bank[h % 4][:, 256:384], k[:, P:T], q[:, P:T], start=True, stop=True
                          ).then_inc(sem("z_done"), 1)
            pe.wait_ge(*upto("z_out", SB_HEADS))
            for li, L in enumerate(ALL_LEVELS):
                pe.wait_ge(*upto("qk_ready", 2 * li + 2))
                if li >= 2:
                    pe.wait_ge(*upto("lv_out", 2 * (li - 1)))
                for h in range(HG_HEADS):
                    b = bank[2 * (li % 2) + h // 2]
                    for t in range(TT):
                        if L == P and t:
                            continue
                        kt, qt = (0, 1) if L == P else (t, t)
                        mm = pe.matmul(b[:, (h % 2) * T + t * P:(h % 2) * T + (t + 1) * P],
                                       kd[li % 2][:, h * T + kt * P:h * T + (kt + 1) * P],
                                       qd[li % 2][:, h * T + qt * P:h * T + (qt + 1) * P],
                                       start=True, stop=True)
                mm.then_inc(sem("lv_done"), 1)
            pe.wait_ge(*upto("k_ready", 4))
            pe.wait_ge(*upto("q_ready"))
            pe.wait_ge(*upto("lv_out", 2 * (len(ALL_LEVELS) - 1)))
            for h in range(HG_HEADS):
                for t in range(TT):
                    mm = pe.matmul(bank[h // 2][:, (h % 2) * T + t * P:(h % 2) * T + (t + 1) * P],
                                   half(projR, 4 + h, t), half(projR, h, t), start=True, stop=True)
            mm.then_inc(sem("lv_done"), 1)
            for b in range(ADA_B):
                pe.wait_ge(*upto("ada_row", b + 1))
                for c in range(4):
                    mm = pe.transpose(bank[4 + b][:, c * P:(c + 1) * P],
                                      mod_row(b)[:, c * P:(c + 1) * P], ident[:, :])
                mm.then_inc(sem("mod_done"), 1)
            pe.wait_ge(*upto("const", 6))
            pe.wait_ge(*upto("mod_ready", ADA_B))
            for h in range(SB_HEADS):
                pe.wait_ge(*upto("lm_ready", h + 1))
                if h >= 2:
                    pe.wait_ge(*upto("sx_ready", h - 1))
                b = bank[4 + h % 2]
                lm = lb_[:, h * 384:(h + 1) * 384]
                pe.matmul(b[:, 0:P], tri_ge[:, :], lm[:, 0:P], start=True, stop=True)
                pe.matmul(b[:, P:T], ones[:, 0:P], lm[:, T:T + P], start=True, stop=False)
                pe.matmul(b[:, P:T], tri_ge[:, :], lm[:, P:T], start=False, stop=True)
                pe.matmul(b[:, T:T + P], tri_ge[:, :], lm[:, T:T + P], start=True, stop=True
                          ).then_inc(sem("sx_done"), 1)
            pe.wait_ge(*upto("lv_out", 2 * (len(ALL_LEVELS) + 1)))
            pe.wait_ge(*upto("vtok_ready", 2 * TT))
            for h in range(HG_HEADS):
                o = bank[h // 2][:, (h % 2) * T:(h % 2 + 1) * T]
                v0, v1 = (V4[:, t * HW + h * P:t * HW + (h + 1) * P] for t in range(TT))
                pe.matmul(o[:, 0:P], v0, half(S4, h, 0), start=True, stop=True)
                pe.matmul(o[:, P:T], v0, SX2[:, h * P:(h + 1) * P], start=True, stop=False)
                mm = pe.matmul(o[:, P:T], v1, half(S4, h, 1), start=False, stop=True)
                if h % 2:
                    mm.then_inc(sem("ohg_done"), 1)
            for h in range(SB_HEADS):
                pe.wait_ge(*upto("a_ready", h + 1))
                a = zb[:, h * 384:(h + 1) * 384]
                r = (h % 2) * 64
                o = bank[2 + h // 4][r:r + 64, (h // 2 % 2) * T:(h // 2 % 2 + 1) * T]
                v0, v1 = (SV4[:, t * HW + h * 64:t * HW + (h + 1) * 64] for t in range(TT))
                pe.matmul(o[:, 0:P], v0, a[:, 0:P], start=True, stop=True)
                pe.matmul(o[:, P:T], v0, a[:, P:T], start=True, stop=False)
                mm = pe.matmul(o[:, P:T], v1, a[:, T:T + P], start=False, stop=True)
                if h % 4 == 3:
                    mm.then_inc(sem("osb_done"), 1)
            pe_norm(pe, "nhg", HT)
            pe_norm(pe, "nsb", HT)
            pe.wait_ge(*upto("ohg_ready"))
            pe.wait_ge(*upto("nsb_out", HT))
            pe_dense(pe, wout1, mixin)
            pe_norm(pe, "npost", KT)
            pe_norm(pe, "nffn", KT)
            pe.wait_ge(*upto("nffn_out", KT))

            def gate_up(i):
                pe.wait_ge(*upto("gate_full", i * 16 + 16))
                pe.wait_ge(*upto("silu_ready", i))
                pe_chunk(pe, bank[0], slot[0], uT, "gate_done")
                pe.wait_ge(*upto("up_full", i * 16 + 16))
                pe.wait_ge(*upto("hid_ready", i))
                pe_chunk(pe, bank[1], slot[1], uT, "up_done")

            def down(i, first, last):
                pe.wait_ge(*upto("down_full", i * 16 + 16))
                pe.wait_ge(*upto("hid_ready", i + 1))
                for k in range(2):
                    for m in range(KT):
                        mm = pe.matmul(bank[2 + m // 2][:, (m % 2) * T:(m % 2 + 1) * T],
                                       slot[4][:, k * D + m * P:k * D + (m + 1) * P],
                                       S4[:, 512 + k * T:512 + (k + 1) * T],
                                       start=(first and k == 0 and m % 2 == 0),
                                       stop=(last and k == 1), skip_group_check=True)
                mm.then_inc(sem("down_done"), 1)

            pe.wait_ge(*upto("wout1_out0", 2))
            pe.wait_ge(*upto("wout1_out1", 2))
            gate_up(0)
            down(0, True, False)
            with pe.Fori(1, NF - 1) as i:
                gate_up(i)
                down(i, False, False)
            gate_up(NF - 1)
            down(NF - 1, False, True)
            pe.drain().then_inc(sem("y_done"), 1)
            pe_norm(pe, "nfpost", KT)
            pe.wait_ge(*upto("pproj_full", 16))
            pe.wait_ge(*upto("pT_ready"))
            pe.wait_ge(*upto("hid_ready", NF))
            for b in range(4):
                for m in range(2):
                    for k in range(PLE // P):
                        mm = pe.matmul(bank[(0, 1, 4, 5)[b]][:, m * T:(m + 1) * T],
                                       slot[5][:, k * D + (2 * b + m) * P:k * D + (2 * b + m + 1) * P],
                                       tile(pT, k), start=(k == 0), stop=(k == PLE // P - 1))
                mm.then_inc(sem("pp_done"), 1)
            pe.wait_ge(*upto("h2_ready"))
            pe_dense(pe, pgate, hT)

            pe_norm(pe, "nmix2", KT)
            pe.wait_ge(*upto("nmix2_shift", KT))
            pe.wait_ge(*upto("pp_out", 4))
            pe_dense(pe, proj2, uT)
            pe.wait_ge(*upto("sw_in", 16 * 10))
            for k in range(KT):
                mm = pe.matmul(bank[4][0:GATE_RANK, 0:T], wlr[:, k * GATE_RANK:(k + 1) * GATE_RANK],
                               tile(uT, k), start=(k == 0), stop=(k == KT - 1))
            mm.then_inc(sem("glr_done"), 1)
            pe.wait_ge(*upto("proj2_out0", IN2_FULL // 512))
            pe.wait_ge(*upto("proj2_out1", IN2_FULL // 512))
            for t in range(TT):
                for c in range(4):
                    mm = pe.transpose(bank[5 + t][:, c * P:(c + 1) * P], half(projR, 12 + c, t),
                                      ident[:, :])
                mm.then_inc(sem("gv_done"), 1)
            pe.wait_ge(*upto("glr_out"))
            for k in range(GLA_QT):
                mm = pe.matmul(bank[4][:, k * T:(k + 1) * T], wa2[:, k * P:(k + 1) * P], glr[:, :],
                               start=True, stop=True)
            mm.then_inc(sem("ga_done"), 1)
            pe.wait_ge(*upto("conv", 4 * HT))
            for b0, w in ((0, wrb), (2, wib)):
                for k in range(HT):
                    mm = pe.matmul(bank[b0 + k // 2][:, (k % 2) * T:(k % 2 + 1) * T],
                                   w[:, k * P:(k + 1) * P], tile(XC, k), start=True, stop=True)
                mm.then_inc(sem("lgate_done"), 1)
            for n, L in enumerate((0, 64, P)):
                pe.wait_ge(*upto("gqk_ready", 2 * n + 2))
                if n >= 1:
                    pe.wait_ge(*upto("gl_out", 2 * n))
                for h in range(GLA_HEADS):
                    r = slice((h % 2) * 64, (h % 2) * 64 + 64)
                    for t in range(TT):
                        if L == P and t:
                            continue
                        kt, qt = (0, 1) if L == P else (t, t)
                        at = (h // 2) * T
                        mm = pe.matmul(bank[6 + h % 2][:, at + t * P:at + (t + 1) * P],
                                       k2[n % 2][r, at + kt * P:at + (kt + 1) * P],
                                       q2[n % 2][r, at + qt * P:at + (qt + 1) * P],
                                       start=True, stop=True)
                    if h >= GLA_HEADS - 2:
                        mm.then_inc(sem("gl_done"), 1)
            pe.wait_ge(*upto("gl_out", 6))
            pe.wait_ge(*upto("gv_out", TT))
            pe.wait_ge(*upto("lgate_out", 2 * HT))
            for h in range(GLA_HEADS):
                o = bank[h // 2][:, (h % 2) * T:(h % 2 + 1) * T]
                v0, v1 = (GV[:, t * HW + h * P:t * HW + (h + 1) * P] for t in range(TT))
                at = (h % 2) * 512 + (h // 2) * T
                pe.matmul(o[:, 0:P], v0, S4[:, at:at + P], start=True, stop=True)
                xat = (h % 2) * T + (h // 2) * P
                pe.matmul(o[:, P:T], v0, SX2[:, xat:xat + P], start=True, stop=False)
                mm = pe.matmul(o[:, P:T], v1, S4[:, at + P:at + T], start=False, stop=True)
                if h % 2:
                    mm.then_inc(sem("og_done"), 1)
            pe.wait_ge(*upto("og_sq"))
            for h in range(GLA_HEADS):
                mm = pe.matmul(bank[2 + h // 2][:, (h % 2) * T:(h % 2 + 1) * T], ones[:, 0:P],
                               tile(sq, h), start=True, stop=True)
                if h % 2:
                    mm.then_inc(sem("og_ss"), 1)
            pe.wait_ge(*upto("mix2_ready", 2))
            pe.wait_ge(*upto("og_rms", 2))
            pe_dense(pe, wout2, mixin)
            pe_norm(pe, "nffn2", KT)
            pe.wait_ge(*upto("nffn2_shift", KT))
            for t in range(TT):
                for k in range(KT):
                    pe.matmul(bank[0][:, t * 64:t * 64 + NL], half(uT, k, t),
                              wcf[:, k * NL:(k + 1) * NL], start=(k == 0), stop=False)
                pe.matmul(bank[0][:, t * 64:t * 64 + NL], ones[0:1, 0:P], bcf[:, :],
                          start=False, stop=True).then_inc(sem("lg_done"), 1)
            for n, (src, name) in enumerate(((uT, "h2tok"), (hT, "x2tok"))):
                for b in range(4):
                    if n:
                        pe.wait_ge(*upto("h2tok", b + 1))
                    for c in range(4):
                        mm = pe.transpose(bank[4 + b][:, c * P:(c + 1) * P],
                                          half(src, (b % 2) * 4 + c, b // 2), ident[:, :])
                    mm.then_inc(sem("tok_done"), 1)
            pe.wait_ge(*upto("a_set"))
            A0, A1 = rt[:, TA:TA + NE], rt[:, TA + NE:TA + 2 * NE]
            pe.matmul(bank[1][:, 0:NE], tri_lt[:, :], A0, start=True, stop=True)
            pe.matmul(bank[1][:, NE:2 * NE], ones[:, 0:P], A0, start=True, stop=False)
            pe.matmul(bank[1][:, NE:2 * NE], tri_lt[:, :], A1, start=False, stop=True)
            pe.matmul(bank[1][:, 2 * NE:3 * NE], ones[:, 0:P], A0, start=True, stop=False)
            pe.matmul(bank[1][:, 2 * NE:3 * NE], ones[:, 0:P], A1, start=False, stop=True
                      ).then_inc(sem("rank_done"), 1)
            pe.wait_ge(*upto("psel_ready", TT))
            pe.wait_ge(*upto("h2tok", 4))
            for k in range(KT):
                if k >= 4:
                    pe.wait_ge(*upto("xs_out", k - 3))
                for t in range(TT):
                    mm = pe.matmul(bank[k % 4][:, :], h2tok[:, t * D + k * P:t * D + (k + 1) * P],
                                   Psel[:, t, :], start=(t == 0), stop=(t == TT - 1))
                mm.then_inc(sem("xs_done"), 1)
            pe.wait_ge(*upto("pw_ready", TT))
            pe.wait_ge(*upto("x2tok", 4))
            for c in range(SLOTS // P):
                for t in range(TT):
                    mm = pe.transpose(bank[4 + c // 2][:, (c % 2) * T + t * P:(c % 2) * T + (t + 1) * P],
                                      Pw[:, t, c * P:(c + 1) * P], ident[:, :])
                if c % 2:
                    mm.then_inc(sem("pwt_done"), 1)
            pe.drain().then_inc(sem("pw_done"), 1)
            pe.wait_ge(*upto("xs_out", KT))
            pe.wait_ge(*upto("pwt_out", 2))

            def release(name, left):
                if left is None:
                    pe.drain().then_inc(sem(name), 1)
                else:
                    with pe.If(left <= WIN):
                        pe.drain().then_inc(sem(name), 1)

            def window(par, name, count, left=None):
                pe.wait_ge(*upto(f"{name}xw{par}", count))
                W = Wx[par]
                for first, full, g0 in ((WG, "wg", 0), (WU, "wu", 2)):
                    if not name:
                        pe.wait_ge(*upto(f"{full}_full{par}", count * 16))
                    for k in range(KT):
                        for h in range(2):
                            g = g0 + h
                            mm = pe.matmul(bank[par][g * WIN:(g + 1) * WIN, 0:256],
                                           xw[par][:, k * WIN:(k + 1) * WIN],
                                           W[:, first + k * DE + h * 256:first + k * DE + h * 256 + 256],
                                           start=(k == 0), stop=(k == KT - 1))
                mm.then_inc(sem(f"{name}gu_done{par}"), 1)
                release(f"gu_free{par}", left)
                pe.wait_ge(*upto(f"{name}hid{par}", count))
                for c in range(2):
                    mm = pe.transpose(bank[2 + par][:, c * P:(c + 1) * P],
                                      hidw[:, c * P:(c + 1) * P], ident[:, :])
                mm.then_inc(sem(f"{name}ht_done{par}"), 1)
                pe.wait_ge(*upto(f"{name}ht_out{par}", count))
                if not name:
                    pe.wait_ge(*upto(f"wd_full{par}", count * 16))
                for f in range(DE // P):
                    at = (f % 2) * 2 * WIN + (f // 2) * WIN
                    for g in range(4):
                        mm = pe.matmul(bank[4 + par][g * WIN:(g + 1) * WIN, 0:256],
                                       hidT[:, at:at + WIN],
                                       W[:, WD + f * D + g * 256:WD + f * D + (g + 1) * 256],
                                       start=(f == 0), stop=(f == DE // P - 1))
                mm.then_inc(sem(f"{name}y_done{par}"), 1)
                release(f"d_free{par}", left)
                pe.wait_ge(*upto(f"{name}y_out{par}", count))
                for c in range(2):
                    mm = pe.transpose(bank[6 + par][:, c * P:(c + 1) * P], yb[:, c * P:(c + 1) * P],
                                      ident[:, :])
                mm.then_inc(sem(f"{name}yt{par}"), 1)

            pe.wait_ge(*upto("hidw_zero"))
            for par in range(2):
                for name in ("wg_full", "wu_full", "wd_full"):
                    pe.wait_ge(*upto(f"{name}{par}", 16))
            with pe.Fori(0, NE // 2) as i:
                for par in range(2):
                    count = pe.value_load(tbl[0:1, bass.ds(i * 2 + (NE + par), 1)],
                                          min_val=0, max_val=T)
                    pe.wait_ge(*upto(f"yt_out{par}", i))
                    pe.wait_ge(*upto(f"byt_out{par}", i * (NWIN - 1)))
                    with pe.If(count > WIN):
                        window(par, "", i + 1, count)
                        pe.wait_ge(*upto(f"yt_out{par}", i + 1))
                        window(par, "b", i * (NWIN - 1) + 1, count - WIN)
                        with pe.If(count > 2 * WIN):
                            with pe.Fori(2, NWIN) as w:
                                with pe.If(count > w * WIN):
                                    pe.wait_ge(*upto(f"byt_out{par}", i * (NWIN - 1) + w - 1))
                                    window(par, "b", i * (NWIN - 1) + w, count - w * WIN)
                                with pe.Else():
                                    for name in ("gu_done", "ht_done", "y_done", "yt"):
                                        pe.drain().then_inc(sem(f"b{name}{par}"), 1)
                        with pe.Else():
                            for name in ("gu_done", "ht_done", "y_done", "yt"):
                                pe.drain().then_inc(sem(f"b{name}{par}"), NWIN - 2)
                    with pe.Else():
                        with pe.If(count > 0):
                            window(par, "", i + 1)
                        with pe.Else():
                            for name in ("gu_done", "ht_done", "y_done", "yt", "gu_free",
                                         "d_free"):
                                pe.drain().then_inc(sem(f"{name}{par}"), 1)
                        for name in ("gu_done", "ht_done", "y_done", "yt"):
                            pe.drain().then_inc(sem(f"b{name}{par}"), NWIN - 1)
            for par in range(2):
                pe.wait_ge(*upto(f"yt_out{par}", NE // 2))
                pe.wait_ge(*upto(f"byt_out{par}", NE // 2 * (NWIN - 1)))
            for c in range(SLOTS // P):
                for b in range(2):
                    for k in range(4):
                        mm = pe.transpose(bank[2 * c + b][:, k * P:(k + 1) * P],
                                          ysT[:, 4 * b + k, c * P:(c + 1) * P], ident[:, :])
                    mm.then_inc(sem("yt_done"), 1)
            pe.wait_ge(*upto("yt_out", 8))
            for t in range(TT):
                for b in range(2):
                    for c in range(SLOTS // P):
                        mm = pe.matmul(bank[2 * t + b][:, :], PwT[:, c, t * P:(t + 1) * P],
                                       ystok[:, c * D + b * 512:c * D + (b + 1) * 512],
                                       start=(c == 0), stop=(c == SLOTS // P - 1))
                    mm.then_inc(sem("comb_done"), 1)

        @block.vector
        def _(dve):
            signal_free(dve, "dve")
            dve.wait_ge(*upto("vec_ready", 2))
            g = VO["hg_lower_gamma"]
            dve.tensor_tensor(small[:, 0:4], vec[:, g:g + HT], vec[:, g + HT:g + 2 * HT],
                              ALU.subtract).then_inc(sem("lbd_ready"), 1)
            dve_norm(dve, "n1", hT, lambda k: v("attn_pre_norm", k), uT, KT)
            dve.wait_ge(*upto("csig_ready"))
            dve.tensor_tensor(csil[:, :], small[:, 16:24], vec[:, VO["c_2"]:VO["c_2"] + KT], ALU.mult
                              ).then_inc(sem("csil_ready"), 1)
            dve.wait_ge(*upto("csil_ready"))
            dve.wait_ge(*upto("ones_set"))
            for k in range(KT):
                dve.tensor_scalar(crep[:, k * 32:(k + 1) * 32], ones[:, 0:32], csil[:, k:k + 1], None,
                                  ALU.mult).then_inc(sem("crep_ready"), 1)
            out_dense(dve, proj1, 1, projR)
            dve.wait_ge(*upto("lb_ready", 2))
            dve.wait_ge(*upto("hg_sig", 1))
            for h in range(HT):
                dve.tensor_scalar(tile(T4, h), tile(T4, h), small[:, 8 + h:9 + h],
                                  small[:, 4 + h:5 + h], ALU.mult, ALU.add
                                  ).then_inc(sem("f_ready"), 1)
            dve.wait_ge(*upto("hg_sig", 2))
            dve.wait_ge(*upto("proj1_out0", IN1 // 512))
            dve.tensor_tensor(tile(projR, 0, 4), tile(projR, 0, 4), S4[:, :], ALU.mult
                              ).then_inc(sem("q_ready"), 1)
            dve.wait_ge(*upto("hg_sig", 4))
            for h in range(HT):
                dve.tensor_scalar(tile(projR, 4 + h), tile(projR, 4 + h), small[:, 8 + h:9 + h], None,
                                  ALU.mult).then_inc(sem("k_ready"), 1)
            dve.tensor_tensor(tile(projR, 12, 4), tile(projR, 12, 4), G4[:, :], ALU.mult
                              ).then_inc(sem("hgate_ready"), 1)
            dve.wait_ge(*upto("g_ready"))
            dve.wait_ge(*upto("hgate_ready"))
            for h in range(HT):
                dve.tensor_tensor_scan(tile(G4, h), ones[:, 0:T], tile(T4, h), 0.0, ALU.mult, ALU.add
                                       ).then_inc(sem("b_ready"), 1)
            dve.wait_ge(*upto("b_ready", HT))
            dve.wait_ge(*upto("q_ready"))
            dve.wait_ge(*upto("k_ready", HT))
            dve.wait_ge(*upto("proj1_done0", IN1 // 512))
            dve.wait_ge(*upto("proj1_done1", IN1 // 512))
            for n, z in enumerate((qd[0], qd[1], kd[0], kd[1])):
                dve.memset(z, 0.0).then_inc(sem("lv_zero"), 1)
            dve.memset(S4[:, :], 0.0).then_inc(sem("lv_zero"), 1)
            dve.wait_ge(*upto("lv_zero", 5))
            dve.wait_ge(*upto("c1", NC1))

            def diffs(li):
                L = ALL_LEVELS[li]
                if li >= 2:
                    dve.wait_ge(*upto("qk_ready", 2 * (li - 1)))
                bv, ev = blocks(hb, L), blocks(ed[li % 2], L)
                ref = bv[:, :, L - 1:L].to_broadcast([P, 1024 // (2 * L), L])
                dve.tensor_tensor(ev[:, :, 0:L], ref, bv[:, :, 0:L], ALU.subtract
                                  ).then_inc(sem("d_ready"), 1)
                dve.tensor_tensor(ev[:, :, L:2 * L], bv[:, :, L:2 * L], ref, ALU.subtract
                                  ).then_inc(sem("d_ready"), 1)

            def products(li):
                L = ALL_LEVELS[li]
                dve.wait_ge(*upto("e_ready", li + 1))
                if li >= 2:
                    dve.wait_ge(*upto("lv_done", li - 1))
                ev = blocks(ed[li % 2], L)
                dve.tensor_tensor(blocks(kd[li % 2], L)[:, :, 0:L],
                                  blocks(tile(projR, 4, 4), L)[:, :, 0:L], ev[:, :, 0:L], ALU.mult
                                  ).then_inc(sem("qk_ready"), 1)
                dve.tensor_tensor(blocks(qd[li % 2], L)[:, :, L:2 * L],
                                  blocks(tile(projR, 0, 4), L)[:, :, L:2 * L], ev[:, :, L:2 * L],
                                  ALU.mult).then_inc(sem("qk_ready"), 1)

            def collect(li, mask):
                dve.wait_ge(*upto("lv_done", li + 1))
                if li:
                    dve.wait_ge(*upto("lv_out", 2 * li))
                m = lmask[:, mask, :].bitcast(U32).unsqueeze(1).to_broadcast([P, 4, P])
                for b in range(2):
                    dve.copy_predicated(
                        S4[:, b * 512:(b + 1) * 512].rearrange("p (n t) -> p n t", t=P), m,
                        bank[(2 * (li % 2) if li < len(ALL_LEVELS) else 0) + b][:, :].rearrange(
                            "p (n t) -> p n t", t=P)).then_inc(sem("lv_out"), 1)

            diffs(0)
            for li in range(len(ALL_LEVELS)):
                if li + 1 < len(ALL_LEVELS):
                    diffs(li + 1)
                products(li)
                if li:
                    collect(li - 1, li - 1)
            li = len(ALL_LEVELS) - 1
            dve.wait_ge(*upto("lv_done", li + 1))
            for b in range(2):
                dve.tensor_copy(
                    SX2[:, b * 256:(b + 1) * 256].rearrange("p (h t) -> p h t", t=P),
                    bank[2 * (li % 2) + b][:, :].rearrange("p (h t) -> p h t", t=T)[:, :, 0:P]
                ).then_inc(sem("lv_out"), 1)
            collect(li + 1, DIAG)
            for b in range(ADA_B):
                dve.wait_ge(*upto(f"ada_done{b}", KT))
                dve.tensor_copy(mod_row(b), bank[4 + b][:, :]).then_inc(sem("ada_row"), 1)
            for b in range(ADA_B):
                dve.wait_ge(*upto("mod_done", b + 1))
                dve.tensor_tensor(
                    modT[:, b * 16:(b + 1) * 16].rearrange("p (j c) -> p j c", c=4),
                    bank[4 + b][:, :].rearrange("p (c j r) -> p j c r", c=4, r=32)[:, :, :, 0],
                    badaT[:, b * 16:(b + 1) * 16].rearrange("p (j c) -> p j c", c=4), ALU.add
                ).then_inc(sem("mod_ready"), 1)
            dve.wait_ge(*upto("sp", 3))
            for h in range(SB_HEADS):
                c = slice(h * 384, (h + 1) * 384)
                dve.scalar_tensor_tensor(out=lb_[:, c], in0=zb[:, c], scalar=0.0, in1=lb_[:, c],
                                         op0=ALU.max, op1=ALU.add).then_inc(sem("sp_full"), 1)
            for h in range(SB_HEADS):
                c = slice(h * 384, (h + 1) * 384)
                dve.wait_ge(*upto("sp_full", h + 1))
                dve.wait_ge(*upto("const", 6))
                dve.tensor_tensor(lb_[:, c], lb_[:, c], negm[:, :], ALU.mult
                                  ).then_inc(sem("lm_ready"), 1)
            for h in range(SB_HEADS):
                c = slice(h * 384, (h + 1) * 384)
                dve.wait_ge(*upto("sx_done", h + 1))
                dve.wait_ge(*upto("zm_ready", h + 1))
                dve.tensor_tensor(zb[:, c], bank[4 + h % 2][:, 0:384], eb[:, c], ALU.add
                                  ).then_inc(sem("sx_ready"), 1)
            dve_norm(dve, "nhg", mixin, lambda k: v("hg_out_norm", k), mixin, HT)
            dve.wait_ge(*upto("nhg_out", HT))
            dve.tensor_tensor(mixin[:, 0:HT * T], mixin[:, 0:HT * T], tile(projR, 12, 4), ALU.mult
                              ).then_inc(sem("ohg_ready"), 1)
            o_sb = mixin[:, HT * T:2 * HT * T]
            dve_norm(dve, "nsb", o_sb, lambda k: v("sb_out_norm", k), o_sb, HT)
            out_dense(dve, wout1, 1, mixT)
            dve_norm(dve, "npost", mixT, lambda k: v("attn_post_norm", k), mixT, KT)
            dve.wait_ge(*upto("npost_out", KT))
            dve.tensor_tensor(hT[:, :], hT[:, :], mixT, ALU.add).then_inc(sem("h1_ready"), 1)
            dve_norm(dve, "nffn", hT, lambda k: v("ffn_pre_norm", k), uT, KT)
            with dve.Fori(0, NF) as i:
                dve.wait_ge(*upto("silu_ready", i + 1))
                dve.wait_ge(*upto("up_done", i + 1))
                dve.wait_ge(*upto("down_done", i))
                dve.tensor_tensor(S4[:, 512:1024], S4[:, 0:512], bank[1][:, :], ALU.mult
                                  ).then_inc(sem("hid_ready"), 1)
            dve_norm(dve, "nfpost", mixT, lambda k: v("ffn_post_norm", k), mixT, KT)
            dve.wait_ge(*upto("nfpost_out", KT))
            dve.tensor_tensor(hT[:, :], hT[:, :], mixT, ALU.add).then_inc(sem("h2_ready"), 1)
            dve.wait_ge(*upto("pp_out", 4))
            dve.wait_ge(*upto("pgate_out0", 2))
            dve.wait_ge(*upto("pgate_out1", 2))
            dve.tensor_tensor(mixT, mixT, xk, ALU.mult).then_inc(sem("ple_ready"), 1)
            dve.wait_ge(*upto("ple_ready"))
            dve.tensor_tensor(hT[:, :], hT[:, :], mixT, ALU.add).then_inc(sem("h3_ready"), 1)


            dve.wait_ge(*upto("mod_ready", ADA_B))
            for n, (name, sc) in enumerate((("g_mix_2", KT), ("g_ffn_2", 4 * KT))):
                dve.scalar_tensor_tensor(out=gs[:, n * KT:(n + 1) * KT], in0=modT[:, sc:sc + KT],
                                         scalar=1.0, in1=vec[:, VO[name]:VO[name] + KT],
                                         op0=ALU.add, op1=ALU.mult).then_inc(sem("gs_ready"), 1)
            dve.wait_ge(*upto("lam", 3))
            lam = vec[:, VO["lru_lambda_2"]:VO["lru_lambda_2"] + HT]
            dve.tensor_scalar(lru[:, HT:2 * HT], lam, 0.0, None, ALU.min).then_inc(sem("lam_v"), 1)
            dve.wait_ge(*upto("lam_v", 1))
            dve.tensor_tensor(lru[:, HT:2 * HT], lru[:, HT:2 * HT], lru[:, 0:HT], ALU.subtract
                              ).then_inc(sem("lam_v"), 1)
            dve.wait_ge(*upto("lam_v", 2))
            dve.tensor_scalar(lru[:, 2 * HT:3 * HT], lru[:, HT:2 * HT], LRU_C, None, ALU.mult
                              ).then_inc(sem("lam_v"), 1)
            dve.wait_ge(*upto("gs_ready", 2))
            dve_norm(dve, "nmix2", hT, lambda k: gs[:, k:k + 1], uT, KT)
            out_dense(dve, proj2, 1, projR)
            dve.wait_ge(*upto("proj2_out0", IN2_FULL // 512))
            dve.wait_ge(*upto("proj2_out1", IN2_FULL // 512))
            for k in range(HT):
                dve.tensor_scalar(tile(XC, k), tile(projR, k), v("conv_w_2", 3 * HT + k),
                                  v("conv_b_2", k), ALU.mult, ALU.add).then_inc(sem("conv"), 1)
            for sh in range(1, 4):
                for k in range(HT):
                    dve.wait_ge(*upto("conv", HT * (sh - 1) + k + 1))
                    dve.scalar_tensor_tensor(
                        out=tile(XC, k)[:, sh:T], in0=tile(projR, k)[:, 0:T - sh],
                        scalar=v("conv_w_2", (3 - sh) * HT + k), in1=tile(XC, k)[:, sh:T],
                        op0=ALU.mult, op1=ALU.add).then_inc(sem("conv"), 1)
            dve.wait_ge(*upto("ga", 5))
            ls = lsx[:, 0:512]
            dve.scalar_tensor_tensor(out=ls, in0=ls, scalar=0.0, in1=lsx[:, 512:1024], op0=ALU.min,
                                     op1=ALU.subtract).then_inc(sem("ls_ready"), 1)
            dve.wait_ge(*upto("ls_ready"))
            dve.wait_ge(*upto("glr_done"))
            for c in range(8):
                dve.tensor_tensor_scan(b64[:, c * 64:(c + 1) * 64], ones[:, 0:64],
                                       ls[:, c * 64:(c + 1) * 64], 0.0, ALU.mult, ALU.add
                                       ).then_inc(sem("b64_ready"), 1)
            for k in range(GLA_QT):
                dve.tensor_tensor_scan(b256[:, k * T:(k + 1) * T], ones[:, 0:T],
                                       ls[:, k * T:(k + 1) * T], 0.0, ALU.mult, ALU.add
                                       ).then_inc(sem("b256_ready"), 1)
            dve.memset(S4[:, :], 0.0).then_inc(sem("gs4_zero"), 1)
            GSC = float(GLA_DK) ** -0.5
            gq, gk = tile(projR, 8, 2), tile(projR, 10, 2)
            dve.wait_ge(*upto("ge_ready", 2))
            dve.scalar_tensor_tensor(out=q2[0], in0=gq, scalar=GSC, in1=e2[0], op0=ALU.mult,
                                     op1=ALU.mult).then_inc(sem("gqk_ready"), 1)
            dve.tensor_tensor(k2[0], gk, e2[1], ALU.mult).then_inc(sem("gqk_ready"), 1)
            dve.memset(q2[1], 0.0).then_inc(sem("gs4_zero"), 1)
            dve.memset(k2[1], 0.0).then_inc(sem("gs4_zero"), 1)
            dve.wait_ge(*upto("gs4_zero", 3))
            dve.wait_ge(*upto("gqk_ready", 2))
            dve.wait_ge(*upto("b256_ready", 2))
            for n, L in enumerate((64, P)):
                bv, ev = blocks(b256, L), blocks(e2[n], L)
                ref = bv[:, :, L - 1:L].to_broadcast([P, 512 // (2 * L), L])
                dve.tensor_tensor(ev[:, :, 0:L], ref, bv[:, :, 0:L], ALU.subtract
                                  ).then_inc(sem("gd_ready"), 1)
                dve.tensor_tensor(ev[:, :, L:2 * L], bv[:, :, L:2 * L], ref, ALU.subtract
                                  ).then_inc(sem("gd_ready"), 1)

            def gla_collect(n, mask):
                dve.wait_ge(*upto("gl_done", 2 * n + 2))
                if n:
                    dve.wait_ge(*upto("gl_out", 2 * n))
                m = lmask[:, mask, :].bitcast(U32).unsqueeze(1).to_broadcast([P, 4, P])
                for b in range(2):
                    dve.copy_predicated(
                        S4[:, b * 512:(b + 1) * 512].rearrange("p (n t) -> p n t", t=P), m,
                        bank[6 + b][:, :].rearrange("p (n t) -> p n t", t=P)
                    ).then_inc(sem("gl_out"), 1)

            for n, L in enumerate((64, P)):
                dve.wait_ge(*upto("ge_ready", 3 + n))
                ev, o = blocks(e2[n], L), (n + 1) % 2
                if n:
                    dve.wait_ge(*upto("gl_done", 2))
                dve.tensor_tensor(blocks(k2[o], L)[:, :, 0:L], blocks(gk, L)[:, :, 0:L],
                                  ev[:, :, 0:L], ALU.mult).then_inc(sem("gqk_ready"), 1)
                dve.scalar_tensor_tensor(out=blocks(q2[o], L)[:, :, L:2 * L],
                                         in0=blocks(gq, L)[:, :, L:2 * L], scalar=GSC,
                                         in1=ev[:, :, L:2 * L], op0=ALU.mult, op1=ALU.mult
                                         ).then_inc(sem("gqk_ready"), 1)
                gla_collect(n, CHUNK if n == 0 else len(LEVELS) - 1)
            dve.wait_ge(*upto("gl_done", 6))
            for b in range(2):
                dve.tensor_copy(SX2[:, b * T:(b + 1) * T].rearrange("p (h t) -> p h t", t=P),
                                bank[6 + b][:, :].rearrange("p (h t) -> p h t", t=T)[:, :, 0:P]
                                ).then_inc(sem("gl_out"), 1)
            dve.wait_ge(*upto("lam_v", 3))
            dve.wait_ge(*upto("lgate_out", HT))
            for k in range(HT):
                dve.tensor_scalar(tile(T4, k), tile(T4, k), lru[:, 2 * HT + k:2 * HT + k + 1], None,
                                  ALU.mult).then_inc(sem("la_ready"), 1)
            dve.wait_ge(*upto("lgate_out", 2 * HT))
            dve.tensor_tensor(G4[:, :], G4[:, :], XC, ALU.mult).then_inc(sem("gi_ready"), 1)
            y = tile(projR, 4, 4)
            dve.wait_ge(*upto("h3_ready"))
            dve.tensor_tensor(gel, y, y, ALU.mult).then_inc(sem("gelu_a"), 1)
            dve.wait_ge(*upto("gelu_a", 1))
            dve.tensor_scalar(gel, gel, GELU_CUBIC, 1.0, ALU.mult, ALU.add
                              ).then_inc(sem("gelu_a"), 1)
            dve.wait_ge(*upto("gelu_a", 2))
            dve.tensor_tensor(gel, gel, y, ALU.mult).then_inc(sem("gelu_in"), 1)
            dve.wait_ge(*upto("lru_a"))
            dve.wait_ge(*upto("lru_th"))
            dve.tensor_tensor(T4[:, :], A8, A8, ALU.mult).then_inc(sem("a2_ready"), 1)
            dve.wait_ge(*upto("a2_ready"))
            dve.scalar_tensor_tensor(out=th, in0=T4[:, :], scalar=1.0, in1=th, op0=ALU.add,
                                     op1=ALU.mult).then_inc(sem("lru_m"), 1)
            dve.wait_ge(*upto("gelu_tanh"))
            dve.scalar_tensor_tensor(out=gel, in0=gel, scalar=1.0, in1=y, op0=ALU.add, op1=ALU.mult
                                     ).then_inc(sem("gelu_y"), 1)
            dve.wait_ge(*upto("lru_root"))
            dve.wait_ge(*upto("gi_ready"))
            dve.tensor_tensor(G4[:, :], G4[:, :], th, ALU.mult).then_inc(sem("u_ready"), 1)
            dve.wait_ge(*upto("u_ready"))
            for k in range(HT):
                dve.tensor_tensor_scan(tile(T4, k), tile(A8, k), tile(G4, k), 0.0, ALU.mult, ALU.add
                                       ).then_inc(sem("lru_h"), 1)
            dve.wait_ge(*upto("lru_h", HT))
            dve.wait_ge(*upto("gelu_y"))
            dve.scalar_tensor_tensor(out=mixin[:, 0:HT * T], in0=gel, scalar=0.5, in1=T4[:, :],
                                     op0=ALU.mult, op1=ALU.mult).then_inc(sem("mix2_ready"), 1)
            dve.wait_ge(*upto("og_rms", 2))
            dve.reciprocal(rms[:, :], rms[:, :]).then_inc(sem("og_rinv"), 1)
            dve.wait_ge(*upto("og_rinv"))
            dve.scalar_tensor_tensor(out=A8, in0=XC, scalar=v("gla_gnorm_2"), in1=rms[:, :],
                                     op0=ALU.mult, op1=ALU.mult).then_inc(sem("og_normed"), 1)
            dve.wait_ge(*upto("og_normed"))
            dve.wait_ge(*upto("gout_ready"))
            dve.tensor_tensor(A8, A8, tile(projR, 16, 4), ALU.mult).then_inc(sem("mix2_ready"), 1)
            out_dense(dve, wout2, 1, mixT2)
            dve.wait_ge(*upto("wout2_out0", 2))
            dve.wait_ge(*upto("wout2_out1", 2))
            for k in range(KT):
                dve.scalar_tensor_tensor(out=tile(hT, k), in0=tile(mixT2, k),
                                         scalar=modT[:, 2 * KT + k:2 * KT + k + 1], in1=tile(hT, k),
                                         op0=ALU.mult, op1=ALU.add).then_inc(sem("x2_ready"), 1)
            dve_norm(dve, "nffn2", hT, lambda k: gs[:, KT + k:KT + k + 1], uT, KT)

            steps = [0]

            def step(ins):
                ins.then_inc(sem("route"), 1)
                steps[0] += 1
                dve.wait_ge(*upto("route", steps[0]))

            def tab(at, n=NE):
                return rt[:, at:at + TT * n].rearrange("p (t n) -> p t n", t=TT)

            def val(i):
                return rs[:, i * TT:(i + 1) * TT]

            def over(i, n):
                return val(i).unsqueeze(2).to_broadcast([P, TT, n])

            ie = iotg[:, :].rearrange("p (t n) -> p t n", t=TT)
            ic = iotc[:, :].rearrange("p (t n) -> p t n", t=TT)
            dve.wait_ge(*upto("iotas", 3))
            dve.wait_ge(*upto("lg_done", TT))
            lgv = lg[:, :].rearrange("p (t n) -> p t n", t=TT)
            step(dve.tensor_copy(lgv, bank[0][:, 0:TT * 64].rearrange("p (t n) -> p t n", t=TT)
                                 [:, :, 0:NL]))
            step(dve.tensor_reduce(val(0), lgv[:, :, 0:NG], AX.X, ALU.max))
            dve.tensor_tensor(tab(0, NG), lgv[:, :, 0:NG], over(0, NG), ALU.subtract
                              ).then_inc(sem("cs_ready"), 1)
            step(dve.tensor_tensor(tab(64, NG), lgv[:, :, 0:NG], over(0, NG), ALU.is_equal))

            def first_of(eq, iota, dst, n, i):
                step(dve.scalar_tensor_tensor(out=eq, in0=eq, scalar=-1000.0, in1=iota,
                                              op0=ALU.mult, op1=ALU.add))
                step(dve.tensor_reduce(val(i), eq, AX.X, ALU.min))
                step(dve.tensor_tensor(dst, eq, over(i, n), ALU.is_equal))

            first_of(tab(64, NG), ic, tab(128, NG), NG, 1)
            dve.wait_ge(*upto("ec_ready"))
            step(dve.tensor_reduce(val(2), tab(0, NG), AX.X, ALU.add))
            step(dve.reciprocal(val(2), val(2)))
            step(dve.tensor_scalar(tab(128, NG), tab(128, NG), -NEG_BIG, NEG_BIG, ALU.mult, ALU.add))
            grp = rt[:, 128:128 + TT * NG].unsqueeze(2).to_broadcast([P, TT * NG, EPG])
            step(dve.tensor_copy(rt[:, 192:192 + TT * NE].rearrange("p (g e) -> p g e", e=EPG), grp))
            step(dve.tensor_tensor(tab(192), tab(192), lgv[:, :, NG:NL], ALU.add))
            step(dve.tensor_reduce(val(5), tab(192), AX.X, ALU.max))
            step(dve.tensor_tensor(tab(256), tab(192), over(5, NE), ALU.is_equal))
            first_of(tab(256), ie, tab(TA1), NE, 1)
            step(dve.scalar_tensor_tensor(out=tab(192), in0=tab(TA1), scalar=2 * NEG_BIG,
                                          in1=tab(192), op0=ALU.mult, op1=ALU.add))
            step(dve.tensor_reduce(val(6), tab(192), AX.X, ALU.max))
            step(dve.tensor_tensor(tab(256), tab(192), over(6, NE), ALU.is_equal))
            first_of(tab(256), ie, tab(TA2), NE, 1)
            dve.tensor_tensor(tab(TA), tab(TA1), tab(TA2), ALU.add).then_inc(sem("a_set"), 1)
            dve.tensor_tensor(val(4), val(6), val(5), ALU.subtract).then_inc(sem("dm_ready"), 1)
            dve.wait_ge(*upto("e21_ready"))
            step(dve.tensor_scalar(val(7), val(4), 1.0, None, ALU.add))
            step(dve.reciprocal(val(7), val(7)))
            step(dve.tensor_tensor(val(7), val(7), val(2), ALU.mult))
            step(dve.tensor_tensor(val(8), val(7), val(4), ALU.mult))
            dve.wait_ge(*upto("rank_done"))
            step(dve.tensor_copy(rt[:, 256:256 + NE], bank[1][:, 2 * NE:3 * NE]))
            step(dve.tensor_tensor_scan(rt[:, 192:192 + NE], ones[:, 0:NE], rt[:, 256:256 + NE], 0.0,
                                        ALU.mult, ALU.add))
            step(dve.tensor_tensor(rt[:, 192:192 + NE], rt[:, 192:192 + NE], rt[:, 256:256 + NE],
                                   ALU.subtract))
            dve.tensor_copy(tbl[:, 0:NE], rt[0:1, 192:192 + NE]).then_inc(sem("tbl_ready"), 1)
            dve.tensor_copy(tbl[:, NE:2 * NE], rt[0:1, 256:256 + NE]).then_inc(sem("tbl_ready"), 1)
            step(dve.tensor_tensor(
                tab(320), bank[1][:, 0:2 * NE].rearrange("p (t n) -> p t n", t=TT),
                rt[:, 192:192 + NE].unsqueeze(1).to_broadcast([P, TT, NE]), ALU.add))
            for c, ta in enumerate((TA1, TA2)):
                step(dve.tensor_tensor(tab(ta), tab(ta), tab(320), ALU.mult))
                step(dve.tensor_reduce(val(12 + c), tab(ta), AX.X, ALU.add))
            for t in range(TT):
                s1, s2 = (rs[:, (12 + c) * TT + t:(12 + c) * TT + t + 1] for c in range(2))
                w1, w2 = (rs[:, (7 + c) * TT + t:(7 + c) * TT + t + 1] for c in range(2))
                step(dve.tensor_scalar(Psel[:, t, :], iot[:, :], s1, None, ALU.is_equal))
                dve.scalar_tensor_tensor(out=Psel[:, t, :], in0=iot[:, :], scalar=s2,
                                         in1=Psel[:, t, :], op0=ALU.is_equal, op1=ALU.add
                                         ).then_inc(sem("psel_ready"), 1)
            for t in range(TT):
                s1, s2 = (rs[:, (12 + c) * TT + t:(12 + c) * TT + t + 1] for c in range(2))
                w1, w2 = (rs[:, (7 + c) * TT + t:(7 + c) * TT + t + 1] for c in range(2))
                step(dve.tensor_scalar(Pw[:, t, :], iot[:, :], s1, w1, ALU.is_equal, ALU.mult))
                step(dve.tensor_scalar(SV4[:, 0:SLOTS], iot[:, :], s2, w2, ALU.is_equal, ALU.mult))
                dve.tensor_tensor(Pw[:, t, :], Pw[:, t, :], SV4[:, 0:SLOTS], ALU.add
                                  ).then_inc(sem("pw_ready"), 1)
                dve.wait_ge(*upto("pw_ready", t + 1))

            gt2 = modT[:, 5 * KT:6 * KT].rearrange("p (q c) -> p q c", c=2).unsqueeze(3
                  ).to_broadcast([P, 4, 2, WIN])

            def hidden(par, name, count):
                dve.wait_ge(*upto(f"{name}sil{par}", count))
                dve.tensor_tensor(hid, sil, bank[par][2 * WIN:P, 0:256], ALU.mult
                                  ).then_inc(sem(f"{name}hid{par}"), 1)
                dve.wait_ge(*upto(f"{name}yt{par}", count))

            def outputs(start, par, name):
                dve.tensor_tensor(
                    ysT[:, :, bass.ds(start, WIN)].rearrange("p (q c) s -> p q c s", c=2),
                    bank[6 + par][:, 0:256].rearrange("p (c q s) -> p q c s", c=2, q=4), gt2,
                    ALU.mult
                ).then_inc(sem(f"{name}yt_out{par}"), 1)

            dve.memset(hidw[0:2 * WIN, :], 0.0).then_inc(sem("hidw_zero"), 1)
            dve.wait_ge(*upto("xs_out", KT))
            dve.wait_ge(*upto("x2tok", 4))
            with dve.Fori(0, NE // 2) as i:
                for par in range(2):
                    start = dve.value_load(tbl[0:1, bass.ds(i * 2 + par, 1)],
                                           min_val=0, max_val=SLOTS)
                    count = dve.value_load(tbl[0:1, bass.ds(i * 2 + (NE + par), 1)],
                                           min_val=0, max_val=T)
                    with dve.If(count > 0):
                        hidden(par, "", i + 1)
                        last = i + 1 if par else i
                        dve.wait_ge(*upto(f"yt_out{1 - par}", last))
                        dve.wait_ge(*upto(f"byt_out{1 - par}", last * (NWIN - 1)))
                        outputs(start, par, "")
                        with dve.If(count > WIN):
                            hidden(par, "b", i * (NWIN - 1) + 1)
                            outputs(start + WIN, par, "b")
                            with dve.If(count > 2 * WIN):
                                with dve.Fori(2, NWIN) as w:
                                    with dve.If(count > w * WIN):
                                        hidden(par, "b", i * (NWIN - 1) + w)
                                        outputs(start + w * WIN, par, "b")
                                    with dve.Else():
                                        for name in ("hid", "yt_out"):
                                            dve.drain().then_inc(sem(f"b{name}{par}"), 1)
                            with dve.Else():
                                for name in ("hid", "yt_out"):
                                    dve.drain().then_inc(sem(f"b{name}{par}"), NWIN - 2)
                        with dve.Else():
                            for name in ("hid", "yt_out"):
                                dve.drain().then_inc(sem(f"b{name}{par}"), NWIN - 1)
                    with dve.Else():
                        for name in ("hid", "yt_out"):
                            dve.drain().then_inc(sem(f"{name}{par}"), 1)
                            dve.drain().then_inc(sem(f"b{name}{par}"), NWIN - 1)
            for t in range(TT):
                for b in range(2):
                    c = slice(t * D + b * 512, t * D + (b + 1) * 512)
                    dve.wait_ge(*upto("comb_done", 2 * t + b + 1))
                    dve.tensor_tensor(x2tok[:, c], x2tok[:, c], bank[2 * t + b][:, :], ALU.add
                                      ).then_inc(sem("x3_ready"), 1)
            for t in range(TT):
                dve.wait_ge(*upto("fin_rms", t + 1))
                dve.wait_ge(*upto("gfin_in", 16))
                dve.reciprocal(rs[:, 22 + t:23 + t], rs[:, 22 + t:23 + t]).then_inc(sem("fin_rinv"), 1)
                dve.wait_ge(*upto("fin_rinv", t + 1))
                c = slice(t * D, (t + 1) * D)
                dve.scalar_tensor_tensor(out=x2tok[:, c], in0=x2tok[:, c], scalar=rs[:, 22 + t:23 + t],
                                         in1=gfin[:, :], op0=ALU.mult, op1=ALU.mult
                                         ).then_inc(sem("y_ready"), 1)

_INS = ["x", "p", "attn_pre_norm", "w_in", "hg_lower_gamma", "hg_out_norm", "sb_out_norm", "w_out",
        "attn_post_norm", "ffn_pre_norm", "w_gate_up", "w_down", "ffn_post_norm", "ple_proj",
        "ple_gate", "c_2", "w_ada_2", "b_ada_2", "g_mix_2", "g_ffn_2", "g_final_2", "w_in_2",
        "conv_w_2", "conv_b_2", "lru_wr_2", "lru_br_2", "lru_wi_2", "lru_bi_2", "lru_lambda_2",
        "gla_wa2_2", "gla_ba_2", "gla_gnorm_2", "w_out_2", "w_coarse_2", "b_coarse_2", "w_fine_2",
        "b_fine_2", "w_gate_2", "w_up_2", "w_down_2"]


def kernel(**inputs):
    import numpy as _np
    import concourse.bacc as _bacc
    from concourse.bass_utils import run_bass_kernel_spmd as _run

    nc = _bacc.Bacc("TRN2", target_bir_lowering=False, num_devices=1)
    arrays, dram = {}, {}
    for name in _INS:
        a = _np.ascontiguousarray(inputs[name])
        arrays[f"in_{name}"] = a
        dram[name] = nc.dram_tensor(f"in_{name}", a.shape, mybir.dt.from_np(a.dtype),
                                    kind="ExternalInput").ap()
    shape = arrays["in_x"].shape
    out = nc.dram_tensor("out_0", shape, F32, kind="ExternalOutput").ap()
    build_program(nc, dram, out)
    r = _run(nc, [arrays], core_ids=[0])
    return r.results[0]["out_0"]
```

```python
from contextlib import ExitStack

import concourse.bass as bass
from concourse import mybir

F32 = mybir.dt.float32
F32R = mybir.dt.float32r
I32 = mybir.dt.int32
U32 = mybir.dt.uint32
ALU = mybir.AluOpType
ACT = mybir.ActivationFunctionType
AX = mybir.AxisListType

P = 128
EPS = 1e-6
SQRT_2_OVER_PI = 0.7978845608028654
GELU_CUBIC = 0.044715
NEG_BIG = -1.0e30


def build_program(nc, d, out):
    T, D = d["x"].shape[1:]
    KT = D // P
    TT = T // P
    D_FF = d["w_down"].shape[1]
    IN1 = d["w_in"].shape[2]
    IN2 = d["w_in_2"].shape[2]
    PLE = d["p"].shape[3]
    HW = d["hg_out_norm"].shape[1]
    HT = HW // P
    HG_HEADS = HT
    SB_DH = 64
    SB_HEADS = HW // SB_DH
    SCALE_SB = float(SB_DH) ** -0.5
    GLA_HEADS, GLA_DK = 4, 64
    GLA_QT = GLA_HEADS * GLA_DK // P
    GLA_CHUNK = 64
    GATE_RANK = d["gla_wa2_2"].shape[1]
    GATE_NORM = 16.0
    LRU_C = 8.0
    NE, _, DE = d["w_gate_2"].shape[1:]
    NG = d["w_coarse_2"].shape[2]
    EPG = NE // NG
    TOPK = 2
    SLOTS = TOPK * T
    WIN = 32
    NWIN = T // WIN
    PADDED = SLOTS + T
    CH = 2048
    assert (T, D, DE, NE) == (256, 1024, 512, 32) and HW == 512

    ctx = ExitStack()
    with ctx:
        def sb(name, shape, dt=F32):
            return ctx.enter_context(nc.sbuf_tensor(name, shape, dt))

        shared, outs = {}, 0
        for n, (norm, tiles) in enumerate((("n1", KT), ("nhg", HT), ("nsb", HT), ("npost", KT),
                                           ("nffn", KT), ("nfpost", KT), ("nmix2", KT),
                                           ("nffn2", KT))):
            for part in ("ss", "rms", "rinv"):
                shared[f"{norm}_{part}"] = (f"norm_{part}", n)
            shared[f"{norm}_sq"] = ("norm_sq", outs // 2)
            shared[f"{norm}_out"] = ("norm_out", outs)
            outs += tiles
        for layers in ((("proj1", IN1 // 512), ("proj2", IN2 // 512)),
                       (("wout1", D // 512), ("pgate", D // 512), ("wout2", D // 512))):
            group, rounds = layers[0][0], 0
            for layer, n in layers:
                for j in range(2):
                    shared[f"{layer}_full{j}"] = (f"{group}_slot{j}_full", 16 * rounds)
                    shared[f"{layer}_hi{j}"] = (f"{group}_slot{j}_hi", 2 * rounds)
                    shared[f"{layer}_lo{j}"] = (f"{group}_slot{j}_lo", 2 * rounds)
                    shared[f"{layer}_done{j}"] = (f"{group}_slot{j}_done", rounds)
                    shared[f"{layer}_out{j}"] = (f"{group}_bank{j}_out", rounds + 1)
                rounds += n
        for n, layer in enumerate(("proj1", "wout1", "ffn", "pgate", "proj2", "wout2")):
            for part in ("hi", "lo"):
                shared[f"{layer}_src_{part}"] = (f"src_{part}", 4 * n)

        FREE = {"act": ["proj1_out0", "proj1_out1", "wout1_out0", "wout1_out1", "silu_ready"],
                "dve": ["hid_ready", "yt_out0", "yt_out1", "byt_out0", "byt_out1"],
                "pe": ["down_done", "gu_free0", "gu_free1", "d_free0", "d_free1"]}
        for names in FREE.values():
            for name in names:
                shared.setdefault(name, (name, 1))

        levels = 8
        for engine, steps in (
                ("act_a", (("hT_ready", 4), ("vec_ready", 2), ("pT_ready", 1), ("lb_ready", 2),
                           ("csig_ready", 1), ("hg_sig", 4), ("g_ready", 1), ("vtok_ready", 4),
                           ("z_out", 8), ("e_ready", levels), ("a_ready", 8),
                           ("ohg_out", 2), ("osb_out", 2), ("y_out", 4), ("pp_out", 4))),
                ("act_b", (("lam", 3), ("glr_out", 1), ("gv_out", 2), ("ga", 5), ("ge_ready", 4),
                           ("lgate_out", 8), ("lru_a", 1), ("lru_th", 1), ("gelu_tanh", 1),
                           ("lru_root", 1), ("gout_ready", 1), ("og_out", 2), ("og_sq", 2),
                           ("og_rms", 2), ("lgt_out", 1), ("ec_ready", 1), ("h2tok", 4),
                           ("e21_ready", 1), ("x2tok", 4), ("xs_out", 8), ("pwt_out", 2), ("yt_out", 8))),
                ("dve_a", (("lbd_ready", 1), ("csil_ready", 1), ("crep_ready", 8), ("f_ready", 4),
                           ("q_ready", 1), ("k_ready", 4), ("hgate_ready", 1), ("b_ready", 4),
                           ("mod_ready", 3), 
                           ("sx_ready", 8), ("ohg_ready", 1), ("ple_ready", 4))),
                ("dve_b", (("gs_ready", 2), ("lam_v", 3), ("conv", 16), ("ls_ready", 1),
                           ("b64_ready", 8), ("b256_ready", 2), ("la_ready", 4), ("gi_ready", 1),
                           ("gelu_a", 2), ("gelu_in", 1), ("a2_ready", 1), ("lru_m", 1),
                           ("gelu_y", 1), ("u_ready", 1), ("lru_h", 4), ("og_rinv", 2),
                           ("og_normed", 2), ("x2_ready", 8), ("cs_ready", 1), ("a_set", 1),
                           ("dm_ready", 1), ("h2lo", 4), ("tbl_ready", 2), ("psel_ready", 2), ("pw_ready", 2),
                           ("x3_ready", 4))),
                ("pool_a", (("lv_zero", 5), ("z_pos", 8), ("sp_full", 8), ("lm_ready", 8),
                            ("h1_ready", 4), ("h2_ready", 4), ("h3_ready", 4))),
                ("pe_a", (("xT_done", 4), ("vT_done", 1), ("vtok_done", 4), ("z_done", 8),
                          ("lv_done", levels + 1), ("mod_done", 3), ("sx_done", 8),
                          ("ohg_done", 2), ("osb_done", 2), ("y_done", 1), ("pp_done", 4))),
                ("pe_b", (("glr_done", 1), ("gv_done", 2), ("ga_done", 1), ("lgate_done", 2),
                          ("gl_done", 6), ("og_done", 2), ("og_ss", 2), ("lgt_done", 1), ("lg_done", 1),
                          ("tok_done", 4), ("rank_done", 1), ("xtok_done", 4), ("xs_done", 8), ("pwt_done", 2),
                          ("pw_done", 1), ("yt_done", 8), ("comb_done", 4)))):
            done = 0
            for name, n in steps:
                shared[name] = (f"{engine}_steps", done)
                done += n

        sems = {}

        def sem(name):
            name, _ = shared.get(name, (name, 0))
            if name not in sems:
                sems[name] = ctx.enter_context(nc.semaphore(name))
            return sems[name]

        def with_float32r(name, shape):
            at = -(-nc.sbuf_base // 32) * 32
            plain = sb(name, shape)
            return plain, nc.alloc_sbuf_tensor_at(name + "_r", shape, F32R, offset=at)

        Wlo, Wlo_r = with_float32r("Wlo", [P, 6 * CH])
        Whi, Whi_r = with_float32r("Whi", [P, 6 * CH])
        slot = [Wlo[:, i * CH:(i + 1) * CH] for i in range(6)]
        slot += [Whi[:, i * CH:(i + 1) * CH] for i in range(6)]
        slot_r = [Wlo_r[:, i * CH:(i + 1) * CH] for i in range(6)]
        slot_r += [Whi_r[:, i * CH:(i + 1) * CH] for i in range(6)]
        projR = sb("projR", [P, (IN1 // P) * T])
        R24, R24_r = with_float32r("R24", [P, 3 * KT * T])
        hT = sb("hT", [P, KT * T])
        mixin = sb("mixin", [P, KT * T])
        G4 = sb("G4", [P, HT * T])
        T4, T4_r = with_float32r("T4", [P, HT * T])
        V4 = sb("V4", [P, TT * HW])
        SV4 = sb("SV4", [P, TT * HW])
        S4 = sb("S4", [P, HT * T])
        SX2 = sb("SX2", [P, HT * P])
        rms = sb("rms", [P, HT * T])

        uT = R24[:, 0:KT * T]
        sq = R24[:, KT * T:2 * KT * T]
        xk = R24[:, 2 * KT * T:3 * KT * T]
        mixT = Whi[:, 5 * CH:6 * CH]
        zb = Whi[:, 0:3072]
        lb_ = Whi[:, 3072:6144]
        eb = Whi[:, 6144:9216]

        ident = sb("ident", [P, P])
        ones = sb("ones", [P, T])
        tri_ge = sb("tri_ge", [P, P])
        tri_lt = sb("tri_lt", [P, P])
        LEVELS = [1, 2, 4, 8, 16, 32, 64]
        lmask = sb("lmask", [P, 9, P])
        DIAG, CHUNK = 7, 8
        negm = sb("negm", [P, 3 * P])
        bigm = sb("bigm", [P, 3 * P])
        epsc = sb("epsc", [P, 1])
        vrow = sb("vrow", [P, P])
        brow = sb("brow", [P, P])
        vec = sb("vec", [P, P])
        badaT = sb("badaT", [P, 6 * KT])
        modT = sb("modT", [P, 6 * KT])
        small = sb("small", [P, 64])

        VROWS = [("attn_pre_norm", KT), ("hg_lower_gamma", 2 * HT), ("hg_out_norm", HT),
                 ("sb_out_norm", HT), ("attn_post_norm", KT), ("ffn_pre_norm", KT),
                 ("ffn_post_norm", KT), ("c_2", KT), ("g_mix_2", KT), ("g_ffn_2", KT),
                 ("conv_w_2", 4 * HT), ("conv_b_2", HT), ("lru_br_2", HT), ("lru_bi_2", HT),
                 ("lru_lambda_2", HT), ("gla_ba_2", GLA_QT), ("gla_gnorm_2", 1)]
        VO, at = {}, 0
        for name, n in VROWS:
            VO[name] = at
            at += n
        NV = at

        def v(name, k=0):
            return vec[:, VO[name] + k:VO[name] + k + 1]

        bank = [ctx.enter_context(nc.psum_tensor(f"bank{i}", [P, 512], F32)) for i in range(8)]

        def tile(region, k, n=1):
            return region[:, k * T:(k + n) * T]

        def half(region, k, t):
            return region[:, k * T + t * P:k * T + (t + 1) * P]

        def vector_rows(name):
            src = d[name]
            if len(src.shape) == 3:
                src = src.rearrange("a b n -> a (b n)")
            return src.rearrange("a (k p) -> (a k) p", p=P)

        x_tok = xk
        p_tok = sb("p_tok", [P, TT * PLE])
        pT = sb("pT", [P, (PLE // P) * T])
        crep = sb("crep", [P, KT * 36])
        csil = sb("csil", [P, KT])
        cnow = crep[:, KT * 32:KT * 36]

        def upto(name, value=1):
            _, before = shared.get(name, (name, 0))
            return sem(name), value + before

        def signal_free(e, engine):
            for name in FREE[engine]:
                e.drain().then_inc(sem(name), 1)

        SRC_LO, SRC_HI = (0, KT * T), (KT * T, 2 * KT * T)
        proj1 = ("proj1", d["w_in"][0], IN1 // 256, (0, 1), (6, 7, 8, 9), (0, 1), SRC_HI)
        wout1 = ("wout1", d["w_out"][0], D // 256, (2, 3), (0, 1, 4, 5), (2, 3), SRC_LO)
        pgate = ("pgate", d["ple_gate"][0], D // 256, (2, 3), (6, 7, 8, 9), (2, 3), SRC_LO)
        proj2 = ("proj2", d["w_in_2"][0], IN2 // 256, (0, 1), (6, 7, 8, 9), (0, 1), SRC_HI)
        wout2 = ("wout2", d["w_out_2"][0], D // 256, (2, 3), (6, 7, 8, 9), (2, 3), SRC_LO)
        IN2_FULL = IN2 // 256 * 256
        HALF = CH // 2

        def sp_load(sp, layer, i, j):
            name, w, _, sl = layer[:4]
            sp.dma_start(slot[sl[j]].rearrange("p (k n) -> p k n", k=KT),
                         w.rearrange("(k p) n -> p k n", p=P)[:, :, bass.ds(i * 512 + j * 256, 256)]
                         ).then_inc(sem(f"{name}_full{j}"), 16)

        def sp_dense(sp, layer):
            name, n = layer[0], layer[2]
            for j in range(2):
                sp_load(sp, layer, 0, j)
            with sp.Fori(1, n // 2) as i:
                for j in range(2):
                    sp.wait_ge(*upto(f"{name}_lo{j}", i * 2))
                    sp_load(sp, layer, i, j)

        def act_hi(act, layer, i, j):
            name, sl, parts = layer[0], layer[3], layer[4]
            act.wait_ge(*upto(f"{name}_full{j}", i * 16 + 16))
            for h in range(2):
                c = slice(h * HALF, (h + 1) * HALF)
                act.activation(slot_r[parts[2 * j]][:, c], slot[sl[j]][:, c], ACT.Copy
                               ).then_inc(sem(f"{name}_hi{j}"), 1)

        def dve_lo(dve, layer, i, j):
            name, sl, parts = layer[0], layer[3], layer[4]
            for h in range(2):
                c = slice(h * HALF, (h + 1) * HALF)
                dve.wait_ge(*upto(f"{name}_hi{j}", i * 2 + (h + 1)))
                dve.tensor_tensor(slot_r[parts[2 * j + 1]][:, c], slot[sl[j]][:, c],
                                  slot_r[parts[2 * j]][:, c].bitcast(F32), ALU.subtract
                                  ).then_inc(sem(f"{name}_lo{j}"), 1)

        def act_first(act, layer):
            for j in range(2):
                act_hi(act, layer, 0, j)

        def dve_first(dve, layer):
            for j in range(2):
                dve_lo(dve, layer, 0, j)

        def act_dense(act, layer, dst, func=ACT.Copy):
            name, n, bk = layer[0], layer[2], layer[5]

            def copy_out(i, j):
                act.activation(dst[:, bass.ds(i * 1024 + j * 512, 512)], bank[bk[j]][:, :], func
                               ).then_inc(sem(f"{name}_out{j}"), 1)

            with act.Fori(1, n // 2) as i:
                for j in range(2):
                    act.wait_ge(*upto(f"{name}_done{j}", i))
                    act_hi(act, layer, i, j)
                    copy_out(i - 1, j)
            for j in range(2):
                act.wait_ge(*upto(f"{name}_done{j}", n // 2))
                copy_out(n // 2 - 1, j)

        def dve_dense(dve, layer):
            with dve.Fori(1, layer[2] // 2) as i:
                for j in range(2):
                    dve_lo(dve, layer, i, j)

        def act_source(act, name, src, at, ready):
            for b in range(4):
                ready(b)
                act.activation(tile(R24_r[:, at[0]:at[0] + KT * T], 2 * b, 2), tile(src, 2 * b, 2),
                               ACT.Copy).then_inc(sem(f"{name}_src_hi"), 1)

        def dve_source(dve, name, src, at):
            for b in range(4):
                dve.wait_ge(*upto(f"{name}_src_hi", b + 1))
                dve.tensor_tensor(tile(R24_r[:, at[1]:at[1] + KT * T], 2 * b, 2),
                                  tile(src, 2 * b, 2),
                                  tile(R24_r[:, at[0]:at[0] + KT * T], 2 * b, 2).bitcast(F32),
                                  ALU.subtract).then_inc(sem(f"{name}_src_lo"), 1)

        def pe_chunk(pe, b, parts, at, name):
            w_hi, w_lo = slot_r[parts[0]], slot_r[parts[1]]
            x_hi, x_lo = (R24_r[:, a:a + KT * T] for a in at)
            for t in range(2):
                for k in range(KT):
                    c = slice(k * 256 + t * P, k * 256 + (t + 1) * P)
                    o = b[:, t * T:(t + 1) * T]
                    pe.matmul(o, w_hi[:, c], tile(x_hi, k), start=(k == 0), stop=False)
                    pe.matmul(o, w_hi[:, c], tile(x_lo, k), start=False, stop=False)
                    mm = pe.matmul(o, w_lo[:, c], tile(x_hi, k), start=False, stop=(k == KT - 1))
            mm.then_inc(sem(name), 1)

        def pe_dense(pe, layer):
            name, n, parts, bk, at = layer[0], layer[2], layer[4], layer[5], layer[6]
            pe.wait_ge(*upto(f"{name}_src_lo", 4))
            with pe.Fori(0, n // 2) as i:
                for j in range(2):
                    pe.wait_ge(*upto(f"{name}_lo{j}", i * 2 + 2))
                    pe.wait_ge(*upto(f"{name}_out{j}", i))
                    pe_chunk(pe, bank[bk[j]], parts[2 * j:2 * j + 2], at, f"{name}_done{j}")

        def rms_of(name):
            return rms[:, T:2 * T] if name == "nsb" else rms[:, 0:T]

        def act_norm(act, name, src, n, width, ready, layer=None):
            for b in range(n // 2):
                ready(b)
                act.activation(tile(sq, 2 * b, 2), tile(src, 2 * b, 2), ACT.Square
                               ).then_inc(sem(f"{name}_sq"), 1)
            if layer:
                act_first(act, layer)
            act.activation(small[:, 63:64], epsc[:, :], ACT.Sqrt).then_inc(sem("root_table"), 1)
            act.wait_ge(*upto(f"{name}_ss"))
            act.activation(rms_of(name), bank[7][:, 0:T], ACT.Sqrt, bias=epsc[:, :],
                           scale=1.0 / width).then_inc(sem(f"{name}_rms"), 1)

        def pe_norm(pe, name, n):
            for k in range(n):
                if k % 2 == 0:
                    pe.wait_ge(*upto(f"{name}_sq", k // 2 + 1))
                mm = pe.matmul(bank[7][:, 0:T], ones[:, 0:P], tile(sq, k),
                               start=(k == 0), stop=(k == n - 1))
            mm.then_inc(sem(f"{name}_ss"), 1)

        def dve_norm(dve, name, src, gain, dst, n):
            dve.wait_ge(*upto(f"{name}_rms"))
            dve.reciprocal(rms_of(name), rms_of(name)).then_inc(sem(f"{name}_rinv"), 1)
            dve.wait_ge(*upto(f"{name}_rinv"))
            for k in range(n):
                dve.scalar_tensor_tensor(out=tile(dst, k), in0=tile(src, k), scalar=gain(k),
                                         in1=rms_of(name), op0=ALU.mult, op1=ALU.mult
                                         ).then_inc(sem(f"{name}_out"), 1)

        mixT2 = xk
        XC = V4[:, :]
        A8 = mixin[:, HT * T:2 * HT * T]
        gel, th = xk[:, 0:1024], xk[:, 1024:2048]
        e2 = [uT[:, 0:512], uT[:, 512:1024]]
        b64, b256 = uT[:, 1024:1536], uT[:, 1536:2048]
        q2 = [sq[:, 0:512], sq[:, 512:1024]]
        k2 = [sq[:, 1024:1536], sq[:, 1536:2048]]
        GV = projR[:, 20 * T:20 * T + TT * HW]
        TA, TA1, TA2 = 384, 448, 512
        lsx = SV4
        wrb = projR[:, 24 * T:24 * T + HT * P]
        wib = projR[:, 26 * T:26 * T + HT * P]
        wa2 = rms[0:GATE_RANK, 3 * T:4 * T]
        wlr = SX2
        glr = rms[0:GATE_RANK, 2 * T:3 * T]
        wcf = crep
        bcf = sb("bcf", [1, NG + NE])
        gfin = rms
        gs = sb("gs", [P, 2 * KT])
        lru = sb("lru", [P, 4 * HT])
        NL = NG + NE
        lg = vrow[:, 0:TT * NL]
        lgT = SV4[0:NL, 0:T]
        rt = V4
        rs = vrow[:, 96:P]
        tbl = sb("tbl", [1, 2 * NE], I32)
        iot = p_tok
        iotg = brow[:, 0:TT * NE]
        iotc = brow[:, TT * NE:TT * NL]
        xsT = projR[:, 0:KT * PADDED].rearrange("p (k s) -> p k s", k=KT)
        ysT = R24[:, :].rearrange("p (k s) -> p k s", k=KT)
        h2_hi, h2_lo = R24_r[:, 2 * KT * T:3 * KT * T], R24_r[:, KT * T:2 * KT * T]
        Psel_r = T4_r[:, :].rearrange("p (t s) -> p t s", t=TT)
        x2tok = mixin
        Pw = S4[:, :].rearrange("p (t s) -> p t s", t=TT)
        PwT = G4[:, :].rearrange("p (c t) -> p c t", t=T)
        xw = [S4[:, 0:KT * WIN], S4[:, KT * WIN:2 * KT * WIN]]
        sil, hid = V4[2 * WIN:P, 0:256], V4[2 * WIN:P, 256:512]
        hidw = V4[:, 256:512]
        hidT, yb = SV4[:, 0:P], SV4[:, P:P + 256]
        ystok = projR[:, 0:SLOTS // P * D]
        Wx = [Whi, Wlo]
        WG, WU, WD = 0, KT * DE, 2 * KT * DE

        qd = [sq[:, 0:1024], sq[:, 1024:2048]]
        kd = [xk[:, 0:1024], xk[:, 1024:2048]]
        ed = [uT[:, 0:1024], uT[:, 1024:2048]]
        ALL_LEVELS = LEVELS + [P]
        NC1 = 3 * len(LEVELS) + 4
        hb = G4[:, :]

        def blocks(ap, L):
            return ap.rearrange("p (n l) -> p n l", l=2 * L)

        def mod_row(b):
            return mixin[:, b * 512:(b + 1) * 512]

        block = ctx.enter_context(nc.Block())

        ffn_g = d["w_gate_up"][0].rearrange("(k p) n -> p k n", p=P)
        ffn_d = d["w_down"][0].rearrange("(k p) n -> p k n", p=P)
        NF = D_FF // 256
        ada_w = d["w_ada_2"][0].rearrange("(k p) n -> p k n", p=P)
        ADA_B = 6 * D // CH
        ADA_SLOTS = ((4, 5, 10), (2, 3, 11))
        ADA_AFTER = ((0,), (1, 2))
        assert IN1 // 512 == KT - 1

        @block.sync
        def _(sp):
            for name, n in VROWS[0::2]:
                sp.dma_start(vrow[VO[name]:VO[name] + n, :], vector_rows(name)
                             ).then_inc(sem("v_in"), 16)
            sp.wait_ge(*upto("x_in", 16))

            def ada_load(k, par, b):
                sp.dma_start(slot[ADA_SLOTS[par][b]],
                             ada_w[:, bass.ds(k, 1), b * CH:(b + 1) * CH].rearrange(
                                 "p k n -> p (k n)")).then_inc(sem(f"ada_full{b}{par}"), 16)

            for j in range(2):
                sp_load(sp, proj1, 0, j)
            for k in range(2):
                for b in range(ADA_B):
                    ada_load(k, k, b)
            with sp.Fori(0, (KT - 2) // 2) as i:
                for par in range(2):
                    r = i * 2 + (1 + par)
                    for j in range(2):
                        sp.wait_ge(*upto(f"proj1_lo{j}", r * 2))
                        sp_load(sp, proj1, r, j)
                        for b in ADA_AFTER[j]:
                            sp.wait_ge(*upto(f"ada_done{b}", r))
                            ada_load(r + 1, par, b)
            for b in range(2):
                sp.wait_ge(*upto(f"ada_done{b}", KT))
            sp_dense(sp, wout1)
            sp.wait_ge(*upto("wout1_done0", 2))
            sp.wait_ge(*upto("wout1_done1", 2))

            def ffn_load(i, first):
                if not first:
                    sp.wait_ge(*upto("gate_lo", i))
                sp.dma_start(slot[0].rearrange("p (k n) -> p k n", k=KT),
                             ffn_g[:, :, bass.ds(i * 256, 256)]).then_inc(sem("gate_full"), 16)
                if not first:
                    sp.wait_ge(*upto("up_lo", i))
                sp.dma_start(slot[1].rearrange("p (k n) -> p k n", k=KT),
                             ffn_g[:, :, bass.ds(i * 256 + D_FF, 256)]).then_inc(sem("up_full"), 16)
                if not first:
                    sp.wait_ge(*upto("down_lo", i))
                sp.dma_start(slot[4].rearrange("p (k n) -> p k n", k=2),
                             ffn_d[:, bass.ds(i * 2, 2), :]).then_inc(sem("down_full"), 16)

            ffn_load(0, True)
            with sp.Fori(1, NF) as i:
                ffn_load(i, False)
            sp.dma_start(slot[5].rearrange("p (k n) -> p k n", k=PLE // P),
                         d["ple_proj"][0].rearrange("(k p) n -> p k n", p=P)
                         ).then_inc(sem("pproj_full"), 16)
            sp.wait_ge(*upto("wout1_lo0", 4))
            sp.wait_ge(*upto("wout1_lo1", 4))
            sp_dense(sp, pgate)
            sp.wait_ge(*upto("gate_lo", NF))
            sp.wait_ge(*upto("up_lo", NF))
            for b in range(ADA_B):
                sp.wait_ge(*upto(f"ada_done{b}", KT))
            sp.wait_ge(*upto("bd_zero", 2))
            for dst, w in ((wrb, "lru_wr_2"), (wib, "lru_wi_2")):
                wv = d[w][0].rearrange("(n two) i j -> two i n j", two=2)
                for r in range(2):
                    sp.dma_start(dst[r * 64:(r + 1) * 64, :].rearrange("p (n j) -> p n j", j=P)
                                  [:, :, r * 64:(r + 1) * 64], wv[r]).then_inc(sem("sw_in"), 16)
            sp.dma_start(wa2[:, :], d["gla_wa2_2"][0]).then_inc(sem("sw_in"), 16)
            sp.dma_start(wlr[:, 0:KT * GATE_RANK].rearrange("p (k n) -> p k n", k=KT),
                          d["w_in_2"][0].rearrange("(k p) n -> p k n", p=P)[:, :, IN2_FULL:IN2]
                          ).then_inc(sem("sw_in"), 16)
            wv = wcf[:, 0:KT * NL].rearrange("p (k n) -> p k n", k=KT)
            sp.dma_start(wv[:, :, 0:NG], d["w_coarse_2"][0].rearrange("(k p) n -> p k n", p=P)
                          ).then_inc(sem("sw_in"), 16)
            sp.dma_start(wv[:, :, NG:NL], d["w_fine_2"][0].rearrange("(k p) n -> p k n", p=P)
                          ).then_inc(sem("sw_in"), 16)
            sp.dma_start(bcf[:, 0:NG], d["b_coarse_2"]).then_inc(sem("sw_in"), 16)
            sp.dma_start(bcf[:, NG:NL], d["b_fine_2"]).then_inc(sem("sw_in"), 16)
            sp_dense(sp, proj2)
            sp.wait_ge(*upto("pgate_lo0", 4))
            sp.wait_ge(*upto("pgate_lo1", 4))
            sp_dense(sp, wout2)

            def expert_load(e, par, i):
                for name, w, at, n in (("wg", "w_gate_2", WG, KT), ("wu", "w_up_2", WU, KT),
                                       ("wd", "w_down_2", WD, DE // P)):
                    if i is not None and name == "wg":
                        sp.wait_ge(*upto(f"gu_free{par}", i))
                    if i is not None and name == "wd":
                        sp.wait_ge(*upto(f"d_free{par}", i))
                    sp.dma_start(Wx[par][:, at:at + KT * DE].rearrange("p (k n) -> p k n", k=n),
                                 d[w][0][bass.ds(e, 1)].rearrange("a (k p) n -> p (a k) n", p=P)
                                 ).then_inc(sem(f"{name}_full{par}"), 16)

            for j in range(2):
                sp.wait_ge(*upto(f"wout2_done{j}", 2))
            expert_load(0, 0, None)
            sp.wait_ge(*upto("pp_done", 4))
            expert_load(1, 1, None)
            sp.wait_ge(*upto("nffn2_out", KT))
            sp.dma_start(gfin[:, :], d["g_final_2"].partition_broadcast(P)
                         ).then_inc(sem("gfin_in"), 16)
            sp.wait_ge(*upto("tbl_ready", 2))
            with sp.Fori(1, NE // 2) as i:
                for par in range(2):
                    count = sp.value_load(tbl[0:1, bass.ds(i * 2 + (NE + par), 1)],
                                          min_val=0, max_val=T)
                    with sp.If(count > 0):
                        expert_load(i * 2 + par, par, i)
                    with sp.Else():
                        sp.wait_ge(*upto(f"gu_free{par}", i))
                        for name in ("wg_full", "wu_full"):
                            sp.drain().then_inc(sem(f"{name}{par}"), 16)
                        sp.wait_ge(*upto(f"d_free{par}", i))
                        sp.drain().then_inc(sem(f"wd_full{par}"), 16)
            for t in range(TT):
                sp.wait_ge(*upto("y_ready", t + 1))
                sp.dma_start(out[0][t * P:(t + 1) * P, :], x2tok[:, t * D:(t + 1) * D]
                             ).then_inc(sem("stored"), 16)
            sp.wait_ge(*upto("stored", 16 * TT))

        @block.gpsimd
        def _(pool):
            pool.memset(ones[:, :], 1.0).then_inc(sem("ones_set"), 1)
            pool.memset(ident[:, :], 0.0).then_inc(sem("c0"), 1)
            pool.memset(tri_ge[:, :], 1.0).then_inc(sem("c0"), 1)
            pool.memset(tri_lt[:, :], 1.0).then_inc(sem("c0"), 1)
            pool.memset(epsc[:, :], EPS).then_inc(sem("c0"), 1)
            pool.memset(negm[:, :], -1.0).then_inc(sem("c0"), 1)
            pool.memset(bigm[:, :], 0.0).then_inc(sem("c0"), 1)
            pool.memset(lmask[:, :, :], 0.0).then_inc(sem("c0"), 1)
            pool.wait_ge(*upto("c0", 7))
            pool.affine_select(out=ident[:, :], in_=ident[:, :], compare_op=ALU.not_equal, fill=1.0,
                               base=0, pattern=[[-1, P]], channel_multiplier=1
                               ).then_inc(sem("ident_set"), 1)
            pool.affine_select(out=tri_ge[:, :], in_=tri_ge[:, :], compare_op=ALU.is_ge, fill=0.0,
                               base=0, pattern=[[-1, P]], channel_multiplier=1
                               ).then_inc(sem("const"), 1)
            pool.affine_select(out=tri_lt[:, :], in_=tri_lt[:, :], compare_op=ALU.is_gt, fill=0.0,
                               base=0, pattern=[[1, P]], channel_multiplier=-1
                               ).then_inc(sem("const"), 1)
            for m, fill in ((negm, 0.0), (bigm, NEG_BIG)):
                for c in (0, 2):
                    pool.affine_select(out=m[:, c * P:(c + 1) * P], in_=m[:, c * P:(c + 1) * P],
                                       compare_op=ALU.is_gt, fill=fill, base=0, pattern=[[1, P]],
                                       channel_multiplier=-1).then_inc(sem("const"), 1)
            n = 0
            for li, L in enumerate(LEVELS):
                second = blocks(lmask[:, li, :], L)[:, :, L:2 * L]
                pool.memset(second, 1.0).then_inc(sem("c1"), 1)
                pool.wait_ge(*upto("c1", n + 1))
                pool.affine_select(out=second, in_=second, compare_op=ALU.is_ge, fill=0.0, base=0,
                                   pattern=[[-2 * L, P // (2 * L)], [0, L]], channel_multiplier=1
                                   ).then_inc(sem("c1"), 1)
                pool.wait_ge(*upto("c1", n + 2))
                pool.affine_select(out=second, in_=second, compare_op=ALU.is_ge, fill=0.0, base=L - 1,
                                   pattern=[[2 * L, P // (2 * L)], [0, L]], channel_multiplier=-1
                                   ).then_inc(sem("c1"), 1)
                n += 3
            ch = lmask[:, CHUNK, :].rearrange("p (n l) -> p n l", l=GLA_CHUNK)
            pool.memset(ch, 1.0).then_inc(sem("c1"), 1)
            pool.wait_ge(*upto("c1", n + 1))
            pool.affine_select(out=ch, in_=ch, compare_op=ALU.is_ge, fill=0.0, base=0,
                               pattern=[[GLA_CHUNK, P // GLA_CHUNK], [1, GLA_CHUNK]],
                               channel_multiplier=-1).then_inc(sem("c1"), 1)
            pool.wait_ge(*upto("c1", n + 2))
            pool.affine_select(out=ch, in_=ch, compare_op=ALU.is_ge, fill=0.0, base=0,
                               pattern=[[-GLA_CHUNK, P // GLA_CHUNK], [0, GLA_CHUNK]],
                               channel_multiplier=1).then_inc(sem("c1"), 1)
            pool.affine_select(out=lmask[:, DIAG, :], in_=lmask[:, DIAG, :],
                               compare_op=ALU.not_equal, fill=1.0, base=0, pattern=[[-1, P]],
                               channel_multiplier=1).then_inc(sem("c1"), 1)
            pool.wait_ge(*upto("crep_ready", KT))
            with pool.Fori(0, KT - 1) as i:
                pool.wait_ge(*upto("ada_done2", i + 1))
                pool.tensor_copy(cnow, crep[:, bass.ds(i * 32 + 32, 32)]
                                 ).then_inc(sem("cnow_ready"), 1)
            pool.wait_ge(*upto("proj1_done0", IN1 // 512))
            pool.wait_ge(*upto("proj1_done1", IN1 // 512))
            for z in (kd[0], qd[0], kd[1], qd[1]):
                pool.memset(z, 0.0).then_inc(sem("lv_zero"), 1)
            pool.wait_ge(*upto("q_ready"))
            pool.memset(S4[:, :], 0.0).then_inc(sem("lv_zero"), 1)
            pool.wait_ge(*upto("vtok_done", 2 * TT))
            pool.memset(wrb[:, :], 0.0).then_inc(sem("bd_zero"), 1)
            pool.memset(wib[:, :], 0.0).then_inc(sem("bd_zero"), 1)
            pool.wait_ge(*upto("vT_done"))
            pool.iota(iot[:, :], pattern=[[1, SLOTS]], base=0, channel_multiplier=0,
                      allow_small_or_imprecise_dtypes=True).then_inc(sem("iotas"), 1)
            pool.iota(iotg[:, :], pattern=[[0, TT], [1, NE]], base=0, channel_multiplier=0,
                      allow_small_or_imprecise_dtypes=True).then_inc(sem("iotas"), 1)
            pool.iota(iotc[:, :], pattern=[[0, TT], [1, NG]], base=0, channel_multiplier=0,
                      allow_small_or_imprecise_dtypes=True).then_inc(sem("iotas"), 1)
            pool.wait_ge(*upto("const", 6))
            pool.wait_ge(*upto("z_out", SB_HEADS))
            for h in range(SB_HEADS):
                pool.tensor_tensor(eb[:, h * 384:(h + 1) * 384], zb[:, h * 384:(h + 1) * 384],
                                   bigm[:, :], ALU.add).then_inc(sem("zm_ready"), 1)
            pool.wait_ge(*upto("sp", 1))
            for h in range(SB_HEADS):
                c = slice(h * 384, (h + 1) * 384)
                pool.tensor_scalar(zb[:, c], zb[:, c], 0.0, None, ALU.max).then_inc(sem("z_pos"), 1)
            pool.wait_ge(*upto("sp", 3))
            for h in range(SB_HEADS):
                c = slice(h * 384, (h + 1) * 384)
                pool.wait_ge(*upto("z_pos", h + 1))
                pool.tensor_tensor(lb_[:, c], zb[:, c], lb_[:, c], ALU.add
                                   ).then_inc(sem("sp_full"), 1)
            for h in range(SB_HEADS):
                c = slice(h * 384, (h + 1) * 384)
                pool.wait_ge(*upto("sp_full", h + 1))
                pool.tensor_tensor(lb_[:, c], lb_[:, c], negm[:, :], ALU.mult
                                   ).then_inc(sem("lm_ready"), 1)

            for name, part, tiles in (("h1_ready", "npost_out", 2), ("h2_ready", "nfpost_out", 2),
                                      ("h3_ready", "ple_ready", 1)):
                for b in range(4):
                    pool.wait_ge(*upto(part, tiles * (b + 1)))
                    pool.tensor_tensor(tile(hT, 2 * b, 2), tile(hT, 2 * b, 2), tile(mixT, 2 * b, 2),
                                       ALU.add).then_inc(sem(name), 1)
            pool.wait_ge(*upto("wout2_done1", 2))
            pool.wait_ge(*upto("mix2_ready", 3))
            pool.memset(xsT[:, :, SLOTS:PADDED], 0.0).then_inc(sem("pad_zero"), 1)
            pool.wait_ge(*upto("pad_zero"))
            pool.wait_ge(*upto("tbl_ready", 2))
            pool.wait_ge(*upto("xs_out", KT))
            pool.wait_ge(*upto("pw_done"))

            def window(start, par, name):
                pool.tensor_copy(xw[par].rearrange("p (k s) -> p k s", k=KT),
                                 xsT[:, :, bass.ds(start, WIN)]
                                 ).then_inc(sem(f"{name}{par}"), 1)

            with pool.Fori(0, NE // 2) as i:
                for par in range(2):
                    start = pool.value_load(tbl[0:1, bass.ds(i * 2 + par, 1)],
                                            min_val=0, max_val=SLOTS)
                    count = pool.value_load(tbl[0:1, bass.ds(i * 2 + (NE + par), 1)],
                                            min_val=0, max_val=T)
                    with pool.If(count > 0):
                        pool.wait_ge(*upto(f"gu_free{par}", i))
                        window(start, par, "xw")
                        with pool.If(count > WIN):
                            pool.wait_ge(*upto(f"gu_done{par}", i + 1))
                            window(start + WIN, par, "bxw")
                            with pool.If(count > 2 * WIN):
                                with pool.Fori(2, NWIN) as w:
                                    with pool.If(count > w * WIN):
                                        pool.wait_ge(*upto(f"bgu_done{par}",
                                                           i * (NWIN - 1) + w - 1))
                                        window(start + w * WIN, par, "bxw")
                                    with pool.Else():
                                        pool.drain().then_inc(sem(f"bxw{par}"), 1)
                            with pool.Else():
                                pool.drain().then_inc(sem(f"bxw{par}"), NWIN - 2)
                        with pool.Else():
                            pool.drain().then_inc(sem(f"bxw{par}"), NWIN - 1)
                    with pool.Else():
                        pool.drain().then_inc(sem(f"xw{par}"), 1)
                        pool.drain().then_inc(sem(f"bxw{par}"), NWIN - 1)

        @block.scalar
        def _(act):
            signal_free(act, "act")
            act.dma_start(x_tok.rearrange("p (t n) -> p t n", t=TT),
                          d["x"][0].rearrange("(t p) n -> p t n", p=P)).then_inc(sem("x_in"), 16)
            for name, n in VROWS[1::2]:
                act.dma_start(vrow[VO[name]:VO[name] + n, :], vector_rows(name)
                              ).then_inc(sem("v_in"), 16)
            act.dma_start(brow[0:6 * KT, :], d["b_ada_2"].rearrange("a (k p) -> (a k) p", p=P)
                          ).then_inc(sem("v_in"), 16)
            act.dma_start(p_tok[:, :].rearrange("p (t n) -> p t n", t=TT),
                          d["p"][0, 0].rearrange("(t p) n -> p t n", p=P)).then_inc(sem("v_in"), 16)

            for b in range(4):
                act.wait_ge(*upto("xT_done", b + 1))
                act.activation(tile(hT, 2 * b, 2), bank[b][:, :], ACT.Copy
                               ).then_inc(sem("hT_ready"), 1)
            act.wait_ge(*upto("c0", 7))
            act_norm(act, "n1", hT, KT, D, lambda b: act.wait_ge(*upto("hT_ready", b + 1)))
            act.wait_ge(*upto("vT_done"))
            act.activation(vec[:, 0:NV], bank[4][:, 0:NV], ACT.Copy).then_inc(sem("vec_ready"), 1)
            act.activation(badaT[:, :], bank[4][:, P:P + 6 * KT], ACT.Copy
                           ).then_inc(sem("vec_ready"), 1)
            act.activation(pT[:, :], bank[5][:, :], ACT.Copy).then_inc(sem("pT_ready"), 1)
            act.wait_ge(*upto("lbd_ready"))
            act.activation(small[:, 4:8], small[:, 0:4], ACT.Sigmoid).then_inc(sem("lb_ready"), 1)
            act.activation(small[:, 8:12], small[:, 0:4], ACT.Sigmoid, scale=-1.0
                           ).then_inc(sem("lb_ready"), 1)
            act.wait_ge(*upto("vec_ready", 2))
            act.activation(small[:, 16:24], vec[:, VO["c_2"]:VO["c_2"] + KT], ACT.Sigmoid
                           ).then_inc(sem("csig_ready"), 1)
            act_first(act, proj1)
            act_source(act, "proj1", uT, SRC_HI, lambda b: act.wait_ge(*upto("n1_out", 2 * b + 2)))
            act_dense(act, proj1, projR)
            act.wait_ge(*upto("proj1_out0", IN1 // 512))
            act.wait_ge(*upto("proj1_out1", IN1 // 512))
            act.activation(T4[:, :], tile(projR, 4, 4), ACT.Sigmoid).then_inc(sem("hg_sig"), 1)
            act.activation(S4[:, :], tile(projR, 0, 4), ACT.Sigmoid).then_inc(sem("hg_sig"), 1)
            act.wait_ge(*upto("f_ready", 4))
            act.activation(tile(projR, 4, 4), tile(projR, 4, 4), ACT.Sigmoid, scale=-1.0
                           ).then_inc(sem("hg_sig"), 1)
            act.activation(G4[:, :], tile(projR, 12, 4), ACT.Sigmoid).then_inc(sem("hg_sig"), 1)
            act.activation(T4[:, :], T4[:, :], ACT.Ln).then_inc(sem("g_ready"), 1)
            for n, dst in enumerate((V4, SV4)):
                for t in range(TT):
                    act.wait_ge(*upto("vtok_done", n * TT + t + 1))
                    act.activation(dst[:, t * HW:(t + 1) * HW], bank[2 + t][:, :], ACT.Copy
                                   ).then_inc(sem("vtok_ready"), 1)
            for h in range(SB_HEADS):
                act.wait_ge(*upto("z_done", h + 1))
                act.activation(zb[:, h * 384:(h + 1) * 384], bank[h % 4][:, 0:384], ACT.Copy,
                               scale=SCALE_SB).then_inc(sem("z_out"), 1)
            for li in range(len(ALL_LEVELS)):
                act.wait_ge(*upto("d_ready", 2 * li + 2))
                act.activation(ed[li % 2], ed[li % 2], ACT.Exp).then_inc(sem("e_ready"), 1)
                if li == 1:
                    act.wait_ge(*upto("z_out", SB_HEADS))
                    act.activation(lb_, zb, ACT.Abs).then_inc(sem("sp"), 1)
                elif li == 2:
                    act.wait_ge(*upto("sp", 1))
                    act.activation(lb_, lb_, ACT.Exp, scale=-1.0).then_inc(sem("sp"), 1)
                elif li == 3:
                    act.wait_ge(*upto("sp", 2))
                    act.activation(lb_, lb_, ACT.Ln, bias=1.0).then_inc(sem("sp"), 1)
                elif li - 4 in range(ADA_B):
                    act.wait_ge(*upto(f"ada_done{li - 4}", KT))
                    act.activation(mod_row(li - 4), bank[li][:, :], ACT.Copy
                                   ).then_inc(sem("ada_row"), 1)
            act.wait_ge(*upto("ada_done1", KT))
            act_first(act, wout1)
            for h in range(SB_HEADS):
                act.wait_ge(*upto("sx_ready", h + 1))
                act.activation(zb[:, h * 384:(h + 1) * 384], zb[:, h * 384:(h + 1) * 384], ACT.Exp
                               ).then_inc(sem("a_ready"), 1)
            for b in range(2):
                act.wait_ge(*upto("ohg_done", b + 1))
                act.activation(tile(mixin, 2 * b, 2), bank[b][:, :], ACT.Copy
                               ).then_inc(sem("ohg_out"), 1)
            act_norm(act, "nhg", mixin, HT, HW, lambda b: act.wait_ge(*upto("ohg_out", b + 1)))
            for b in range(2):
                act.wait_ge(*upto("osb_done", b + 1))
                act.activation(tile(mixin, HT + 2 * b, 2), bank[2 + b][:, :], ACT.Copy
                               ).then_inc(sem("osb_out"), 1)
            act_norm(act, "nsb", mixin[:, HT * T:2 * HT * T], HT, HW,
                     lambda b: act.wait_ge(*upto("osb_out", b + 1)))

            def mixer_ready(b):
                if b < 2:
                    act.wait_ge(*upto("ohg_ready"))
                else:
                    act.wait_ge(*upto("nsb_out", 2 * b - 2))

            act_source(act, "wout1", mixin, SRC_LO, mixer_ready)
            act_dense(act, wout1, mixT)
            act.wait_ge(*upto("wout1_out0", 2))
            act.wait_ge(*upto("wout1_out1", 2))
            act_norm(act, "npost", mixT, KT, D,
                     lambda b: act.wait_ge(*upto(f"wout1_out{b % 2}", b // 2 + 1)))
            act.wait_ge(*upto("gate_full", 16))
            act.activation(slot_r[6], slot[0], ACT.Copy).then_inc(sem("gate_hi"), 1)
            act.wait_ge(*upto("up_full", 16))
            act.activation(slot_r[8], slot[1], ACT.Copy).then_inc(sem("up_hi"), 1)
            act_norm(act, "nffn", hT, KT, D, lambda b: act.wait_ge(*upto("h1_ready", b + 1)))

            act.wait_ge(*upto("wout1_out1", 2))
            act_source(act, "ffn", uT, SRC_HI, lambda b: act.wait_ge(*upto("nffn_out", 2 * b + 2)))

            def ffn_parts(i, last):
                act.wait_ge(*upto("gate_done", i + 1))
                act.wait_ge(*upto("hid_ready", i))
                act.activation(S4[:, 0:512], bank[0][:, :], ACT.Silu).then_inc(sem("silu_ready"), 1)
                if not last:
                    act.wait_ge(*upto("gate_full", i * 16 + 32))
                    act.activation(slot_r[6], slot[0], ACT.Copy).then_inc(sem("gate_hi"), 1)
                act.wait_ge(*upto("down_full", i * 16 + 16))
                act.wait_ge(*upto("down_done", i))
                act.activation(slot_r[10], slot[4], ACT.Copy).then_inc(sem("down_hi"), 1)
                act.wait_ge(*upto("hid_ready", i + 1))
                act.activation(T4_r[:, 0:512], S4[:, 512:1024], ACT.Copy).then_inc(sem("hid_hi"), 1)
                if not last:
                    act.wait_ge(*upto("up_full", i * 16 + 32))
                    act.wait_ge(*upto("up_done", i + 1))
                    act.activation(slot_r[8], slot[1], ACT.Copy).then_inc(sem("up_hi"), 1)

            with act.Fori(0, NF - 1) as i:
                ffn_parts(i, False)
            ffn_parts(NF - 1, True)
            for b in range(4):
                act.wait_ge(*upto("y_done"))
                act.activation(tile(mixT, 2 * b, 2), bank[2 + b][:, :], ACT.Copy
                               ).then_inc(sem("y_out"), 1)
            act_norm(act, "nfpost", mixT, KT, D, lambda b: act.wait_ge(*upto("y_out", b + 1)),
                     pgate)
            for b in range(4):
                act.wait_ge(*upto("pp_done", b + 1))
                act.activation(tile(xk, 2 * b, 2), bank[(0, 1, 4, 5)[b]][:, :], ACT.Copy
                               ).then_inc(sem("pp_out"), 1)
            act_source(act, "pgate", hT, SRC_LO, lambda b: act.wait_ge(*upto("h2_ready", b + 1)))
            act.wait_ge(*upto("vec_ready", 2))
            lam = vec[:, VO["lru_lambda_2"]:VO["lru_lambda_2"] + HT]
            act.activation(lru[:, 0:HT], lam, ACT.Abs).then_inc(sem("lam"), 1)
            act.wait_ge(*upto("lam", 1))
            act.activation(lru[:, 0:HT], lru[:, 0:HT], ACT.Exp, scale=-1.0).then_inc(sem("lam"), 1)
            act.wait_ge(*upto("lam", 2))
            act.activation(lru[:, 0:HT], lru[:, 0:HT], ACT.Ln, bias=1.0).then_inc(sem("lam"), 1)
            act_dense(act, pgate, mixT, ACT.Sigmoid)

            def shift(name, mod_tile):
                for k in range(KT):
                    act.wait_ge(*upto(f"{name}_out", k + 1))
                    act.activation(tile(uT, k), tile(uT, k), ACT.Identity,
                                   bias=modT[:, mod_tile + k:mod_tile + k + 1]
                                   ).then_inc(sem(f"{name}_shift"), 1)

            act_first(act, proj2)
            act_norm(act, "nmix2", hT, KT, D, lambda b: act.wait_ge(*upto("h3_ready", b + 1)))
            shift("nmix2", 0)
            act_source(act, "proj2", uT, SRC_HI,
                       lambda b: act.wait_ge(*upto("nmix2_shift", 2 * b + 2)))
            act_dense(act, proj2, projR)
            act.wait_ge(*upto("glr_done"))
            act.activation(glr[:, :], bank[4][0:GATE_RANK, 0:T], ACT.Copy).then_inc(sem("glr_out"), 1)
            act.wait_ge(*upto("proj2_out0", IN2_FULL // 512))
            act.wait_ge(*upto("proj2_out1", IN2_FULL // 512))
            for t in range(TT):
                act.wait_ge(*upto("gv_done", t + 1))
                act.activation(GV[:, t * HW:(t + 1) * HW], bank[5 + t][:, :], ACT.Copy
                               ).then_inc(sem("gv_out"), 1)
            act.wait_ge(*upto("ga_done"))
            for k in range(GLA_QT):
                act.activation(lsx[:, k * T:(k + 1) * T], bank[4][:, k * T:(k + 1) * T], ACT.Identity,
                               bias=v("gla_ba_2", k)).then_inc(sem("ga"), 1)
            act.wait_ge(*upto("ga", 2))
            act.activation(lsx[:, 512:1024], lsx[:, 0:512], ACT.Abs).then_inc(sem("ga"), 1)
            act.wait_ge(*upto("ga", 3))
            act.activation(lsx[:, 512:1024], lsx[:, 512:1024], ACT.Exp, scale=-1.0
                           ).then_inc(sem("ga"), 1)
            act.wait_ge(*upto("ga", 4))
            act.activation(lsx[:, 512:1024], lsx[:, 512:1024], ACT.Ln, bias=1.0
                           ).then_inc(sem("ga"), 1)
            IG = 1.0 / GATE_NORM
            act.wait_ge(*upto("b64_ready", 8))
            act.activation(e2[0], b64, ACT.Exp, scale=IG).then_inc(sem("ge_ready"), 1)
            act.activation(e2[1], b64, ACT.Exp, scale=-IG).then_inc(sem("ge_ready"), 1)
            for n in range(2):
                act.wait_ge(*upto("gd_ready", 2 * n + 2))
                act.activation(e2[n], e2[n], ACT.Exp, scale=IG).then_inc(sem("ge_ready"), 1)
            for n, (b0, dst, bias) in enumerate(((0, T4, "lru_br_2"), (2, G4, "lru_bi_2"))):
                act.wait_ge(*upto("lgate_done", n + 1))
                for k in range(HT):
                    act.activation(tile(dst, k), bank[b0 + k // 2][:, (k % 2) * T:(k % 2 + 1) * T],
                                   ACT.Sigmoid, bias=v(bias, k)).then_inc(sem("lgate_out"), 1)
            act.wait_ge(*upto("la_ready", HT))
            act.activation(A8, T4[:, :], ACT.Exp).then_inc(sem("lru_a"), 1)
            act.activation(th, T4[:, :], ACT.Tanh, scale=-1.0).then_inc(sem("lru_th"), 1)
            act.wait_ge(*upto("gelu_in"))
            act.activation(gel, gel, ACT.Tanh, scale=SQRT_2_OVER_PI).then_inc(sem("gelu_tanh"), 1)
            act.wait_ge(*upto("lru_m"))
            act.activation(th, th, ACT.Sqrt).then_inc(sem("lru_root"), 1)
            act.activation(tile(projR, 16, 4), tile(projR, 16, 4), ACT.Silu
                           ).then_inc(sem("gout_ready"), 1)
            for b in range(2):
                act.wait_ge(*upto("og_done", b + 1))
                if b == 0:
                    act.wait_ge(*upto("gi_ready"))
                act.activation(tile(XC, 2 * b, 2), bank[b][:, :], ACT.Copy).then_inc(sem("og_out"), 1)
            for b in range(2):
                act.wait_ge(*upto("og_out", b + 1))
                act.activation(tile(sq, 2 * b, 2), tile(XC, 2 * b, 2), ACT.Square
                               ).then_inc(sem("og_sq"), 1)
            act_first(act, wout2)
            for b in range(2):
                act.wait_ge(*upto("og_ss", b + 1))
                act.activation(rms[:, b * 512:(b + 1) * 512], bank[2 + b][:, :], ACT.Sqrt,
                               bias=epsc[:, :], scale=1.0 / P).then_inc(sem("og_rms"), 1)
            act_source(act, "wout2", mixin, SRC_LO,
                       lambda b: act.wait_ge(*upto("mix2_ready", max(1, b))))
            act_dense(act, wout2, mixT2)
            act_norm(act, "nffn2", hT, KT, D, lambda b: act.wait_ge(*upto("x2_ready", 2 * b + 2)))
            shift("nffn2", 3 * KT)
            act.wait_ge(*upto("lgt_done"))
            act.activation(lgT, bank[0][0:NL, 0:T], ACT.Copy).then_inc(sem("lgt_out"), 1)
            act.wait_ge(*upto("cs_ready"))
            act.activation(rt[:, 0:TT * NG], rt[:, 0:TT * NG], ACT.Exp).then_inc(sem("ec_ready"), 1)
            for b in range(4):
                act.wait_ge(*upto("tok_done", b + 1))
                act.activation(h2_hi[:, b * 512:(b + 1) * 512], bank[4 + b][:, :], ACT.Copy
                               ).then_inc(sem("h2tok"), 1)
            act.wait_ge(*upto("dm_ready"))
            act.activation(rs[:, 8:8 + TT], rs[:, 8:8 + TT], ACT.Exp).then_inc(sem("e21_ready"), 1)
            for b in range(4):
                act.wait_ge(*upto("xtok_done", b + 1))
                act.activation(x2tok[:, b * 512:(b + 1) * 512], bank[4 + b][:, :], ACT.Copy
                               ).then_inc(sem("x2tok"), 1)
            for k in range(KT):
                act.wait_ge(*upto("xs_done", k + 1))
                act.activation(xsT[:, k, 0:SLOTS], bank[k % 4][:, :], ACT.Copy
                               ).then_inc(sem("xs_out"), 1)
            for b in range(2):
                act.wait_ge(*upto("pwt_done", b + 1))
                act.activation(PwT[:, 2 * b:2 * b + 2, :],
                               bank[4 + b][:, :].rearrange("p (c t) -> p c t", t=T), ACT.Copy
                               ).then_inc(sem("pwt_out"), 1)

            def window(par, name, count):
                act.wait_ge(*upto(f"{name}gu_done{par}", count))
                act.activation(sil, bank[par][0:2 * WIN, 0:256], ACT.Silu).then_inc(sem(f"{name}sil{par}"), 1)
                act.wait_ge(*upto(f"{name}ht_done{par}", count))
                act.activation(hidT.rearrange("p (c s) -> p c s", c=2),
                               bank[2 + par][:, 0:2 * P].rearrange("p (c s) -> p c s", c=2)
                               [:, :, 2 * WIN:P], ACT.Copy
                               ).then_inc(sem(f"{name}ht_out{par}"), 1)
                act.wait_ge(*upto(f"{name}y_done{par}", count))
                act.activation(yb, bank[4 + par][:, 0:256], ACT.Copy).then_inc(sem(f"{name}y_out{par}"), 1)

            with act.Fori(0, NE // 2) as i:
                for par in range(2):
                    count = act.value_load(tbl[0:1, bass.ds(i * 2 + (NE + par), 1)],
                                           min_val=0, max_val=T)
                    with act.If(count > 0):
                        window(par, "", i + 1)
                        with act.If(count > WIN):
                            window(par, "b", i * (NWIN - 1) + 1)
                            with act.If(count > 2 * WIN):
                                with act.Fori(2, NWIN) as w:
                                    with act.If(count > w * WIN):
                                        window(par, "b", i * (NWIN - 1) + w)
                                    with act.Else():
                                        for name in ("sil", "ht_out", "y_out"):
                                            act.drain().then_inc(sem(f"b{name}{par}"), 1)
                            with act.Else():
                                for name in ("sil", "ht_out", "y_out"):
                                    act.drain().then_inc(sem(f"b{name}{par}"), NWIN - 2)
                        with act.Else():
                            for name in ("sil", "ht_out", "y_out"):
                                act.drain().then_inc(sem(f"b{name}{par}"), NWIN - 1)
                    with act.Else():
                        for name in ("sil", "ht_out", "y_out"):
                            act.drain().then_inc(sem(f"{name}{par}"), 1)
                            act.drain().then_inc(sem(f"b{name}{par}"), NWIN - 1)
            for n in range(8):
                act.wait_ge(*upto("yt_done", n + 1))
                act.activation(ystok[:, n * 512:(n + 1) * 512], bank[n][:, :], ACT.Copy
                               ).then_inc(sem("yt_out"), 1)
            for t in range(TT):
                act.wait_ge(*upto("x3_ready", t * 2 + 2))
                act.activation(R24[:, t * D:(t + 1) * D], x2tok[:, t * D:(t + 1) * D], ACT.Square,
                               accum_out=rs[:, 20 + t:21 + t]).then_inc(sem("fin_ss"), 1)
                act.wait_ge(*upto("fin_ss", t + 1))
                act.activation(rs[:, 22 + t:23 + t], rs[:, 20 + t:21 + t], ACT.Sqrt, bias=epsc[:, :],
                               scale=1.0 / D).then_inc(sem("fin_rms"), 1)

        @block.tensor
        def _(pe):
            signal_free(pe, "pe")
            pe.wait_ge(*upto("ident_set"))
            pe.wait_ge(*upto("x_in", 16))
            for b in range(4):
                for k in range(2):
                    for t in range(TT):
                        mm = pe.transpose(bank[b][:, k * T + t * P:k * T + (t + 1) * P],
                                          x_tok[:, t * D + (2 * b + k) * P:t * D + (2 * b + k + 1) * P],
                                          ident[:, :])
                mm.then_inc(sem("xT_done"), 1)
            pe.wait_ge(*upto("ones_set"))
            pe_norm(pe, "n1", KT)
            pe.wait_ge(*upto("v_in", 16 * (len(VROWS) + 2)))
            pe.transpose(bank[4][:, 0:NV], vrow[0:NV, :], ident[0:NV, 0:NV])
            pe.transpose(bank[4][:, P:P + 6 * KT], brow[0:6 * KT, :], ident[0:6 * KT, 0:6 * KT])
            for k in range(PLE // P):
                for t in range(TT):
                    mm = pe.transpose(bank[5][:, k * T + t * P:k * T + (t + 1) * P],
                                      p_tok[:, t * PLE + k * P:t * PLE + (k + 1) * P], ident[:, :])
            mm.then_inc(sem("vT_done"), 1)

            def ada(n, par, b, c, first, last):
                pe.wait_ge(*upto(f"ada_full{b}{par}", n * 16 + 16))
                for j in range(4):
                    mm = pe.matmul(bank[4 + b][32 * j:32 * j + 32, :],
                                   c, slot[ADA_SLOTS[par][b]][:, j * 512:(j + 1) * 512],
                                   start=first, stop=last, skip_group_check=True)
                mm.then_inc(sem(f"ada_done{b}"), 1)

            pe.wait_ge(*upto("crep_ready", KT))
            pe.wait_ge(*upto("pT_ready"))
            for b in range(ADA_B):
                ada(0, 0, b, crep[:, 0:32], True, False)
            pe.wait_ge(*upto("proj1_src_lo", 4))

            def proj1_round(r, n, par, last):
                for j in range(2):
                    pe.wait_ge(*upto(f"proj1_lo{j}", r * 2 + 2))
                    pe.wait_ge(*upto(f"proj1_out{j}", r))
                    pe_chunk(pe, bank[j], proj1[4][2 * j:2 * j + 2], SRC_HI, f"proj1_done{j}")
                    for b in ADA_AFTER[j]:
                        if b == 0:
                            pe.wait_ge(*upto("cnow_ready", r + 1))
                        ada(n, par, b, cnow, False, last)

            proj1_round(0, 0, 1, False)
            with pe.Fori(1, KT // 2 - 1) as n:
                for par in range(2):
                    proj1_round(n * 2 + (par - 1), n, par, False)
            for par in range(2):
                proj1_round(KT - 3 + par, KT // 2 - 1, par, par == 1)
            pe.wait_ge(*upto("proj1_out0", IN1 // 512))
            pe.wait_ge(*upto("proj1_out1", IN1 // 512))
            for n, first in enumerate((8, 24)):
                for t in range(TT):
                    if n:
                        pe.wait_ge(*upto("vtok_ready", t + 1))
                    for c in range(4):
                        mm = pe.transpose(bank[2 + t][:, c * P:(c + 1) * P],
                                          half(projR, first + c, t), ident[:, :])
                    mm.then_inc(sem("vtok_done"), 1)
            pe.wait_ge(*upto("vtok_ready", 2 * TT))
            for h in range(SB_HEADS):
                if h >= 4:
                    pe.wait_ge(*upto("z_out", h - 3))
                r = slice((h % 2) * 64, (h % 2) * 64 + 64)
                q, k = tile(projR, 16 + h // 2)[r, :], tile(projR, 20 + h // 2)[r, :]
                pe.matmul(bank[h % 4][:, 0:256], k[:, 0:P], q[:, 0:T], start=True, stop=True)
                pe.matmul(bank[h % 4][:, 256:384], k[:, P:T], q[:, P:T], start=True, stop=True
                          ).then_inc(sem("z_done"), 1)
            pe.wait_ge(*upto("z_out", SB_HEADS))
            for li, L in enumerate(ALL_LEVELS):
                pe.wait_ge(*upto("qk_ready", 2 * li + 2))
                if li >= 2:
                    pe.wait_ge(*upto("lv_out", 2 * (li - 1)))
                for h in range(HG_HEADS):
                    b = bank[2 * (li % 2) + h // 2]
                    for t in range(TT):
                        if L == P and t:
                            continue
                        kt, qt = (0, 1) if L == P else (t, t)
                        mm = pe.matmul(b[:, (h % 2) * T + t * P:(h % 2) * T + (t + 1) * P],
                                       kd[li % 2][:, h * T + kt * P:h * T + (kt + 1) * P],
                                       qd[li % 2][:, h * T + qt * P:h * T + (qt + 1) * P],
                                       start=True, stop=True)
                mm.then_inc(sem("lv_done"), 1)
            pe.wait_ge(*upto("k_ready", 4))
            pe.wait_ge(*upto("q_ready"))
            pe.wait_ge(*upto("lv_out", 2 * (len(ALL_LEVELS) - 1)))
            for h in range(HG_HEADS):
                for t in range(TT):
                    mm = pe.matmul(bank[h // 2][:, (h % 2) * T + t * P:(h % 2) * T + (t + 1) * P],
                                   half(projR, 4 + h, t), half(projR, h, t), start=True, stop=True)
            mm.then_inc(sem("lv_done"), 1)
            for b in range(ADA_B):
                pe.wait_ge(*upto("ada_row", b + 1))
                for c in range(4):
                    mm = pe.transpose(bank[4 + b][:, c * P:(c + 1) * P],
                                      mod_row(b)[:, c * P:(c + 1) * P], ident[:, :])
                mm.then_inc(sem("mod_done"), 1)
            pe.wait_ge(*upto("const", 6))
            pe.wait_ge(*upto("mod_ready", ADA_B))
            for h in range(SB_HEADS):
                pe.wait_ge(*upto("lm_ready", h + 1))
                if h >= 2:
                    pe.wait_ge(*upto("sx_ready", h - 1))
                b = bank[4 + h % 2]
                lm = lb_[:, h * 384:(h + 1) * 384]
                pe.matmul(b[:, 0:P], tri_ge[:, :], lm[:, 0:P], start=True, stop=True)
                pe.matmul(b[:, P:T], ones[:, 0:P], lm[:, T:T + P], start=True, stop=False)
                pe.matmul(b[:, P:T], tri_ge[:, :], lm[:, P:T], start=False, stop=True)
                pe.matmul(b[:, T:T + P], tri_ge[:, :], lm[:, T:T + P], start=True, stop=True
                          ).then_inc(sem("sx_done"), 1)
            pe.wait_ge(*upto("lv_out", 2 * (len(ALL_LEVELS) + 1)))
            pe.wait_ge(*upto("vtok_ready", 2 * TT))
            for h in range(HG_HEADS):
                o = bank[h // 2][:, (h % 2) * T:(h % 2 + 1) * T]
                v0, v1 = (V4[:, t * HW + h * P:t * HW + (h + 1) * P] for t in range(TT))
                pe.matmul(o[:, 0:P], v0, half(S4, h, 0), start=True, stop=True)
                pe.matmul(o[:, P:T], v0, SX2[:, h * P:(h + 1) * P], start=True, stop=False)
                mm = pe.matmul(o[:, P:T], v1, half(S4, h, 1), start=False, stop=True)
                if h % 2:
                    mm.then_inc(sem("ohg_done"), 1)
            for h in range(SB_HEADS):
                pe.wait_ge(*upto("a_ready", h + 1))
                a = zb[:, h * 384:(h + 1) * 384]
                r = (h % 2) * 64
                o = bank[2 + h // 4][r:r + 64, (h // 2 % 2) * T:(h // 2 % 2 + 1) * T]
                v0, v1 = (SV4[:, t * HW + h * 64:t * HW + (h + 1) * 64] for t in range(TT))
                pe.matmul(o[:, 0:P], v0, a[:, 0:P], start=True, stop=True)
                pe.matmul(o[:, P:T], v0, a[:, P:T], start=True, stop=False)
                mm = pe.matmul(o[:, P:T], v1, a[:, T:T + P], start=False, stop=True)
                if h % 4 == 3:
                    mm.then_inc(sem("osb_done"), 1)
            pe_norm(pe, "nhg", HT)
            pe_norm(pe, "nsb", HT)
            pe_dense(pe, wout1)
            pe_norm(pe, "npost", KT)
            pe_norm(pe, "nffn", KT)
            pe.wait_ge(*upto("ffn_src_lo", 4))

            def gate(i):
                pe.wait_ge(*upto("gate_lo", i + 1))
                pe.wait_ge(*upto("silu_ready", i))
                pe_chunk(pe, bank[0], (6, 7), SRC_HI, "gate_done")

            def up(i):
                pe.wait_ge(*upto("up_lo", i + 1))
                pe.wait_ge(*upto("hid_ready", i))
                pe_chunk(pe, bank[1], (8, 9), SRC_HI, "up_done")

            def down(i, first, last):
                pe.wait_ge(*upto("down_lo", i + 1))
                pe.wait_ge(*upto("hid_lo", i + 1))
                for k in range(2):
                    x_hi, x_lo = T4_r[:, k * T:(k + 1) * T], T4_r[:, 512 + k * T:512 + (k + 1) * T]
                    for m in range(KT):
                        o = bank[2 + m // 2][:, (m % 2) * T:(m % 2 + 1) * T]
                        c = slice(k * D + m * P, k * D + (m + 1) * P)
                        pe.matmul(o, slot_r[10][:, c], x_hi,
                                  start=(first and k == 0 and m % 2 == 0), stop=False,
                                  skip_group_check=True)
                        pe.matmul(o, slot_r[10][:, c], x_lo, start=False, stop=False,
                                  skip_group_check=True)
                        mm = pe.matmul(o, slot_r[11][:, c], x_hi, start=False,
                                       stop=(last and k == 1), skip_group_check=True)
                mm.then_inc(sem("down_done"), 1)

            pe.wait_ge(*upto("wout1_out0", 2))
            pe.wait_ge(*upto("wout1_out1", 2))
            gate(0)
            up(0)
            gate(1)
            down(0, True, False)
            up(1)
            with pe.Fori(1, NF - 1) as i:
                gate(i + 1)
                down(i, False, False)
                up(i + 1)
            down(NF - 1, False, True)
            pe.drain().then_inc(sem("y_done"), 1)
            pe_norm(pe, "nfpost", KT)
            pe.wait_ge(*upto("pproj_full", 16))
            pe.wait_ge(*upto("pT_ready"))
            pe.wait_ge(*upto("hid_ready", NF))
            for b in range(4):
                for m in range(2):
                    for k in range(PLE // P):
                        mm = pe.matmul(bank[(0, 1, 4, 5)[b]][:, m * T:(m + 1) * T],
                                       slot[5][:, k * D + (2 * b + m) * P:k * D + (2 * b + m + 1) * P],
                                       tile(pT, k), start=(k == 0), stop=(k == PLE // P - 1))
                mm.then_inc(sem("pp_done"), 1)
            pe_dense(pe, pgate)

            pe_norm(pe, "nmix2", KT)
            pe.wait_ge(*upto("nmix2_shift", KT))
            pe.wait_ge(*upto("pp_out", 4))
            pe_dense(pe, proj2)
            pe.wait_ge(*upto("sw_in", 16 * 10))
            for k in range(KT):
                mm = pe.matmul(bank[4][0:GATE_RANK, 0:T], wlr[:, k * GATE_RANK:(k + 1) * GATE_RANK],
                               tile(uT, k), start=(k == 0), stop=(k == KT - 1))
            mm.then_inc(sem("glr_done"), 1)
            pe.wait_ge(*upto("proj2_out0", IN2_FULL // 512))
            pe.wait_ge(*upto("proj2_out1", IN2_FULL // 512))
            for t in range(TT):
                for c in range(4):
                    mm = pe.transpose(bank[5 + t][:, c * P:(c + 1) * P], half(projR, 12 + c, t),
                                      ident[:, :])
                mm.then_inc(sem("gv_done"), 1)
            pe.wait_ge(*upto("glr_out"))
            for k in range(GLA_QT):
                mm = pe.matmul(bank[4][:, k * T:(k + 1) * T], wa2[:, k * P:(k + 1) * P], glr[:, :],
                               start=True, stop=True)
            mm.then_inc(sem("ga_done"), 1)
            pe.wait_ge(*upto("conv", 4 * HT))
            for b0, w in ((0, wrb), (2, wib)):
                for k in range(HT):
                    mm = pe.matmul(bank[b0 + k // 2][:, (k % 2) * T:(k % 2 + 1) * T],
                                   w[:, k * P:(k + 1) * P], tile(XC, k), start=True, stop=True)
                mm.then_inc(sem("lgate_done"), 1)
            for n, L in enumerate((0, 64, P)):
                pe.wait_ge(*upto("gqk_ready", 2 * n + 2))
                if n >= 1:
                    pe.wait_ge(*upto("gl_out", 2 * n))
                for h in range(GLA_HEADS):
                    r = slice((h % 2) * 64, (h % 2) * 64 + 64)
                    for t in range(TT):
                        if L == P and t:
                            continue
                        kt, qt = (0, 1) if L == P else (t, t)
                        at = (h // 2) * T
                        mm = pe.matmul(bank[6 + h % 2][:, at + t * P:at + (t + 1) * P],
                                       k2[n % 2][r, at + kt * P:at + (kt + 1) * P],
                                       q2[n % 2][r, at + qt * P:at + (qt + 1) * P],
                                       start=True, stop=True)
                    if h >= GLA_HEADS - 2:
                        mm.then_inc(sem("gl_done"), 1)
            pe.wait_ge(*upto("gl_out", 6))
            pe.wait_ge(*upto("gv_out", TT))
            pe.wait_ge(*upto("lgate_out", 2 * HT))
            for h in range(GLA_HEADS):
                o = bank[h // 2][:, (h % 2) * T:(h % 2 + 1) * T]
                v0, v1 = (GV[:, t * HW + h * P:t * HW + (h + 1) * P] for t in range(TT))
                at = (h % 2) * 512 + (h // 2) * T
                pe.matmul(o[:, 0:P], v0, S4[:, at:at + P], start=True, stop=True)
                xat = (h % 2) * T + (h // 2) * P
                pe.matmul(o[:, P:T], v0, SX2[:, xat:xat + P], start=True, stop=False)
                mm = pe.matmul(o[:, P:T], v1, S4[:, at + P:at + T], start=False, stop=True)
                if h % 2:
                    mm.then_inc(sem("og_done"), 1)
            for h in range(GLA_HEADS):
                if h % 2 == 0:
                    pe.wait_ge(*upto("og_sq", h // 2 + 1))
                mm = pe.matmul(bank[2 + h // 2][:, (h % 2) * T:(h % 2 + 1) * T], ones[:, 0:P],
                               tile(sq, h), start=True, stop=True)
                if h % 2:
                    mm.then_inc(sem("og_ss"), 1)
            pe.wait_ge(*upto("og_rms", 2))
            pe_dense(pe, wout2)
            pe_norm(pe, "nffn2", KT)
            for k in range(KT):
                pe.wait_ge(*upto("nffn2_shift", k + 1))
                pe.matmul(bank[0][0:NL, 0:T], wcf[:, k * NL:(k + 1) * NL], tile(uT, k),
                          start=(k == 0), stop=False)
            pe.matmul(bank[0][0:NL, 0:T], bcf[:, :], ones[0:1, 0:T], start=False, stop=True
                      ).then_inc(sem("lgt_done"), 1)
            pe.wait_ge(*upto("lgt_out"))
            for t in range(TT):
                mm = pe.transpose(bank[1][:, t * 64:t * 64 + NL], lgT[:, t * P:(t + 1) * P],
                                  ident[0:NL, 0:NL])
            mm.then_inc(sem("lg_done"), 1)
            for b in range(4):
                for c in range(4):
                    mm = pe.transpose(bank[4 + b][:, c * P:(c + 1) * P],
                                      half(uT, (b % 2) * 4 + c, b // 2), ident[:, :])
                mm.then_inc(sem("tok_done"), 1)
            pe.wait_ge(*upto("a_set"))
            A0, A1 = rt[:, TA:TA + NE], rt[:, TA + NE:TA + 2 * NE]
            pe.matmul(bank[1][:, 0:NE], tri_lt[:, :], A0, start=True, stop=True)
            pe.matmul(bank[1][:, NE:2 * NE], ones[:, 0:P], A0, start=True, stop=False)
            pe.matmul(bank[1][:, NE:2 * NE], tri_lt[:, :], A1, start=False, stop=True)
            pe.matmul(bank[1][:, 2 * NE:3 * NE], ones[:, 0:P], A0, start=True, stop=False)
            pe.matmul(bank[1][:, 2 * NE:3 * NE], ones[:, 0:P], A1, start=False, stop=True
                      ).then_inc(sem("rank_done"), 1)
            for b in range(4):
                pe.wait_ge(*upto("h2lo", b + 1))
                for c in range(4):
                    mm = pe.transpose(bank[4 + b][:, c * P:(c + 1) * P],
                                      half(hT, (b % 2) * 4 + c, b // 2), ident[:, :])
                mm.then_inc(sem("xtok_done"), 1)
            pe.wait_ge(*upto("psel_ready", TT))
            for k in range(KT):
                if k >= 4:
                    pe.wait_ge(*upto("xs_out", k - 3))
                for t in range(TT):
                    c = slice(t * D + k * P, t * D + (k + 1) * P)
                    pe.matmul(bank[k % 4][:, :], h2_hi[:, c], Psel_r[:, t, :], start=(t == 0),
                              stop=False)
                    mm = pe.matmul(bank[k % 4][:, :], h2_lo[:, c], Psel_r[:, t, :], start=False,
                                   stop=(t == TT - 1))
                mm.then_inc(sem("xs_done"), 1)
            pe.wait_ge(*upto("pw_ready", TT))
            pe.wait_ge(*upto("x2tok", 4))
            for c in range(SLOTS // P):
                for t in range(TT):
                    mm = pe.transpose(bank[4 + c // 2][:, (c % 2) * T + t * P:(c % 2) * T + (t + 1) * P],
                                      Pw[:, t, c * P:(c + 1) * P], ident[:, :])
                if c % 2:
                    mm.then_inc(sem("pwt_done"), 1)
            pe.drain().then_inc(sem("pw_done"), 1)
            pe.wait_ge(*upto("xs_out", KT))
            pe.wait_ge(*upto("pwt_out", 2))

            def release(name, left):
                if left is None:
                    pe.drain().then_inc(sem(name), 1)
                else:
                    with pe.If(left <= WIN):
                        pe.drain().then_inc(sem(name), 1)

            def window(par, name, count, left=None):
                pe.wait_ge(*upto(f"{name}xw{par}", count))
                W = Wx[par]
                for first, full, g0 in ((WG, "wg", 0), (WU, "wu", 2)):
                    if not name:
                        pe.wait_ge(*upto(f"{full}_full{par}", count * 16))
                    for k in range(KT):
                        for h in range(2):
                            g = g0 + h
                            mm = pe.matmul(bank[par][g * WIN:(g + 1) * WIN, 0:256],
                                           xw[par][:, k * WIN:(k + 1) * WIN],
                                           W[:, first + k * DE + h * 256:first + k * DE + h * 256 + 256],
                                           start=(k == 0), stop=(k == KT - 1))
                mm.then_inc(sem(f"{name}gu_done{par}"), 1)
                release(f"gu_free{par}", left)
                pe.wait_ge(*upto(f"{name}hid{par}", count))
                for c in range(2):
                    mm = pe.transpose(bank[2 + par][:, c * P:(c + 1) * P],
                                      hidw[:, c * P:(c + 1) * P], ident[:, :])
                mm.then_inc(sem(f"{name}ht_done{par}"), 1)
                pe.wait_ge(*upto(f"{name}ht_out{par}", count))
                if not name:
                    pe.wait_ge(*upto(f"wd_full{par}", count * 16))
                for f in range(DE // P):
                    at = (f % 2) * 2 * WIN + (f // 2) * WIN
                    for g in range(4):
                        mm = pe.matmul(bank[4 + par][g * WIN:(g + 1) * WIN, 0:256],
                                       hidT[:, at:at + WIN],
                                       W[:, WD + f * D + g * 256:WD + f * D + (g + 1) * 256],
                                       start=(f == 0), stop=(f == DE // P - 1))
                mm.then_inc(sem(f"{name}y_done{par}"), 1)
                release(f"d_free{par}", left)
                pe.wait_ge(*upto(f"{name}y_out{par}", count))
                for c in range(2):
                    mm = pe.transpose(bank[6 + par][:, c * P:(c + 1) * P], yb[:, c * P:(c + 1) * P],
                                      ident[:, :])
                mm.then_inc(sem(f"{name}yt{par}"), 1)

            pe.wait_ge(*upto("hidw_zero"))
            for par in range(2):
                for name in ("wg_full", "wu_full", "wd_full"):
                    pe.wait_ge(*upto(f"{name}{par}", 16))
            with pe.Fori(0, NE // 2) as i:
                for par in range(2):
                    count = pe.value_load(tbl[0:1, bass.ds(i * 2 + (NE + par), 1)],
                                          min_val=0, max_val=T)
                    pe.wait_ge(*upto(f"yt_out{par}", i))
                    pe.wait_ge(*upto(f"byt_out{par}", i * (NWIN - 1)))
                    with pe.If(count > WIN):
                        window(par, "", i + 1, count)
                        pe.wait_ge(*upto(f"yt_out{par}", i + 1))
                        window(par, "b", i * (NWIN - 1) + 1, count - WIN)
                        with pe.If(count > 2 * WIN):
                            with pe.Fori(2, NWIN) as w:
                                with pe.If(count > w * WIN):
                                    pe.wait_ge(*upto(f"byt_out{par}", i * (NWIN - 1) + w - 1))
                                    window(par, "b", i * (NWIN - 1) + w, count - w * WIN)
                                with pe.Else():
                                    for name in ("gu_done", "ht_done", "y_done", "yt"):
                                        pe.drain().then_inc(sem(f"b{name}{par}"), 1)
                        with pe.Else():
                            for name in ("gu_done", "ht_done", "y_done", "yt"):
                                pe.drain().then_inc(sem(f"b{name}{par}"), NWIN - 2)
                    with pe.Else():
                        with pe.If(count > 0):
                            window(par, "", i + 1)
                        with pe.Else():
                            for name in ("gu_done", "ht_done", "y_done", "yt", "gu_free",
                                         "d_free"):
                                pe.drain().then_inc(sem(f"{name}{par}"), 1)
                        for name in ("gu_done", "ht_done", "y_done", "yt"):
                            pe.drain().then_inc(sem(f"b{name}{par}"), NWIN - 1)
            for par in range(2):
                pe.wait_ge(*upto(f"yt_out{par}", NE // 2))
                pe.wait_ge(*upto(f"byt_out{par}", NE // 2 * (NWIN - 1)))
            for c in range(SLOTS // P):
                for b in range(2):
                    for k in range(4):
                        mm = pe.transpose(bank[2 * c + b][:, k * P:(k + 1) * P],
                                          ysT[:, 4 * b + k, c * P:(c + 1) * P], ident[:, :])
                    mm.then_inc(sem("yt_done"), 1)
            pe.wait_ge(*upto("yt_out", 8))
            for t in range(TT):
                for b in range(2):
                    for c in range(SLOTS // P):
                        mm = pe.matmul(bank[2 * t + b][:, :], PwT[:, c, t * P:(t + 1) * P],
                                       ystok[:, c * D + b * 512:c * D + (b + 1) * 512],
                                       start=(c == 0), stop=(c == SLOTS // P - 1))
                    mm.then_inc(sem("comb_done"), 1)

        @block.vector
        def _(dve):
            signal_free(dve, "dve")
            dve.wait_ge(*upto("vec_ready", 2))
            g = VO["hg_lower_gamma"]
            dve.tensor_tensor(small[:, 0:4], vec[:, g:g + HT], vec[:, g + HT:g + 2 * HT],
                              ALU.subtract).then_inc(sem("lbd_ready"), 1)
            dve_norm(dve, "n1", hT, lambda k: v("attn_pre_norm", k), uT, KT)
            dve.wait_ge(*upto("csig_ready"))
            dve.tensor_tensor(csil[:, :], small[:, 16:24], vec[:, VO["c_2"]:VO["c_2"] + KT], ALU.mult
                              ).then_inc(sem("csil_ready"), 1)
            dve.wait_ge(*upto("csil_ready"))
            dve.wait_ge(*upto("ones_set"))
            for k in range(KT):
                dve.tensor_scalar(crep[:, k * 32:(k + 1) * 32], ones[:, 0:32], csil[:, k:k + 1], None,
                                  ALU.mult).then_inc(sem("crep_ready"), 1)
            dve_first(dve, proj1)
            dve_source(dve, "proj1", uT, SRC_HI)
            dve_dense(dve, proj1)
            dve.wait_ge(*upto("lb_ready", 2))
            dve.wait_ge(*upto("hg_sig", 1))
            for h in range(HT):
                dve.tensor_scalar(tile(T4, h), tile(T4, h), small[:, 8 + h:9 + h],
                                  small[:, 4 + h:5 + h], ALU.mult, ALU.add
                                  ).then_inc(sem("f_ready"), 1)
            dve.wait_ge(*upto("hg_sig", 2))
            dve.wait_ge(*upto("proj1_out0", IN1 // 512))
            dve.tensor_tensor(tile(projR, 0, 4), tile(projR, 0, 4), S4[:, :], ALU.mult
                              ).then_inc(sem("q_ready"), 1)
            dve.wait_ge(*upto("hg_sig", 4))
            for h in range(HT):
                dve.tensor_scalar(tile(projR, 4 + h), tile(projR, 4 + h), small[:, 8 + h:9 + h], None,
                                  ALU.mult).then_inc(sem("k_ready"), 1)
            dve.tensor_tensor(tile(projR, 12, 4), tile(projR, 12, 4), G4[:, :], ALU.mult
                              ).then_inc(sem("hgate_ready"), 1)
            dve.wait_ge(*upto("g_ready"))
            dve.wait_ge(*upto("hgate_ready"))
            for h in range(HT):
                dve.tensor_tensor_scan(tile(G4, h), ones[:, 0:T], tile(T4, h), 0.0, ALU.mult, ALU.add
                                       ).then_inc(sem("b_ready"), 1)
            dve.wait_ge(*upto("b_ready", HT))
            dve.wait_ge(*upto("q_ready"))
            dve.wait_ge(*upto("k_ready", HT))
            dve.wait_ge(*upto("lv_zero", 5))
            dve.wait_ge(*upto("c1", NC1))

            def diffs(li):
                L = ALL_LEVELS[li]
                if li >= 2:
                    dve.wait_ge(*upto("qk_ready", 2 * (li - 1)))
                bv, ev = blocks(hb, L), blocks(ed[li % 2], L)
                ref = bv[:, :, L - 1:L].to_broadcast([P, 1024 // (2 * L), L])
                dve.tensor_tensor(ev[:, :, 0:L], ref, bv[:, :, 0:L], ALU.subtract
                                  ).then_inc(sem("d_ready"), 1)
                dve.tensor_tensor(ev[:, :, L:2 * L], bv[:, :, L:2 * L], ref, ALU.subtract
                                  ).then_inc(sem("d_ready"), 1)

            def products(li):
                L = ALL_LEVELS[li]
                dve.wait_ge(*upto("e_ready", li + 1))
                if li >= 2:
                    dve.wait_ge(*upto("lv_done", li - 1))
                ev = blocks(ed[li % 2], L)
                dve.tensor_tensor(blocks(kd[li % 2], L)[:, :, 0:L],
                                  blocks(tile(projR, 4, 4), L)[:, :, 0:L], ev[:, :, 0:L], ALU.mult
                                  ).then_inc(sem("qk_ready"), 1)
                dve.tensor_tensor(blocks(qd[li % 2], L)[:, :, L:2 * L],
                                  blocks(tile(projR, 0, 4), L)[:, :, L:2 * L], ev[:, :, L:2 * L],
                                  ALU.mult).then_inc(sem("qk_ready"), 1)

            def collect(li, mask):
                dve.wait_ge(*upto("lv_done", li + 1))
                if li:
                    dve.wait_ge(*upto("lv_out", 2 * li))
                m = lmask[:, mask, :].bitcast(U32).unsqueeze(1).to_broadcast([P, 4, P])
                for b in range(2):
                    dve.copy_predicated(
                        S4[:, b * 512:(b + 1) * 512].rearrange("p (n t) -> p n t", t=P), m,
                        bank[(2 * (li % 2) if li < len(ALL_LEVELS) else 0) + b][:, :].rearrange(
                            "p (n t) -> p n t", t=P)).then_inc(sem("lv_out"), 1)

            diffs(0)
            for li in range(len(ALL_LEVELS)):
                if li + 1 < len(ALL_LEVELS):
                    diffs(li + 1)
                products(li)
                if li:
                    collect(li - 1, li - 1)
            li = len(ALL_LEVELS) - 1
            dve.wait_ge(*upto("lv_done", li + 1))
            for b in range(2):
                dve.tensor_copy(
                    SX2[:, b * 256:(b + 1) * 256].rearrange("p (h t) -> p h t", t=P),
                    bank[2 * (li % 2) + b][:, :].rearrange("p (h t) -> p h t", t=T)[:, :, 0:P]
                ).then_inc(sem("lv_out"), 1)
            collect(li + 1, DIAG)
            for b in range(ADA_B):
                dve.wait_ge(*upto("mod_done", b + 1))
                dve.tensor_tensor(
                    modT[:, b * 16:(b + 1) * 16].rearrange("p (j c) -> p j c", c=4),
                    bank[4 + b][:, :].rearrange("p (c j r) -> p j c r", c=4, r=32)[:, :, :, 0],
                    badaT[:, b * 16:(b + 1) * 16].rearrange("p (j c) -> p j c", c=4), ALU.add
                ).then_inc(sem("mod_ready"), 1)
            for h in range(SB_HEADS):
                c = slice(h * 384, (h + 1) * 384)
                dve.wait_ge(*upto("sx_done", h + 1))
                dve.wait_ge(*upto("zm_ready", h + 1))
                dve.tensor_tensor(zb[:, c], bank[4 + h % 2][:, 0:384], eb[:, c], ALU.add
                                  ).then_inc(sem("sx_ready"), 1)
            dve_first(dve, wout1)
            dve_norm(dve, "nhg", mixin, lambda k: v("hg_out_norm", k), mixin, HT)
            dve.wait_ge(*upto("nhg_out", HT))
            dve.tensor_tensor(mixin[:, 0:HT * T], mixin[:, 0:HT * T], tile(projR, 12, 4), ALU.mult
                              ).then_inc(sem("ohg_ready"), 1)
            o_sb = mixin[:, HT * T:2 * HT * T]
            dve_norm(dve, "nsb", o_sb, lambda k: v("sb_out_norm", k), o_sb, HT)
            dve_source(dve, "wout1", mixin, SRC_LO)
            dve_dense(dve, wout1)
            dve.wait_ge(*upto("wout1_out0", 2))
            dve.wait_ge(*upto("wout1_out1", 2))
            dve_norm(dve, "npost", mixT, lambda k: v("attn_post_norm", k), mixT, KT)
            def lo(raw, hi, dst, name, count):
                dve.wait_ge(*upto(f"{name}_hi", count))
                dve.tensor_tensor(dst, raw, hi.bitcast(F32), ALU.subtract
                                  ).then_inc(sem(f"{name}_lo"), 1)

            lo(slot[0], slot_r[6], slot_r[7], "gate", 1)
            lo(slot[1], slot_r[8], slot_r[9], "up", 1)
            dve_norm(dve, "nffn", hT, lambda k: v("ffn_pre_norm", k), uT, KT)
            dve_source(dve, "ffn", uT, SRC_HI)

            def ffn_parts(i, last):
                if not last:
                    lo(slot[0], slot_r[6], slot_r[7], "gate", i + 2)
                lo(slot[4], slot_r[10], slot_r[11], "down", i + 1)
                dve.wait_ge(*upto("silu_ready", i + 1))
                dve.wait_ge(*upto("up_done", i + 1))
                dve.tensor_tensor(S4[:, 512:1024], S4[:, 0:512], bank[1][:, :], ALU.mult
                                  ).then_inc(sem("hid_ready"), 1)
                dve.wait_ge(*upto("hid_ready", i + 1))
                lo(S4[:, 512:1024], T4_r[:, 0:512], T4_r[:, 512:1024], "hid", i + 1)
                if not last:
                    lo(slot[1], slot_r[8], slot_r[9], "up", i + 2)

            with dve.Fori(0, NF - 1) as i:
                ffn_parts(i, False)
            ffn_parts(NF - 1, True)
            dve_first(dve, pgate)
            dve_norm(dve, "nfpost", mixT, lambda k: v("ffn_post_norm", k), mixT, KT)
            dve_source(dve, "pgate", hT, SRC_LO)
            dve_dense(dve, pgate)
            dve.wait_ge(*upto("pp_out", 4))
            for b in range(4):
                dve.wait_ge(*upto(f"pgate_out{b % 2}", b // 2 + 1))
                dve.tensor_tensor(tile(mixT, 2 * b, 2), tile(mixT, 2 * b, 2), tile(xk, 2 * b, 2),
                                  ALU.mult).then_inc(sem("ple_ready"), 1)


            dve.wait_ge(*upto("mod_ready", ADA_B))
            for n, (name, sc) in enumerate((("g_mix_2", KT), ("g_ffn_2", 4 * KT))):
                dve.scalar_tensor_tensor(out=gs[:, n * KT:(n + 1) * KT], in0=modT[:, sc:sc + KT],
                                         scalar=1.0, in1=vec[:, VO[name]:VO[name] + KT],
                                         op0=ALU.add, op1=ALU.mult).then_inc(sem("gs_ready"), 1)
            dve.wait_ge(*upto("lam", 3))
            lam = vec[:, VO["lru_lambda_2"]:VO["lru_lambda_2"] + HT]
            dve.tensor_scalar(lru[:, HT:2 * HT], lam, 0.0, None, ALU.min).then_inc(sem("lam_v"), 1)
            dve.wait_ge(*upto("lam_v", 1))
            dve.tensor_tensor(lru[:, HT:2 * HT], lru[:, HT:2 * HT], lru[:, 0:HT], ALU.subtract
                              ).then_inc(sem("lam_v"), 1)
            dve.wait_ge(*upto("lam_v", 2))
            dve.tensor_scalar(lru[:, 2 * HT:3 * HT], lru[:, HT:2 * HT], LRU_C, None, ALU.mult
                              ).then_inc(sem("lam_v"), 1)
            dve_first(dve, proj2)
            dve.wait_ge(*upto("gs_ready", 2))
            dve_norm(dve, "nmix2", hT, lambda k: gs[:, k:k + 1], uT, KT)
            dve_source(dve, "proj2", uT, SRC_HI)
            dve_dense(dve, proj2)
            dve.wait_ge(*upto("proj2_out0", IN2_FULL // 512))
            dve.wait_ge(*upto("proj2_out1", IN2_FULL // 512))
            for k in range(HT):
                dve.tensor_scalar(tile(XC, k), tile(projR, k), v("conv_w_2", 3 * HT + k),
                                  v("conv_b_2", k), ALU.mult, ALU.add).then_inc(sem("conv"), 1)
            for sh in range(1, 4):
                for k in range(HT):
                    dve.wait_ge(*upto("conv", HT * (sh - 1) + k + 1))
                    dve.scalar_tensor_tensor(
                        out=tile(XC, k)[:, sh:T], in0=tile(projR, k)[:, 0:T - sh],
                        scalar=v("conv_w_2", (3 - sh) * HT + k), in1=tile(XC, k)[:, sh:T],
                        op0=ALU.mult, op1=ALU.add).then_inc(sem("conv"), 1)
            dve.wait_ge(*upto("ga", 5))
            ls = lsx[:, 0:512]
            dve.scalar_tensor_tensor(out=ls, in0=ls, scalar=0.0, in1=lsx[:, 512:1024], op0=ALU.min,
                                     op1=ALU.subtract).then_inc(sem("ls_ready"), 1)
            dve.wait_ge(*upto("ls_ready"))
            dve.wait_ge(*upto("glr_done"))
            for c in range(8):
                dve.tensor_tensor_scan(b64[:, c * 64:(c + 1) * 64], ones[:, 0:64],
                                       ls[:, c * 64:(c + 1) * 64], 0.0, ALU.mult, ALU.add
                                       ).then_inc(sem("b64_ready"), 1)
            for k in range(GLA_QT):
                dve.tensor_tensor_scan(b256[:, k * T:(k + 1) * T], ones[:, 0:T],
                                       ls[:, k * T:(k + 1) * T], 0.0, ALU.mult, ALU.add
                                       ).then_inc(sem("b256_ready"), 1)
            dve.memset(S4[:, :], 0.0).then_inc(sem("gs4_zero"), 1)
            GSC = float(GLA_DK) ** -0.5
            gq, gk = tile(projR, 8, 2), tile(projR, 10, 2)
            dve.wait_ge(*upto("ge_ready", 2))
            dve.scalar_tensor_tensor(out=q2[0], in0=gq, scalar=GSC, in1=e2[0], op0=ALU.mult,
                                     op1=ALU.mult).then_inc(sem("gqk_ready"), 1)
            dve.tensor_tensor(k2[0], gk, e2[1], ALU.mult).then_inc(sem("gqk_ready"), 1)
            dve.memset(q2[1], 0.0).then_inc(sem("gs4_zero"), 1)
            dve.memset(k2[1], 0.0).then_inc(sem("gs4_zero"), 1)
            dve.wait_ge(*upto("gs4_zero", 3))
            dve.wait_ge(*upto("gqk_ready", 2))
            dve.wait_ge(*upto("b256_ready", 2))
            for n, L in enumerate((64, P)):
                bv, ev = blocks(b256, L), blocks(e2[n], L)
                ref = bv[:, :, L - 1:L].to_broadcast([P, 512 // (2 * L), L])
                dve.tensor_tensor(ev[:, :, 0:L], ref, bv[:, :, 0:L], ALU.subtract
                                  ).then_inc(sem("gd_ready"), 1)
                dve.tensor_tensor(ev[:, :, L:2 * L], bv[:, :, L:2 * L], ref, ALU.subtract
                                  ).then_inc(sem("gd_ready"), 1)

            def gla_collect(n, mask):
                dve.wait_ge(*upto("gl_done", 2 * n + 2))
                if n:
                    dve.wait_ge(*upto("gl_out", 2 * n))
                m = lmask[:, mask, :].bitcast(U32).unsqueeze(1).to_broadcast([P, 4, P])
                for b in range(2):
                    dve.copy_predicated(
                        S4[:, b * 512:(b + 1) * 512].rearrange("p (n t) -> p n t", t=P), m,
                        bank[6 + b][:, :].rearrange("p (n t) -> p n t", t=P)
                    ).then_inc(sem("gl_out"), 1)

            for n, L in enumerate((64, P)):
                dve.wait_ge(*upto("ge_ready", 3 + n))
                ev, o = blocks(e2[n], L), (n + 1) % 2
                if n:
                    dve.wait_ge(*upto("gl_done", 2))
                dve.tensor_tensor(blocks(k2[o], L)[:, :, 0:L], blocks(gk, L)[:, :, 0:L],
                                  ev[:, :, 0:L], ALU.mult).then_inc(sem("gqk_ready"), 1)
                dve.scalar_tensor_tensor(out=blocks(q2[o], L)[:, :, L:2 * L],
                                         in0=blocks(gq, L)[:, :, L:2 * L], scalar=GSC,
                                         in1=ev[:, :, L:2 * L], op0=ALU.mult, op1=ALU.mult
                                         ).then_inc(sem("gqk_ready"), 1)
                gla_collect(n, CHUNK if n == 0 else len(LEVELS) - 1)
            dve.wait_ge(*upto("gl_done", 6))
            for b in range(2):
                dve.tensor_copy(SX2[:, b * T:(b + 1) * T].rearrange("p (h t) -> p h t", t=P),
                                bank[6 + b][:, :].rearrange("p (h t) -> p h t", t=T)[:, :, 0:P]
                                ).then_inc(sem("gl_out"), 1)
            dve.wait_ge(*upto("lam_v", 3))
            dve.wait_ge(*upto("lgate_out", HT))
            for k in range(HT):
                dve.tensor_scalar(tile(T4, k), tile(T4, k), lru[:, 2 * HT + k:2 * HT + k + 1], None,
                                  ALU.mult).then_inc(sem("la_ready"), 1)
            dve.wait_ge(*upto("lgate_out", 2 * HT))
            dve.tensor_tensor(G4[:, :], G4[:, :], XC, ALU.mult).then_inc(sem("gi_ready"), 1)
            y = tile(projR, 4, 4)
            dve.wait_ge(*upto("h3_ready", 4))
            dve.tensor_tensor(gel, y, y, ALU.mult).then_inc(sem("gelu_a"), 1)
            dve.wait_ge(*upto("gelu_a", 1))
            dve.tensor_scalar(gel, gel, GELU_CUBIC, 1.0, ALU.mult, ALU.add
                              ).then_inc(sem("gelu_a"), 1)
            dve.wait_ge(*upto("gelu_a", 2))
            dve.tensor_tensor(gel, gel, y, ALU.mult).then_inc(sem("gelu_in"), 1)
            dve.wait_ge(*upto("lru_a"))
            dve.wait_ge(*upto("lru_th"))
            dve.tensor_tensor(T4[:, :], A8, A8, ALU.mult).then_inc(sem("a2_ready"), 1)
            dve.wait_ge(*upto("a2_ready"))
            dve.scalar_tensor_tensor(out=th, in0=T4[:, :], scalar=1.0, in1=th, op0=ALU.add,
                                     op1=ALU.mult).then_inc(sem("lru_m"), 1)
            dve.wait_ge(*upto("gelu_tanh"))
            dve.scalar_tensor_tensor(out=gel, in0=gel, scalar=1.0, in1=y, op0=ALU.add, op1=ALU.mult
                                     ).then_inc(sem("gelu_y"), 1)
            dve.wait_ge(*upto("lru_root"))
            dve.wait_ge(*upto("gi_ready"))
            dve.tensor_tensor(G4[:, :], G4[:, :], th, ALU.mult).then_inc(sem("u_ready"), 1)
            dve.wait_ge(*upto("u_ready"))
            for k in range(HT):
                dve.tensor_tensor_scan(tile(T4, k), tile(A8, k), tile(G4, k), 0.0, ALU.mult, ALU.add
                                       ).then_inc(sem("lru_h"), 1)
            dve.wait_ge(*upto("lru_h", HT))
            dve.wait_ge(*upto("gelu_y"))
            dve.scalar_tensor_tensor(out=mixin[:, 0:HT * T], in0=gel, scalar=0.5, in1=T4[:, :],
                                     op0=ALU.mult, op1=ALU.mult).then_inc(sem("mix2_ready"), 1)
            dve_first(dve, wout2)
            for b in range(2):
                dve.wait_ge(*upto("og_rms", b + 1))
                c = slice(b * 512, (b + 1) * 512)
                dve.reciprocal(rms[:, c], rms[:, c]).then_inc(sem("og_rinv"), 1)
            for b in range(2):
                dve.wait_ge(*upto("og_rinv", b + 1))
                c = slice(b * 512, (b + 1) * 512)
                dve.scalar_tensor_tensor(out=A8[:, c], in0=XC[:, c], scalar=v("gla_gnorm_2"),
                                         in1=rms[:, c], op0=ALU.mult, op1=ALU.mult
                                         ).then_inc(sem("og_normed"), 1)
            dve.wait_ge(*upto("gout_ready"))
            for b in range(2):
                dve.wait_ge(*upto("og_normed", b + 1))
                c = slice(b * 512, (b + 1) * 512)
                dve.tensor_tensor(A8[:, c], A8[:, c], tile(projR, 16 + 2 * b, 2), ALU.mult
                                  ).then_inc(sem("mix2_ready"), 1)
            dve_source(dve, "wout2", mixin, SRC_LO)
            dve_dense(dve, wout2)
            dve.wait_ge(*upto("wout2_out0", 2))
            dve.wait_ge(*upto("wout2_out1", 2))
            for k in range(KT):
                dve.scalar_tensor_tensor(out=tile(hT, k), in0=tile(mixT2, k),
                                         scalar=modT[:, 2 * KT + k:2 * KT + k + 1], in1=tile(hT, k),
                                         op0=ALU.mult, op1=ALU.add).then_inc(sem("x2_ready"), 1)
            dve_norm(dve, "nffn2", hT, lambda k: gs[:, KT + k:KT + k + 1], uT, KT)

            steps = [0]

            def step(ins):
                ins.then_inc(sem("route"), 1)
                steps[0] += 1
                dve.wait_ge(*upto("route", steps[0]))

            def tab(at, n=NE):
                return rt[:, at:at + TT * n].rearrange("p (t n) -> p t n", t=TT)

            def val(i):
                return rs[:, i * TT:(i + 1) * TT]

            def over(i, n):
                return val(i).unsqueeze(2).to_broadcast([P, TT, n])

            ie = iotg[:, :].rearrange("p (t n) -> p t n", t=TT)
            ic = iotc[:, :].rearrange("p (t n) -> p t n", t=TT)
            dve.wait_ge(*upto("iotas", 3))
            dve.wait_ge(*upto("lg_done"))
            lgv = lg[:, :].rearrange("p (t n) -> p t n", t=TT)
            step(dve.tensor_copy(lgv, bank[1][:, 0:TT * 64].rearrange("p (t n) -> p t n", t=TT)
                                 [:, :, 0:NL]))
            step(dve.tensor_reduce(val(0), lgv[:, :, 0:NG], AX.X, ALU.max))
            dve.tensor_tensor(tab(0, NG), lgv[:, :, 0:NG], over(0, NG), ALU.subtract
                              ).then_inc(sem("cs_ready"), 1)
            step(dve.tensor_tensor(tab(64, NG), lgv[:, :, 0:NG], over(0, NG), ALU.is_equal))

            def first_of(eq, iota, dst, n, i):
                step(dve.scalar_tensor_tensor(out=eq, in0=eq, scalar=-1000.0, in1=iota,
                                              op0=ALU.mult, op1=ALU.add))
                step(dve.tensor_reduce(val(i), eq, AX.X, ALU.min))
                step(dve.tensor_tensor(dst, eq, over(i, n), ALU.is_equal))

            first_of(tab(64, NG), ic, tab(128, NG), NG, 1)
            dve.wait_ge(*upto("ec_ready"))
            step(dve.tensor_reduce(val(2), tab(0, NG), AX.X, ALU.add))
            step(dve.reciprocal(val(2), val(2)))
            step(dve.tensor_scalar(tab(128, NG), tab(128, NG), -NEG_BIG, NEG_BIG, ALU.mult, ALU.add))
            grp = rt[:, 128:128 + TT * NG].unsqueeze(2).to_broadcast([P, TT * NG, EPG])
            step(dve.tensor_copy(rt[:, 192:192 + TT * NE].rearrange("p (g e) -> p g e", e=EPG), grp))
            step(dve.tensor_tensor(tab(192), tab(192), lgv[:, :, NG:NL], ALU.add))
            step(dve.tensor_reduce(val(5), tab(192), AX.X, ALU.max))
            step(dve.tensor_tensor(tab(256), tab(192), over(5, NE), ALU.is_equal))
            first_of(tab(256), ie, tab(TA1), NE, 1)
            step(dve.scalar_tensor_tensor(out=tab(192), in0=tab(TA1), scalar=2 * NEG_BIG,
                                          in1=tab(192), op0=ALU.mult, op1=ALU.add))
            step(dve.tensor_reduce(val(6), tab(192), AX.X, ALU.max))
            step(dve.tensor_tensor(tab(256), tab(192), over(6, NE), ALU.is_equal))
            first_of(tab(256), ie, tab(TA2), NE, 1)
            dve.tensor_tensor(tab(TA), tab(TA1), tab(TA2), ALU.add).then_inc(sem("a_set"), 1)
            dve.tensor_tensor(val(4), val(6), val(5), ALU.subtract).then_inc(sem("dm_ready"), 1)
            for b in range(4):
                dve.wait_ge(*upto("h2tok", b + 1))
                c = slice(b * 512, (b + 1) * 512)
                dve.tensor_tensor(h2_lo[:, c], bank[4 + b][:, :], h2_hi[:, c].bitcast(F32),
                                  ALU.subtract).then_inc(sem("h2lo"), 1)
            dve.wait_ge(*upto("e21_ready"))
            step(dve.tensor_scalar(val(7), val(4), 1.0, None, ALU.add))
            step(dve.reciprocal(val(7), val(7)))
            step(dve.tensor_tensor(val(7), val(7), val(2), ALU.mult))
            step(dve.tensor_tensor(val(8), val(7), val(4), ALU.mult))
            dve.wait_ge(*upto("rank_done"))
            step(dve.tensor_copy(rt[:, 256:256 + NE], bank[1][:, 2 * NE:3 * NE]))
            step(dve.tensor_tensor_scan(rt[:, 192:192 + NE], ones[:, 0:NE], rt[:, 256:256 + NE], 0.0,
                                        ALU.mult, ALU.add))
            step(dve.tensor_tensor(rt[:, 192:192 + NE], rt[:, 192:192 + NE], rt[:, 256:256 + NE],
                                   ALU.subtract))
            dve.tensor_copy(tbl[:, 0:NE], rt[0:1, 192:192 + NE]).then_inc(sem("tbl_ready"), 1)
            dve.tensor_copy(tbl[:, NE:2 * NE], rt[0:1, 256:256 + NE]).then_inc(sem("tbl_ready"), 1)
            step(dve.tensor_tensor(
                tab(320), bank[1][:, 0:2 * NE].rearrange("p (t n) -> p t n", t=TT),
                rt[:, 192:192 + NE].unsqueeze(1).to_broadcast([P, TT, NE]), ALU.add))
            for c, ta in enumerate((TA1, TA2)):
                step(dve.tensor_tensor(tab(ta), tab(ta), tab(320), ALU.mult))
                step(dve.tensor_reduce(val(12 + c), tab(ta), AX.X, ALU.add))
            for t in range(TT):
                s1, s2 = (rs[:, (12 + c) * TT + t:(12 + c) * TT + t + 1] for c in range(2))
                w1, w2 = (rs[:, (7 + c) * TT + t:(7 + c) * TT + t + 1] for c in range(2))
                step(dve.tensor_scalar(Psel_r[:, t, :], iot[:, :], s1, None, ALU.is_equal))
                dve.scalar_tensor_tensor(out=Psel_r[:, t, :], in0=iot[:, :], scalar=s2,
                                         in1=Psel_r[:, t, :].bitcast(F32), op0=ALU.is_equal, op1=ALU.add
                                         ).then_inc(sem("psel_ready"), 1)
            for t in range(TT):
                s1, s2 = (rs[:, (12 + c) * TT + t:(12 + c) * TT + t + 1] for c in range(2))
                w1, w2 = (rs[:, (7 + c) * TT + t:(7 + c) * TT + t + 1] for c in range(2))
                step(dve.tensor_scalar(Pw[:, t, :], iot[:, :], s1, w1, ALU.is_equal, ALU.mult))
                step(dve.tensor_scalar(SV4[:, 0:SLOTS], iot[:, :], s2, w2, ALU.is_equal, ALU.mult))
                dve.tensor_tensor(Pw[:, t, :], Pw[:, t, :], SV4[:, 0:SLOTS], ALU.add
                                  ).then_inc(sem("pw_ready"), 1)
                dve.wait_ge(*upto("pw_ready", t + 1))

            gt2 = modT[:, 5 * KT:6 * KT].rearrange("p (q c) -> p q c", c=2).unsqueeze(3
                  ).to_broadcast([P, 4, 2, WIN])

            def hidden(par, name, count):
                dve.wait_ge(*upto(f"{name}sil{par}", count))
                dve.tensor_tensor(hid, sil, bank[par][2 * WIN:P, 0:256], ALU.mult
                                  ).then_inc(sem(f"{name}hid{par}"), 1)
                dve.wait_ge(*upto(f"{name}yt{par}", count))

            def outputs(start, par, name):
                dve.tensor_tensor(
                    ysT[:, :, bass.ds(start, WIN)].rearrange("p (q c) s -> p q c s", c=2),
                    bank[6 + par][:, 0:256].rearrange("p (c q s) -> p q c s", c=2, q=4), gt2,
                    ALU.mult
                ).then_inc(sem(f"{name}yt_out{par}"), 1)

            dve.memset(hidw[0:2 * WIN, :], 0.0).then_inc(sem("hidw_zero"), 1)
            dve.wait_ge(*upto("xs_out", KT))
            dve.wait_ge(*upto("x2tok", 4))
            with dve.Fori(0, NE // 2) as i:
                for par in range(2):
                    start = dve.value_load(tbl[0:1, bass.ds(i * 2 + par, 1)],
                                           min_val=0, max_val=SLOTS)
                    count = dve.value_load(tbl[0:1, bass.ds(i * 2 + (NE + par), 1)],
                                           min_val=0, max_val=T)
                    with dve.If(count > 0):
                        hidden(par, "", i + 1)
                        last = i + 1 if par else i
                        dve.wait_ge(*upto(f"yt_out{1 - par}", last))
                        dve.wait_ge(*upto(f"byt_out{1 - par}", last * (NWIN - 1)))
                        outputs(start, par, "")
                        with dve.If(count > WIN):
                            hidden(par, "b", i * (NWIN - 1) + 1)
                            outputs(start + WIN, par, "b")
                            with dve.If(count > 2 * WIN):
                                with dve.Fori(2, NWIN) as w:
                                    with dve.If(count > w * WIN):
                                        hidden(par, "b", i * (NWIN - 1) + w)
                                        outputs(start + w * WIN, par, "b")
                                    with dve.Else():
                                        for name in ("hid", "yt_out"):
                                            dve.drain().then_inc(sem(f"b{name}{par}"), 1)
                            with dve.Else():
                                for name in ("hid", "yt_out"):
                                    dve.drain().then_inc(sem(f"b{name}{par}"), NWIN - 2)
                        with dve.Else():
                            for name in ("hid", "yt_out"):
                                dve.drain().then_inc(sem(f"b{name}{par}"), NWIN - 1)
                    with dve.Else():
                        for name in ("hid", "yt_out"):
                            dve.drain().then_inc(sem(f"{name}{par}"), 1)
                            dve.drain().then_inc(sem(f"b{name}{par}"), NWIN - 1)
            for t in range(TT):
                for b in range(2):
                    c = slice(t * D + b * 512, t * D + (b + 1) * 512)
                    dve.wait_ge(*upto("comb_done", 2 * t + b + 1))
                    dve.tensor_tensor(x2tok[:, c], x2tok[:, c], bank[2 * t + b][:, :], ALU.add
                                      ).then_inc(sem("x3_ready"), 1)
            for t in range(TT):
                dve.wait_ge(*upto("fin_rms", t + 1))
                dve.wait_ge(*upto("gfin_in", 16))
                dve.reciprocal(rs[:, 22 + t:23 + t], rs[:, 22 + t:23 + t]).then_inc(sem("fin_rinv"), 1)
                dve.wait_ge(*upto("fin_rinv", t + 1))
                c = slice(t * D, (t + 1) * D)
                dve.scalar_tensor_tensor(out=x2tok[:, c], in0=x2tok[:, c], scalar=rs[:, 22 + t:23 + t],
                                         in1=gfin[:, :], op0=ALU.mult, op1=ALU.mult
                                         ).then_inc(sem("y_ready"), 1)

_INS = ["x", "p", "attn_pre_norm", "w_in", "hg_lower_gamma", "hg_out_norm", "sb_out_norm", "w_out",
        "attn_post_norm", "ffn_pre_norm", "w_gate_up", "w_down", "ffn_post_norm", "ple_proj",
        "ple_gate", "c_2", "w_ada_2", "b_ada_2", "g_mix_2", "g_ffn_2", "g_final_2", "w_in_2",
        "conv_w_2", "conv_b_2", "lru_wr_2", "lru_br_2", "lru_wi_2", "lru_bi_2", "lru_lambda_2",
        "gla_wa2_2", "gla_ba_2", "gla_gnorm_2", "w_out_2", "w_coarse_2", "b_coarse_2", "w_fine_2",
        "b_fine_2", "w_gate_2", "w_up_2", "w_down_2"]


def kernel(**inputs):
    import numpy as _np
    import concourse.bacc as _bacc
    from concourse.bass_utils import run_bass_kernel_spmd as _run

    nc = _bacc.Bacc("TRN2", target_bir_lowering=False, num_devices=1)
    arrays, dram = {}, {}
    for name in _INS:
        a = _np.ascontiguousarray(inputs[name])
        arrays[f"in_{name}"] = a
        dram[name] = nc.dram_tensor(f"in_{name}", a.shape, mybir.dt.from_np(a.dtype),
                                    kind="ExternalInput").ap()
    shape = arrays["in_x"].shape
    out = nc.dram_tensor("out_0", shape, F32, kind="ExternalOutput").ap()
    build_program(nc, dram, out)
    r = _run(nc, [arrays], core_ids=[0])
    return r.results[0]["out_0"]
```
